# Optimizing a Trainium2 kernel written in Bass

```python
import jax, jax.numpy as jnp
from jax import lax
import numpy as np
import math
import jax
import jax.numpy as jnp

D_MODEL = 2048
BATCH = 1
SEQ = 256
DEPTH = 1

N_MIXERS = 3
EPS = 1e-6
SB_HEADS = 16
SB_HEAD_DIM = D_MODEL // SB_HEADS
SB_WIDTH = SB_HEADS * SB_HEAD_DIM
Q_BLOCK = 128
GM_CHUNK = 128
GM_GROUPS = 16
GM_WIDTH = D_MODEL
GM_GROUP_DIM = GM_WIDTH // GM_GROUPS
SSD_INNER = 2 * D_MODEL
SSD_HEAD_DIM = 64
SSD_HEADS = SSD_INNER // SSD_HEAD_DIM
SSD_GROUPS = 8
SSD_HPG = SSD_HEADS // SSD_GROUPS
SSD_STATE = 128
SSD_CONV = 4
SSD_CHUNK = 128
SSD_CONV_DIM = SSD_INNER + 2 * SSD_GROUPS * SSD_STATE
SSD_PROJ = SSD_INNER + SSD_CONV_DIM + SSD_HEADS
MLP_HIDDEN = 4 * D_MODEL
N_A = len(range(0, DEPTH, N_MIXERS))
N_B = len(range(1, DEPTH, N_MIXERS))
N_C = len(range(2, DEPTH, N_MIXERS))


def rms_norm(x, g):
    xf = x.astype(jnp.float32)
    y = xf * lax.rsqrt(jnp.mean(xf * xf, axis=-1, keepdims=True) + EPS)
    return (y * g.astype(jnp.float32)).astype(x.dtype)

def stick_breaking_attention(h, w_qkv, q_g, k_g, w_o):
    b, s, _ = h.shape
    q, k, v = jnp.split(h @ w_qkv, 3, axis=-1)
    q = rms_norm(q.reshape(b, s, SB_HEADS, SB_HEAD_DIM), q_g).transpose(0, 2, 1, 3)
    k = rms_norm(k.reshape(b, s, SB_HEADS, SB_HEAD_DIM), k_g).transpose(0, 2, 1, 3)
    v = v.reshape(b, s, SB_HEADS, SB_HEAD_DIM).transpose(0, 2, 1, 3)
    scale = SB_HEAD_DIM ** -0.5
    n_blk = s // Q_BLOCK
    q_blocks = q.reshape(b, SB_HEADS, n_blk, Q_BLOCK, SB_HEAD_DIM).transpose(2, 0, 1, 3, 4)
    k_pos = jnp.arange(s)

    def one_block(args):
        qb, start = args
        z = jnp.einsum('bhqd,bhkd->bhqk', qb, k).astype(jnp.float32) * scale
        q_pos = start + jnp.arange(Q_BLOCK)
        mask = k_pos[None, :] < q_pos[:, None]
        log_beta = jax.nn.log_sigmoid(z)
        log_1m = jnp.where(mask, jax.nn.log_sigmoid(-z), 0.0)
        suffix = lax.cumsum(log_1m, axis=3, reverse=True) - log_1m
        a = jnp.where(mask, jnp.exp(log_beta + suffix), 0.0)
        return jnp.einsum('bhqk,bhkd->bhqd', a.astype(v.dtype), v)

    starts = jnp.arange(n_blk, dtype=jnp.int32) * Q_BLOCK
    o = lax.map(one_block, (q_blocks, starts))
    o = o.transpose(1, 0, 3, 2, 4).reshape(b, s, SB_WIDTH)
    return o @ w_o

def chunked_spatial_gating(h, w_in, v_g, w_s, b_s, w_o):
    b, s, _ = h.shape
    u, v = jnp.split(jax.nn.gelu(h @ w_in, approximate=False), 2, axis=-1)
    v = rms_norm(v, v_g)
    n_chunk = s // GM_CHUNK
    v = v.reshape(b, n_chunk, GM_CHUNK, GM_GROUPS, GM_GROUP_DIM)
    u = u.reshape(b, n_chunk, GM_CHUNK, GM_GROUPS, GM_GROUP_DIM)
    causal = jnp.tril(jnp.ones((GM_CHUNK, GM_CHUNK), dtype=bool))
    w = jnp.where(causal[None], w_s, 0.0)
    mixed = jnp.einsum('gts,bcsgd->bctgd', w.astype(v.dtype), v) + b_s.T[:, :, None]
    y = (u * mixed).reshape(b, s, GM_WIDTH)
    return y @ w_o

def ssd_chunked_scan(x, dt, a, bm, cm):
    b, s = x.shape[:2]
    c, L = s // SSD_CHUNK, SSD_CHUNK
    xs = (x * dt[..., None]).reshape(b, c, L, SSD_GROUPS, SSD_HPG, SSD_HEAD_DIM)
    da = (dt * a).reshape(b, c, L, SSD_GROUPS, SSD_HPG).transpose(0, 3, 4, 1, 2)
    bc = bm.reshape(b, c, L, SSD_GROUPS, SSD_STATE)
    cc = cm.reshape(b, c, L, SSD_GROUPS, SSD_STATE)
    a_cum = jnp.cumsum(da, axis=-1)
    seg = a_cum[..., :, None] - a_cum[..., None, :]
    tri = jnp.tril(jnp.ones((L, L), dtype=bool))
    decay = jnp.exp(jnp.where(tri, seg, -jnp.inf))
    cb = jnp.einsum('bclgn,bcsgn->bgcls', cc, bc)
    y_diag = jnp.einsum('bgcls,bgrcls,bcsgrp->bclgrp', cb, decay, xs)
    decay_states = jnp.exp(a_cum[..., -1:] - a_cum)
    states = jnp.einsum('bclgn,bgrcl,bclgrp->cbgrpn', bc, decay_states, xs)
    chunk_decay = jnp.exp(a_cum[..., -1]).transpose(3, 0, 1, 2)

    def step(carry, inp):
        st, dec = inp
        return carry * dec[..., None, None] + st, carry

    _, prev = lax.scan(step, jnp.zeros_like(states[0]), (states, chunk_decay))
    y_off = jnp.einsum('bclgn,cbgrpn,bgrcl->bclgrp', cc, prev, jnp.exp(a_cum))
    return (y_diag + y_off).reshape(b, s, SSD_GROUPS, SSD_HPG, SSD_HEAD_DIM)

def ssd_mixer(h, w_in, conv_w, conv_b, dt_bias, a_log, d_skip, norm_g, w_o):
    b, s, _ = h.shape
    z, xbc, dt = jnp.split(h @ w_in, [SSD_INNER, SSD_INNER + SSD_CONV_DIM], axis=-1)
    xbc = lax.conv_general_dilated(xbc, conv_w[:, None, :].astype(xbc.dtype), window_strides=(1,),
                                   padding=[(SSD_CONV - 1, 0)],
                                   dimension_numbers=('NWC', 'WIO', 'NWC'),
                                   feature_group_count=SSD_CONV_DIM) + conv_b
    xbc = jax.nn.silu(xbc)
    xi, bm, cm = jnp.split(xbc, [SSD_INNER, SSD_INNER + SSD_GROUPS * SSD_STATE], axis=-1)
    f32 = jnp.float32
    dt = jax.nn.softplus(dt.astype(f32) + dt_bias.astype(f32))
    a = -jnp.exp(a_log.astype(f32))
    xi = xi.astype(f32).reshape(b, s, SSD_GROUPS, SSD_HPG, SSD_HEAD_DIM)
    y = ssd_chunked_scan(xi, dt.reshape(b, s, SSD_GROUPS, SSD_HPG), a.reshape(SSD_GROUPS, SSD_HPG),
                         bm.astype(f32).reshape(b, s, SSD_GROUPS, SSD_STATE),
                         cm.astype(f32).reshape(b, s, SSD_GROUPS, SSD_STATE))
    y = y + d_skip.astype(f32).reshape(SSD_GROUPS, SSD_HPG)[:, :, None] * xi
    y = y.reshape(b, s, SSD_INNER).astype(h.dtype) * jax.nn.silu(z)
    y = rms_norm(y.reshape(b, s, SSD_GROUPS, SSD_INNER // SSD_GROUPS),
                 norm_g.reshape(SSD_GROUPS, SSD_INNER // SSD_GROUPS)).reshape(b, s, SSD_INNER)
    return y @ w_o

def squared_relu_mlp(h, w_in, w_out):
    return jnp.square(jax.nn.relu(h @ w_in)) @ w_out

def first_inputs(seed: int = 0) -> dict:
    key = jax.random.key(seed)
    ks = jax.random.split(key, 24)
    nrm = jax.random.normal
    f32 = jnp.float32
    d = D_MODEL
    dt = jnp.exp(jax.random.uniform(ks[14], (N_C, SSD_HEADS), f32, np.log(1e-3), np.log(1e-1)))
    return {
        "x": nrm(ks[0], (BATCH, SEQ, d), f32),
        "norm_mix_g": 1.0 + 0.02 * nrm(ks[1], (DEPTH, d), f32),
        "norm_mlp_g": 1.0 + 0.02 * nrm(ks[2], (DEPTH, d), f32),
        "sb_w_qkv": nrm(ks[3], (N_A, d, 3 * SB_WIDTH), f32) * d ** -0.5,
        "sb_q_norm_g": 1.0 + 0.02 * nrm(ks[4], (N_A, SB_HEAD_DIM), f32),
        "sb_k_norm_g": 1.0 + 0.02 * nrm(ks[5], (N_A, SB_HEAD_DIM), f32),
        "sb_w_o": nrm(ks[6], (N_A, SB_WIDTH, d), f32) * SB_WIDTH ** -0.5,
        "gm_w_in": nrm(ks[7], (N_B, d, 2 * GM_WIDTH), f32) * d ** -0.5,
        "gm_v_norm_g": 1.0 + 0.02 * nrm(ks[8], (N_B, GM_WIDTH), f32),
        "gm_w_s": nrm(ks[9], (N_B, GM_GROUPS, GM_CHUNK, GM_CHUNK), f32) * (1.0 / GM_CHUNK),
        "gm_b_s": 1.0 + 0.02 * nrm(ks[10], (N_B, GM_GROUPS, GM_CHUNK), f32),
        "gm_w_o": nrm(ks[11], (N_B, GM_WIDTH, d), f32) * GM_WIDTH ** -0.5,
        "ssd_w_in": nrm(ks[12], (N_C, d, SSD_PROJ), f32) * d ** -0.5,
        "ssd_conv_w": nrm(ks[13], (N_C, SSD_CONV, SSD_CONV_DIM), f32) * SSD_CONV ** -0.5,
        "ssd_conv_b": 0.02 * nrm(ks[15], (N_C, SSD_CONV_DIM), f32),
        "ssd_dt_bias": dt + jnp.log(-jnp.expm1(-dt)),
        "ssd_a_log": jnp.log(jax.random.uniform(ks[16], (N_C, SSD_HEADS), f32, 1.0, 16.0)),
        "ssd_d": 1.0 + 0.02 * nrm(ks[17], (N_C, SSD_HEADS), f32),
        "ssd_norm_g": 1.0 + 0.02 * nrm(ks[18], (N_C, SSD_INNER), f32),
        "ssd_w_o": nrm(ks[19], (N_C, SSD_INNER, d), f32) * SSD_INNER ** -0.5,
        "mlp_w_in": nrm(ks[20], (DEPTH, d, MLP_HIDDEN), f32) * d ** -0.5,
        "mlp_w_out": nrm(ks[21], (DEPTH, MLP_HIDDEN, d), f32) * MLP_HIDDEN ** -0.5,
    }

def first_block(x, norm_mix_g, norm_mlp_g, sb_w_qkv, sb_q_norm_g, sb_k_norm_g, sb_w_o,
              gm_w_in, gm_v_norm_g, gm_w_s, gm_b_s, gm_w_o,
              ssd_w_in, ssd_conv_w, ssd_conv_b, ssd_dt_bias, ssd_a_log, ssd_d, ssd_norm_g, ssd_w_o,
              mlp_w_in, mlp_w_out):
    h = x
    for i in range(DEPTH):
        kind, j = i % N_MIXERS, i // N_MIXERS
        hn = rms_norm(h, norm_mix_g[i])
        if kind == 0:
            mix = stick_breaking_attention(hn, sb_w_qkv[j], sb_q_norm_g[j], sb_k_norm_g[j], sb_w_o[j])
        elif kind == 1:
            mix = chunked_spatial_gating(hn, gm_w_in[j], gm_v_norm_g[j], gm_w_s[j], gm_b_s[j], gm_w_o[j])
        else:
            mix = ssd_mixer(hn, ssd_w_in[j], ssd_conv_w[j], ssd_conv_b[j], ssd_dt_bias[j],
                            ssd_a_log[j], ssd_d[j], ssd_norm_g[j], ssd_w_o[j])
        h = h + mix
        h = h + squared_relu_mlp(rms_norm(h, norm_mlp_g[i]), mlp_w_in[i], mlp_w_out[i])
    return h


HEAD_DIM = 64
NSA_HEADS = 16
NSA_KV_HEADS = 2
NSA_HPG = NSA_HEADS // NSA_KV_HEADS
CMP_LEN = 32
CMP_STRIDE = 16
CMP_HIDDEN = 128
SLC_BLOCK = 64
N_SELECT = 16
NSA_WINDOW = 512
FORCE_BONUS = 1e4
SWA_HEADS = 16
SWA_KV_HEADS = 2
SWA_HPG = SWA_HEADS // SWA_KV_HEADS
SWA_WINDOW = 128
REL_BUCKETS = 32
REL_EXACT = 16
REL_MAX_DIST = 2048
PEER_HEADS = 8
PEER_NKEYS = 128
PEER_EXPERTS = PEER_NKEYS * PEER_NKEYS
PEER_QDIM = 256
PEER_TOPK = 16
PEER_CHUNK = 128

NEG = -1e30
RMS_EPS = 1e-6
NSA_Q_W = NSA_HEADS * HEAD_DIM
NSA_KV_W = NSA_KV_HEADS * HEAD_DIM
NSA_GATE_W = NSA_HEADS * 3
SWA_Q_W = SWA_HEADS * HEAD_DIM
SWA_KV_W = SWA_KV_HEADS * HEAD_DIM
MIX_WIDTH = NSA_Q_W + SWA_Q_W
PROJ_SPLITS = (NSA_Q_W, NSA_KV_W, NSA_KV_W, NSA_KV_W, NSA_KV_W, NSA_KV_W, NSA_KV_W, NSA_GATE_W, SWA_Q_W, SWA_KV_W, SWA_KV_W)
PROJ_WIDTH = sum(PROJ_SPLITS)
SLC_OFFSETS = (-1, 0, 1, 2, 3)
SLC_WEIGHTS = (1.0, 2.0, 2.0, 2.0, 1.0)


def rmsnorm(x, g):
    xf = x.astype(jnp.float32)
    y = xf * lax.rsqrt(jnp.mean(xf * xf, axis=-1, keepdims=True) + RMS_EPS)
    return (y * g.astype(jnp.float32)).astype(x.dtype)

def rel_bucket(dist):
    d = jnp.maximum(dist, 0)
    n_log = REL_BUCKETS - REL_EXACT
    large = REL_EXACT + (jnp.log(jnp.maximum(d, 1).astype(jnp.float32) / REL_EXACT)
                         / math.log(REL_MAX_DIST / REL_EXACT) * n_log).astype(jnp.int32)
    large = jnp.minimum(large, REL_BUCKETS - 1)
    return jnp.where(d < REL_EXACT, d, large)

def masked_softmax(logits, valid):
    p = jax.nn.softmax(jnp.where(valid, logits, NEG), axis=-1)
    return jnp.where(valid, p, 0.0)

def compress(k, pos, w1, w2):
    B, S, G, Dh = k.shape
    chunks = k.reshape(B, S // CMP_STRIDE, CMP_STRIDE, G, Dh)
    blocks = jnp.concatenate([chunks[:, :-1], chunks[:, 1:]], axis=2)
    blocks = blocks + pos[None, None, :, None, :]
    flat = jnp.moveaxis(blocks, 3, 2).reshape(B, blocks.shape[1], G, CMP_LEN * Dh)
    return jax.nn.gelu(flat @ w1) @ w2

def hybrid_mixer(xn, w_in, cmp_pos_k, cmp_w1_k, cmp_w2_k, cmp_pos_v, cmp_w1_v, cmp_w2_v,
                 sinks, rel_bias, w_out):
    B, S, _ = xn.shape
    f32 = jnp.float32
    GA, GB = NSA_KV_HEADS, SWA_KV_HEADS
    NS = S // SLC_BLOCK
    n_sel = min(N_SELECT, NS)
    scale = HEAD_DIM ** -0.5
    offs = [int(c) for c in np.cumsum(PROJ_SPLITS)[:-1]]
    (q_a, kc, vc, ks, vs, kw, vw, gate_a, q_b, k_b, v_b) = jnp.split(xn @ w_in, offs, axis=-1)

    q_a = q_a.reshape(B, S, GA, NSA_HPG, HEAD_DIM)
    q_b = q_b.reshape(B, S, GB, SWA_HPG, HEAD_DIM)
    gate_a = jax.nn.sigmoid(gate_a).reshape(B, S, GA, NSA_HPG, 3)
    kc_c = compress(kc.reshape(B, S, GA, HEAD_DIM), cmp_pos_k, cmp_w1_k, cmp_w2_k)
    vc_c = compress(vc.reshape(B, S, GA, HEAD_DIM), cmp_pos_v, cmp_w1_v, cmp_w2_v)
    n_cmp = kc_c.shape[1]
    cmp_end = jnp.arange(n_cmp) * CMP_STRIDE + CMP_LEN - 1
    ks_blk = ks.reshape(B, NS, SLC_BLOCK, GA, HEAD_DIM).transpose(0, 3, 1, 2, 4)
    vs_blk = vs.reshape(B, NS, SLC_BLOCK, GA, HEAD_DIM).transpose(0, 3, 1, 2, 4)
    pad_a = ((0, 0), (NSA_WINDOW, 0), (0, 0), (0, 0))
    kw_pad = jnp.pad(kw.reshape(B, S, GA, HEAD_DIM), pad_a)
    vw_pad = jnp.pad(vw.reshape(B, S, GA, HEAD_DIM), pad_a)
    pad_b = ((0, 0), (SWA_WINDOW, 0), (0, 0), (0, 0))
    kb_pad = jnp.pad(k_b.reshape(B, S, GB, HEAD_DIM), pad_b)
    vb_pad = jnp.pad(v_b.reshape(B, S, GB, HEAD_DIM), pad_b)

    bias_a = rel_bias[:, :NSA_HEADS].reshape(REL_BUCKETS, GA, NSA_HPG).astype(f32)
    bias_b = rel_bias[:, NSA_HEADS:].reshape(REL_BUCKETS, GB, SWA_HPG).astype(f32)
    sink = sinks.astype(f32).reshape(1, GB, SWA_HPG, 1, 1)
    b_idx = jnp.arange(B)[:, None, None, None]
    g_idx = jnp.arange(GA)[None, :, None, None]
    blk_ids = jnp.arange(NS)
    slc_tok = jnp.arange(SLC_BLOCK)

    def token_bias(table, dist):
        return table[rel_bucket(dist)].transpose(2, 3, 0, 1)

    def query_block(i):
        q0 = i * Q_BLOCK
        pos_q = q0 + jnp.arange(Q_BLOCK)
        qa = lax.dynamic_slice_in_dim(q_a, q0, Q_BLOCK, axis=1)
        dt = qa.dtype

        dist_c = pos_q[:, None] - cmp_end[None, :]
        lg_c = jnp.einsum('bqghd,bcgd->bghqc', qa, kc_c, preferred_element_type=f32) * scale
        p_cmp = masked_softmax(lg_c + token_bias(bias_a, dist_c), dist_c >= 0)
        o_cmp = jnp.einsum('bghqc,bcgd->bqghd', p_cmp.astype(dt), vc_c)

        imp = jnp.pad(p_cmp.sum(axis=2), ((0, 0), (0, 0), (0, 0), (1, 1)))
        imp_s = jnp.zeros(imp.shape[:-1] + (NS,), f32)
        for r, w in zip(SLC_OFFSETS, SLC_WEIGHTS):
            imp_s = imp_s + w * imp[..., r + 1: r + 2 + 4 * (NS - 1): 4]
        cb = pos_q[:, None] // SLC_BLOCK
        j = blk_ids[None, :]
        forced = (j == 0) | (j == cb) | (j == cb - 1)
        score = jnp.where(j > cb, NEG, imp_s + jnp.where(forced, FORCE_BONUS, 0.0))
        _, sel = lax.top_k(score, n_sel)
        ks_g = ks_blk[b_idx, g_idx, sel].reshape(B, GA, Q_BLOCK, n_sel * SLC_BLOCK, HEAD_DIM)
        vs_g = vs_blk[b_idx, g_idx, sel].reshape(B, GA, Q_BLOCK, n_sel * SLC_BLOCK, HEAD_DIM)
        kpos = (sel[..., None] * SLC_BLOCK + slc_tok).reshape(B, GA, Q_BLOCK, n_sel * SLC_BLOCK)
        dist_s = pos_q[:, None] - kpos
        bias_s = jnp.moveaxis(bias_a[rel_bucket(dist_s), g_idx], -1, 2)
        lg_s = jnp.einsum('bqghd,bgqkd->bghqk', qa, ks_g, preferred_element_type=f32) * scale
        p_s = masked_softmax(lg_s + bias_s, (dist_s >= 0)[:, :, None])
        o_slc = jnp.einsum('bghqk,bgqkd->bqghd', p_s.astype(dt), vs_g)

        La = Q_BLOCK + NSA_WINDOW
        kwin = lax.dynamic_slice_in_dim(kw_pad, q0, La, axis=1)
        vwin = lax.dynamic_slice_in_dim(vw_pad, q0, La, axis=1)
        kpos_w = q0 - NSA_WINDOW + jnp.arange(La)
        dist_w = pos_q[:, None] - kpos_w[None, :]
        valid_w = (dist_w >= 0) & (dist_w < NSA_WINDOW) & (kpos_w[None, :] >= 0)
        lg_w = jnp.einsum('bqghd,blgd->bghql', qa, kwin, preferred_element_type=f32) * scale
        p_w = masked_softmax(lg_w + token_bias(bias_a, dist_w), valid_w)
        o_win = jnp.einsum('bghql,blgd->bqghd', p_w.astype(dt), vwin)

        g = lax.dynamic_slice_in_dim(gate_a, q0, Q_BLOCK, axis=1)
        o_a = g[..., 0:1] * o_cmp + g[..., 1:2] * o_slc + g[..., 2:3] * o_win

        qb = lax.dynamic_slice_in_dim(q_b, q0, Q_BLOCK, axis=1)
        Lb = Q_BLOCK + SWA_WINDOW
        kbw = lax.dynamic_slice_in_dim(kb_pad, q0, Lb, axis=1)
        vbw = lax.dynamic_slice_in_dim(vb_pad, q0, Lb, axis=1)
        kpos_b = q0 - SWA_WINDOW + jnp.arange(Lb)
        dist_b = pos_q[:, None] - kpos_b[None, :]
        valid_b = (dist_b >= 0) & (dist_b < SWA_WINDOW) & (kpos_b[None, :] >= 0)
        lg_b = jnp.einsum('bqghd,blgd->bghql', qb, kbw, preferred_element_type=f32) * scale
        lg_b = jnp.where(valid_b, lg_b + token_bias(bias_b, dist_b), NEG)
        m = jnp.maximum(lg_b.max(axis=-1, keepdims=True), sink)
        e = jnp.exp(lg_b - m)
        p_b = e / (e.sum(axis=-1, keepdims=True) + jnp.exp(sink - m))
        o_b = jnp.einsum('bghql,blgd->bqghd', p_b.astype(dt), vbw)

        return jnp.concatenate([o_a.reshape(B, Q_BLOCK, NSA_Q_W),
                                o_b.reshape(B, Q_BLOCK, SWA_Q_W)], axis=-1)

    out = lax.map(query_block, jnp.arange(S // Q_BLOCK))
    out = out.transpose(1, 0, 2, 3).reshape(B, S, MIX_WIDTH)
    return out @ w_out

def peer(xn, wq, subkeys, u, v):
    B, S, D = xn.shape
    T = B * S
    xt = xn.reshape(T, D)
    q = (xt @ wq).reshape(T, PEER_HEADS, 2, PEER_QDIM // 2).astype(jnp.float32)
    s1 = jnp.einsum('thd,nd->thn', q[:, :, 0], subkeys[0].astype(jnp.float32))
    s2 = jnp.einsum('thd,nd->thn', q[:, :, 1], subkeys[1].astype(jnp.float32))
    v1, i1 = lax.top_k(s1, PEER_TOPK)
    v2, i2 = lax.top_k(s2, PEER_TOPK)
    cand = (v1[..., :, None] + v2[..., None, :]).reshape(T, PEER_HEADS, PEER_TOPK * PEER_TOPK)
    sc, ci = lax.top_k(cand, PEER_TOPK)
    e1 = jnp.take_along_axis(i1, ci // PEER_TOPK, axis=-1)
    e2 = jnp.take_along_axis(i2, ci % PEER_TOPK, axis=-1)
    idx = e1 * PEER_NKEYS + e2
    gate = jax.nn.softmax(sc, axis=-1).astype(xn.dtype)
    n_ch = T // PEER_CHUNK

    def chunk(args):
        xc, ic, gc = args
        h = jax.nn.gelu(jnp.einsum('cd,chkd->chk', xc, u[ic]))
        return jnp.einsum('chk,chkd->cd', gc * h, v[ic])

    out = lax.map(chunk, (xt.reshape(n_ch, PEER_CHUNK, D),
                          idx.reshape(n_ch, PEER_CHUNK, PEER_HEADS, PEER_TOPK),
                          gate.reshape(n_ch, PEER_CHUNK, PEER_HEADS, PEER_TOPK)))
    return out.reshape(B, S, D)

def second_inputs(seed: int = 0) -> dict:
    key = jax.random.key(seed)
    ks = jax.random.split(key, 18)

    def nrm(k, shape, s):
        return jax.random.normal(k, shape, jnp.float32) * s

    return {
        'x': nrm(ks[0], (BATCH, SEQ, D_MODEL), 1.0),
        'attn_norm': 1.0 + nrm(ks[1], (DEPTH, D_MODEL), 0.02),
        'w_in': nrm(ks[2], (DEPTH, D_MODEL, PROJ_WIDTH), D_MODEL ** -0.5),
        'cmp_pos_k': nrm(ks[3], (DEPTH, CMP_LEN, HEAD_DIM), 0.1),
        'cmp_w1_k': nrm(ks[4], (DEPTH, CMP_LEN * HEAD_DIM, CMP_HIDDEN), (CMP_LEN * HEAD_DIM) ** -0.5),
        'cmp_w2_k': nrm(ks[5], (DEPTH, CMP_HIDDEN, HEAD_DIM), CMP_HIDDEN ** -0.5),
        'cmp_pos_v': nrm(ks[6], (DEPTH, CMP_LEN, HEAD_DIM), 0.1),
        'cmp_w1_v': nrm(ks[7], (DEPTH, CMP_LEN * HEAD_DIM, CMP_HIDDEN), (CMP_LEN * HEAD_DIM) ** -0.5),
        'cmp_w2_v': nrm(ks[8], (DEPTH, CMP_HIDDEN, HEAD_DIM), CMP_HIDDEN ** -0.5),
        'sinks': nrm(ks[9], (DEPTH, SWA_HEADS), 0.5),
        'w_out': nrm(ks[10], (DEPTH, MIX_WIDTH, D_MODEL), MIX_WIDTH ** -0.5),
        'ffn_norm': 1.0 + nrm(ks[11], (DEPTH, D_MODEL), 0.02),
        'peer_wq': nrm(ks[12], (DEPTH, D_MODEL, PEER_HEADS * PEER_QDIM), D_MODEL ** -0.5),
        'peer_subkeys': nrm(ks[13], (DEPTH, 2, PEER_NKEYS, PEER_QDIM // 2), (PEER_QDIM // 2) ** -0.5),
        'peer_u': nrm(ks[14], (DEPTH, PEER_EXPERTS, D_MODEL), D_MODEL ** -0.5),
        'peer_v': nrm(ks[15], (DEPTH, PEER_EXPERTS, D_MODEL), (PEER_HEADS * PEER_TOPK) ** -0.5),
        'rel_bias': nrm(ks[16], (REL_BUCKETS, NSA_HEADS + SWA_HEADS), 0.5),
        'final_norm': 1.0 + nrm(ks[17], (D_MODEL,), 0.02),
    }

def second_block(x, attn_norm, w_in, cmp_pos_k, cmp_w1_k, cmp_w2_k, cmp_pos_v, cmp_w1_v, cmp_w2_v,
              sinks, w_out, ffn_norm, peer_wq, peer_subkeys, peer_u, peer_v, rel_bias, final_norm):
    h = x
    for l in range(DEPTH):
        h = h + hybrid_mixer(rmsnorm(h, attn_norm[l]), w_in[l],
                             cmp_pos_k[l], cmp_w1_k[l], cmp_w2_k[l],
                             cmp_pos_v[l], cmp_w1_v[l], cmp_w2_v[l],
                             sinks[l], rel_bias, w_out[l])
        h = h + peer(rmsnorm(h, ffn_norm[l]), peer_wq[l], peer_subkeys[l], peer_u[l], peer_v[l])
    return rmsnorm(h, final_norm)


def setup_inputs(seed=0):
    out = dict(first_inputs(seed))
    for name, value in second_inputs(seed + 1).items():
        if name != "x":
            out[name + "_2"] = value
    return out


def reference(
    x, norm_mix_g, norm_mlp_g, sb_w_qkv, sb_q_norm_g, sb_k_norm_g, sb_w_o, gm_w_in, gm_v_norm_g,
    gm_w_s, gm_b_s, gm_w_o, ssd_w_in, ssd_conv_w, ssd_conv_b, ssd_dt_bias, ssd_a_log, ssd_d,
    ssd_norm_g, ssd_w_o, mlp_w_in, mlp_w_out, attn_norm_2, w_in_2, cmp_pos_k_2, cmp_w1_k_2,
    cmp_w2_k_2, cmp_pos_v_2, cmp_w1_v_2, cmp_w2_v_2, sinks_2, w_out_2, ffn_norm_2, peer_wq_2,
    peer_subkeys_2, peer_u_2, peer_v_2, rel_bias_2, final_norm_2,
):
    x = first_block(
        x, norm_mix_g, norm_mlp_g, sb_w_qkv, sb_q_norm_g, sb_k_norm_g, sb_w_o, gm_w_in,
        gm_v_norm_g, gm_w_s, gm_b_s, gm_w_o, ssd_w_in, ssd_conv_w, ssd_conv_b, ssd_dt_bias,
        ssd_a_log, ssd_d, ssd_norm_g, ssd_w_o, mlp_w_in, mlp_w_out,
    )
    return second_block(
        x, attn_norm_2, w_in_2, cmp_pos_k_2, cmp_w1_k_2, cmp_w2_k_2, cmp_pos_v_2, cmp_w1_v_2,
        cmp_w2_v_2, sinks_2, w_out_2, ffn_norm_2, peer_wq_2, peer_subkeys_2, peer_u_2, peer_v_2,
        rel_bias_2, final_norm_2,
    )


_drawn_inputs = setup_inputs


def setup_inputs(seed=0):
    import zlib

    import numpy as np

    out = dict(_drawn_inputs(seed))
    spreads = {}
    factors = {'norm_mix_g': 3.796,
     'norm_mlp_g': 3.281,
     'sb_q_norm_g': 8.0,
     'sb_k_norm_g': 8.0,
     'attn_norm_2': 8.0,
     'cmp_pos_k_2': 8.0,
     'cmp_pos_v_2': 27.356,
     'sinks_2': 64.0,
     'ffn_norm_2': 64.0,
     'final_norm_2': 7.81}
    for name, (base, spread) in spreads.items():
        noise = np.random.default_rng([zlib.crc32(name.encode()), seed]).standard_normal(out[name].shape)
        drawn = base * np.exp(spread * noise) if base else spread * noise
        out[name] = jnp.asarray(drawn.astype(out[name].dtype))
    for name, factor in factors.items():
        out[name] = (out[name] * factor).astype(out[name].dtype)
    return out
```

```python
from contextlib import ExitStack

import concourse.bass as bass
import numpy as np
from concourse import mybir

F32 = mybir.dt.float32
F32R = mybir.dt.float32r
U32 = mybir.dt.uint32
ACT = mybir.ActivationFunctionType
ALU = mybir.AluOpType
AX = mybir.AxisListType

P = 128
SEQ = 256
TT = SEQ // P
D = 2048
DK = D // P
EPS = 1e-6
NEG = -1e30
PANEL = 1024
BANK = 512

HEADS1 = 16
HEADS2 = 16
HD2 = 64
GROUPS2 = 2
HPG2 = HEADS2 // GROUPS2
MLP = 4 * D
CMP_BLOCKS = 15
CMP_STRIDE = 16
CMP_LEN = 32
SWA_WINDOW = 128
PEER_HEADS = 8
NKEYS = 128
TOPK = 16
SLOTS = PEER_HEADS * TOPK
LOWEST = -3.0e38

W2_QA, W2_KV, W2_QB, W2_KVB = 0, 1024, 1840, 2864
KV_KC, KV_VC, KV_KS, KV_VS, KV_KW, KV_VW, KV_GATE = 0, 128, 256, 384, 512, 640, 768

TOE = 384
C_IDENT, C_FLIP, C_STICK, C_TRI, C_ONES, C_IOTA, C_BLOCK = 0, 128, 256, 384, 512, 640, 656
C_ROWOK, C_END = 664, 665
C_OHA, C_OHB, C_OHC = 0, TOE, 2 * TOE
OHC_BASE = 256
OH_END = C_OHC + 512


def rel_bucket(dist):
    d = np.maximum(dist, 0)
    large = 16 + (np.log(np.maximum(d, 1).astype(np.float32) / np.float32(16)) / np.float32(np.log(128.0))
                  * np.float32(16)).astype(np.int32)
    return np.where(d < 16, d, np.minimum(large, 31))


def constants():
    c = np.zeros((P, C_END), np.float32)
    r = np.arange(P)
    c[:, C_IDENT:C_IDENT + P] = np.eye(P)
    c[:, C_FLIP:C_FLIP + P] = np.eye(P)[::-1]
    c[:, C_STICK:C_STICK + P] = np.where(r[:, None] < r[None, :], 0.0, NEG)
    c[:, C_TRI:C_TRI + P] = r[:, None] >= r[None, :]
    c[:, C_ONES:C_ONES + P] = 1.0
    c[:, C_IOTA:C_IOTA + TOPK] = np.arange(TOPK)
    for h in range(HPG2):
        c[h * CMP_BLOCKS:(h + 1) * CMP_BLOCKS, C_BLOCK + h] = 1.0
    c[:, C_ROWOK] = r >= CMP_LEN - 1
    return c


def onehots():
    c = np.zeros((33, OH_END), np.float32)
    dist = 255 - np.arange(TOE)
    for col, bad in ((C_OHA, dist < 0), (C_OHB, (dist < 0) | (dist >= SWA_WINDOW))):
        c[np.where(bad, 32, rel_bucket(dist)), col + np.arange(TOE)] = 1.0
    dist = np.arange(512) - OHC_BASE
    c[np.where(dist < 0, 32, rel_bucket(dist)), C_OHC + np.arange(512)] = 1.0
    return c


class Line:

    def __init__(self, sem=None):
        self.sem, self.count, self.steps, self.met = sem, 0, [], {}

    def wait(self, *tokens):
        for sem, value in tokens:
            if self.met.get(sem, 0) < value:
                self.met[sem] = value
                self.steps.append(lambda e, s=sem, v=value: e.wait_ge(s, v))

    def do(self, make, *after):
        self.wait(*after)
        self.count += 1
        self.steps.append(lambda e, s=self.sem: make(e).then_inc(s, 1))
        return (self.sem, self.count)

    def then(self, make, *after):
        if self.count:
            self.wait((self.sem, self.count))
        return self.do(make, *after)

    def quiet(self, make, *after):
        self.wait(*after)
        self.steps.append(lambda e: make(e))

    def run(self, e):
        for step in self.steps:
            step(e)


def build(nc, ins, out):
    with ExitStack() as ctx:
        def sb(name, shape, dt=F32):
            return ctx.enter_context(nc.sbuf_tensor(name, shape, dt))

        def sem(name):
            return ctx.enter_context(nc.semaphore(name))

        act_hi = sb("act_hi", [P, DK, SEQ], F32R)
        act_lo = sb("act_lo", [P, DK, SEQ], F32R)
        hid_hi = sb("hid_hi", [P, PANEL // P, SEQ], F32R)
        hid_lo = sb("hid_lo", [P, PANEL // P, SEQ], F32R)
        NSPLIT = 2
        w_hi = sb("w_hi", [P, NSPLIT, PANEL], F32R)
        w_lo = sb("w_lo", [P, NSPLIT, PANEL], F32R)
        RING = 8
        ring = sb("ring", [P, RING, PANEL])
        resid = sb("resid", [P, TT, D])
        panels = sb("panels", [P, 2, TT, PANEL])
        WORK = 17408
        work = sb("work", [P, WORK])
        stat = sb("stat", [P, 448])
        table = sb("table", [33, 32])
        biascmp = sb("biascmp", [P, TT, CMP_BLOCKS, HEADS2])
        qk_gain = sb("qk_gain", [P, 2, P])
        sink = sb("sink", [P, HEADS2])
        const = sb("const", [P, C_END])
        top_pos = sb("top_pos", [P, 2 * PEER_HEADS, TOPK], U32)
        cand_pos = sb("cand_pos", [P, 2, SLOTS], U32)
        expert = sb("expert", [P, TT, SLOTS], U32)
        acc = [ctx.enter_context(nc.psum_tensor(f"acc{i}", [P, BANK], F32)) for i in range(4)]
        wk = [ctx.enter_context(nc.psum_tensor(f"wk{i}", [P, BANK], F32)) for i in range(4)]
        bias_rows = nc.dram_tensor("bias_rows", [2 * HEADS2, TOE], F32, kind="Internal").ap()

        def region(at, *shape):
            n = int(np.prod(shape))
            v = work[:, at:at + n]
            if len(shape) == 1:
                return v
            names = "abcd"[:len(shape)]
            return v.rearrange(f"p ({' '.join(names)}) -> p {' '.join(names)}", **dict(zip(names, shape)))

        def cst(at, n=P):
            return const[:, at:at + n]

        ident, flip = cst(C_IDENT), cst(C_FLIP)
        gain = region(15360, D)

        pe, act, dve, pool, sp = (Line(sem("pe")), Line(sem("act")), Line(sem("dve")), Line(sem("pool")), Line())
        landing = [sem(f"chunk{i}") for i in range(RING)]
        landed = [0] * RING

        def load(dst, src, *after, name):
            s = sem(name)
            sp.wait(*after)
            sp.steps.append(lambda e: e.dma_start(dst, src).then_inc(s, 16))
            return (s, 16)

        acc_free = [()] * 4
        wk_free = [()] * 4
        ring_free = [()] * RING
        split_free = [()] * NSPLIT
        state = {"chunk": 0, "post": None}

        def gemm_panel(w, row0, nk, col0, width, hi, lo, after_x):
            cuts = [(n, min(BANK, width - n)) for n in range(0, width, BANK)]
            for k in range(nk):
                c = state["chunk"]
                state["chunk"] += 1
                s, b = c % RING, c % NSPLIT
                sp.wait(*ring_free[s])
                src, dst = w[row0 + k * P:row0 + (k + 1) * P, col0:col0 + width], ring[:, s, :width]
                sp.steps.append(lambda e, d=dst, r=src, m=landing[s]: e.dma_start(d, r).then_inc(m, 16))
                landed[s] += 16
                there = (landing[s], landed[s])
                high = act.do(lambda e, s=s, b=b: e.activation(w_hi[:, b, :width], ring[:, s, :width], ACT.Copy),
                              there, *split_free[b])
                low = dve.do(lambda e, s=s, b=b: e.tensor_tensor(w_lo[:, b, :width], ring[:, s, :width],
                                                                 w_hi[:, b, :width].bitcast(F32), ALU.subtract),
                             high, there, *split_free[b])
                ring_free[s] = (low,)
                pe.wait(*after_x, high)
                for t in range(TT):
                    xs = [x[:, k, t * P:(t + 1) * P] for x in (hi, lo)]
                    for i, (x, wp) in enumerate(((xs[0], w_hi), (xs[0], w_lo), (xs[1], w_hi))):
                        if i == 1:
                            pe.wait(low)
                        for j, (n, m) in enumerate(cuts):
                            if k == 0 and i == 0:
                                pe.wait(*acc_free[2 * t + j])
                            mm = (lambda e, x=x, wp=wp, j=j, t=t, n=n, m=m, i=i, k=k, b=b: e.matmul(
                                acc[2 * t + j][:, :m], x, wp[:, b, n:n + m],
                                start=(k == 0 and i == 0), stop=(k == nk - 1 and i == 2)))
                            if (t, i, j) == (TT - 1, 2, len(cuts) - 1):
                                done = pe.do(mm)
                            else:
                                pe.quiet(mm)
                split_free[b] = (done,)
                if k == 2 and state["post"]:
                    post, state["post"] = state["post"], None
                    post()
            return done

        def flush():
            if state["post"]:
                post, state["post"] = state["post"], None
                post()

        def take_panel(width, done, store, *after):
            tokens = []
            for t in range(TT):
                for j, n in enumerate(range(0, width, BANK)):
                    bank = 2 * t + j
                    tok = store(t, n, min(BANK, width - n), acc[bank], done, *after)
                    acc_free[bank] = (tok,)
                    tokens.append(tok)
            return tokens

        def store_copy(dst):
            def store(t, n, m, bank, *after):
                if n == 0:
                    return act.do(lambda e: e.activation(dst[:, t, n:n + m], bank[:, :m], ACT.Copy), *after)
                return dve.do(lambda e: e.tensor_copy(dst[:, t, n:n + m], bank[:, :m]), *after)
            return store

        def transposes(srcs, bank, *after):
            pe.wait(*after, *wk_free[bank])
            for i, src in enumerate(srcs):
                f = (lambda e, i=i, src=src: e.transpose(wk[bank][:, i * P:(i + 1) * P], src, ident))
                if i == len(srcs) - 1:
                    return pe.do(f)
                pe.quiet(f)

        def split_transposed(src, nk, hi, lo, *after, square=None):
            tokens = []
            for t in range(TT):
                for k0 in range(0, nk, 4):
                    bank = (t * nk + k0) // 4 % 4
                    there = transposes([src(t)[:, k * P:(k + 1) * P] for k in range(k0, k0 + 4)], bank, *after)
                    grid = wk[bank][:, :].rearrange("p (k q) -> p k q", k=4)
                    to = lambda x, k0=k0, t=t: x[:, k0:k0 + 4, t * P:(t + 1) * P]
                    if square is None:
                        h = act.do(lambda e, to=to, grid=grid: e.activation(to(hi), grid, ACT.Copy), there)
                        l = dve.do(lambda e, to=to, grid=grid: e.tensor_tensor(
                            to(lo), grid, to(hi).bitcast(F32), ALU.subtract), h)
                        wk_free[bank] = (l,)
                    else:
                        b = square[:, bank % 2, :].rearrange("p (k q) -> p k q", k=4)
                        sq = act.do(lambda e, b=b, grid=grid: e.activation(b, grid, ACT.Square),
                                    there, *tokens[-2:-1])
                        wk_free[bank] = (sq,)
                        h = act.then(lambda e, to=to, b=b: e.activation(to(hi), b, ACT.Copy))
                        l = dve.do(lambda e, to=to, b=b: e.tensor_tensor(
                            to(lo), b, to(hi).bitcast(F32), ALU.subtract), h)
                    tokens.append(l)
            return tokens[-1:] + [h]

        ss, rs = stat[:, 0:2], stat[:, 2:4]

        def inv_rms(total, width, dst, *after):
            a = dve.then(lambda e: e.tensor_scalar(dst, total, 1.0 / width, EPS, ALU.mult, ALU.add), *after)
            b = act.then(lambda e: e.activation(dst, dst, ACT.Sqrt), a)
            return dve.then(lambda e: e.reciprocal(dst, dst), b)

        def norm(dst, gain_there, *after):
            for t in range(TT):
                sq = act.then(lambda e, t=t: e.activation(dst[:, t, :], resid[:, t, :], ACT.Square,
                                                          accum_out=ss[:, t:t + 1]), *after)
            r = inv_rms(ss, D, rs, sq)
            return [dve.then(lambda e, t=t: e.scalar_tensor_tensor(dst[:, t, :], resid[:, t, :], rs[:, t:t + 1], gain,
                                                                   ALU.mult, ALU.mult), gain_there)
                    for t in range(TT)]

        def spread(row, n=D):
            return bass.AP(tensor=row.tensor, offset=0, ap=[[0, P], [1, n]])

        wide = panels[:, :, :, :].rearrange("p b t n -> p (b t n)").rearrange("p (t n) -> p t n", t=TT)
        slab = lambda b: panels[:, b, :, :]

        x_there = load(resid[:, :, :], ins["x"].rearrange("b (t p) d -> p (b t) d", p=P), name="x_in")
        gain1_there = load(gain, spread(ins["norm_mix_g"]), name="gain1_in")
        const_there = load(const[:, :], ins["const"], name="const_in")
        qg_there = load(qk_gain[:, 0, :], spread(ins["sb_q_norm_g"], P), name="qgain_in")
        kg_there = load(qk_gain[:, 1, :], spread(ins["sb_k_norm_g"], P), name="kgain_in")
        sink_there = load(sink[:, :], spread(ins["sinks_2"], HEADS2), name="sink_in")
        onehot_b = work[:33, 2048:2048 + OH_END]
        onehot_there = load(onehot_b, ins["onehot"], name="onehot_in")
        neg_row = dve.do(lambda e: e.memset(table[:, :], NEG))
        table_there = load(table[0:32, :], ins["rel_bias_2"], neg_row, name="table_in")

        normed = norm(wide, gain1_there, x_there)
        x_ready = split_transposed(lambda t: wide[:, t, :], DK, act_hi, act_lo, *normed, const_there)

        bias_sb = work[:HEADS2, 0:2 * TOE].rearrange("p (a n) -> p a n", a=2)
        for half, oh in ((0, C_OHA), (1, C_OHB)):
            rows = pe.do(lambda e, half=half, oh=oh: e.matmul(
                wk[half][:HEADS2, :TOE], table[:, half * 16:half * 16 + 16], onehot_b[:, oh:oh + TOE],
                start=True, stop=True), table_there, onehot_there, *wk_free[half])
            taken = dve.do(lambda e, half=half: e.tensor_copy(bias_sb[:, half, :], wk[half][:HEADS2, :TOE]), rows)
            wk_free[half] = (taken,)
        bias_out = sem("bias_out")
        sp.wait(taken)
        sp.steps.append(lambda e: e.dma_start(bias_rows.rearrange("(a h) n -> h a n", a=2), bias_sb)
                        .then_inc(bias_out, 16))
        bias_written = (bias_out, 16)

        for t in range(TT):
            pe.wait(*wk_free[2 + t])
            for c in range(CMP_BLOCKS):
                col = C_OHC + OHC_BASE + t * P - CMP_STRIDE * c - (CMP_LEN - 1)
                f = (lambda e, t=t, c=c, col=col: e.matmul(
                    wk[2 + t][:, c * HEADS2:(c + 1) * HEADS2], onehot_b[:, col:col + P], table[:, 0:HEADS2],
                    start=True, stop=True))
                rows = pe.do(f) if c == CMP_BLOCKS - 1 else pe.quiet(f)
            taken = dve.do(lambda e, t=t: e.tensor_copy(
                biascmp[:, t, :, :].rearrange("p c h -> p (c h)"), wk[2 + t][:, :CMP_BLOCKS * HEADS2]), rows)
            wk_free[2 + t] = (taken,)

        q_t, k_t = region(0, HEADS1, SEQ), region(4096, HEADS1, SEQ)
        v_tok = region(8192, TT, D)
        w_qkv = ins["sb_w_qkv"][0]
        scale1 = float(P) ** -0.5
        sum8, inv8 = stat[:, 8:24].rearrange("p (t h) -> p t h", t=TT), stat[:, 24:40].rearrange("p (t h) -> p t h", t=TT)
        head_ready = {}
        slab_free = [(), ()]

        def heads_post(panel, stored, dst, which, scale):
            def post():
                v = slab(panel % 2)
                heads = v.rearrange("p t (h d) -> p t h d", d=P)
                last = None
                for t in range(TT):
                    sq = act.then(lambda e, t=t: e.activation(work[:, 12288:13312], v[:, t, :], ACT.Square), *stored)
                    sm = dve.then(lambda e, t=t: e.tensor_reduce(sum8[:, t, :], work[:, 12288:13312].rearrange(
                        "p (h d) -> p h d", d=P), AX.X, ALU.add), sq)
                    act.wait(sm)
                inv_rms(sum8.rearrange("p t h -> p (t h)"), P, inv8.rearrange("p t h -> p (t h)"), sm)
                for t in range(TT):
                    dve.then(lambda e, t=t: e.tensor_tensor(
                        heads[:, t], heads[:, t], inv8[:, t, :].unsqueeze(2).to_broadcast([P, 8, P]), ALU.mult))
                    last = dve.then(lambda e, t=t: e.scalar_tensor_tensor(
                        heads[:, t], heads[:, t], scale, qk_gain[:, which, :].unsqueeze(1).to_broadcast([P, 8, P]),
                        ALU.mult, ALU.mult), qg_there, kg_there)
                tokens = []
                for t in range(TT):
                    for k0 in (0, 4):
                        bank = 2 * t + k0 // 4
                        there = transposes([v[:, t, k * P:(k + 1) * P] for k in range(k0, k0 + 4)], bank, last)
                        h0 = (panel % 2) * 8 + k0
                        tok = act.do(lambda e, h0=h0, t=t, bank=bank: e.activation(
                            dst[:, h0:h0 + 4, t * P:(t + 1) * P], wk[bank][:, :].rearrange("p (k q) -> p k q", k=4),
                            ACT.Copy), there, bias_written)
                        wk_free[bank] = (tok,)
                slab_free[panel % 2] = (tok,)
                head_ready[panel] = tok
            return post

        for panel in range(4):
            done = gemm_panel(w_qkv, 0, DK, panel * PANEL, PANEL, act_hi, act_lo, x_ready)
            stored = take_panel(PANEL, done, store_copy(slab(panel % 2)), *slab_free[panel % 2], *normed)
            state["post"] = heads_post(panel, stored, q_t if panel < 2 else k_t, panel // 2,
                                       scale1 if panel < 2 else 1.0)
        v_stored = []
        for panel in range(2):
            done = gemm_panel(w_qkv, 0, DK, 2 * D + panel * PANEL, PANEL, act_hi, act_lo, x_ready)
            v_stored += take_panel(PANEL, done, store_copy(v_tok[:, :, panel * PANEL:(panel + 1) * PANEL]), bias_written)
        act_free = (done,)

        GH = 4
        COLS = SEQ + P
        z_a, z_b = region(12288, GH, COLS), region(13824, GH, COLS)
        pair_free = {0: (), 1: ()}
        stick, tri, ones = cst(C_STICK), cst(C_TRI), cst(C_ONES)
        for g in range(HEADS1 // GH):
            z_done = []
            for i in range(GH):
                h = g * GH + i
                z = acc[i]
                pe.wait(*acc_free[i], head_ready[0], head_ready[1], head_ready[2], head_ready[3])
                m = dict(skip_group_check=True)
                pe.quiet(lambda e, z=z, h=h: e.matmul(z[:, :SEQ], k_t[:, h, :P], q_t[:, h, :], start=True, stop=False, **m))
                pe.quiet(lambda e, z=z, h=h: e.matmul(z[:, SEQ:COLS], k_t[:, h, P:], q_t[:, h, P:], start=False, stop=False, **m))
                pe.quiet(lambda e, z=z: e.matmul(z[:, :P], ident, stick, start=False, stop=False, **m))
                z_done.append(pe.do(lambda e, z=z: e.matmul(z[:, SEQ:COLS], ident, stick, start=False, stop=True, **m)))
            for i in range(GH):
                act.do(lambda e, i=i: e.activation(z_a[:, i, :], acc[i][:, :COLS], ACT.Abs), z_done[i], *pair_free[0])
            act.then(lambda e: e.activation(z_a, z_a, ACT.Exp, scale=-1.0))
            ln = act.then(lambda e: e.activation(z_a, z_a, ACT.Ln, bias=1.0))
            for i in range(GH):
                dve.do(lambda e, i=i: e.scalar_tensor_tensor(z_b[:, i, :], acc[i][:, :COLS], 0.0, z_a[:, i, :],
                                                             ALU.max, ALU.add), ln, *pair_free[1])
            neg = dve.then(lambda e: e.tensor_scalar(z_b, z_b, -1.0, None, ALU.mult))
            s_done = []
            for i in range(GH):
                z = acc[i]
                pe.wait(neg)
                pe.quiet(lambda e, z=z, i=i: e.matmul(z[:, :SEQ], tri, z_b[:, i, :SEQ], start=False, stop=False, **m))
                pe.quiet(lambda e, z=z, i=i: e.matmul(z[:, P:SEQ], ones, z_b[:, i, SEQ:], start=False, stop=False, **m))
                s_done.append(pe.do(lambda e, z=z, i=i: e.matmul(z[:, SEQ:COLS], tri, z_b[:, i, SEQ:], start=False,
                                                                 stop=True, **m)))
            a_done = []
            for i in range(GH):
                tok = act.do(lambda e, i=i: e.activation(z_a[:, i, :], acc[i][:, :COLS], ACT.Exp), s_done[i], neg)
                acc_free[i] = (tok,)
                a_done.append(tok)
            pair_free[1] = (s_done[-1],)
            for i in range(0, GH, 2):
                bank = (2 * g + i // 2) % 4
                o = wk[bank]
                pe.wait(a_done[i], a_done[i + 1], *v_stored, *wk_free[bank])
                for j in range(2):
                    h = g * GH + i + j
                    v0, v1 = (v_tok[:, t, h * P:(h + 1) * P] for t in range(TT))
                    c = j * SEQ
                    pe.quiet(lambda e, o=o, c=c, v0=v0, n=i + j: e.matmul(
                        o[:, c:c + SEQ], v0, z_a[:, n, :SEQ], start=True, stop=False, **m))
                    o_done = pe.do(lambda e, o=o, c=c, v1=v1, n=i + j: e.matmul(
                        o[:, c + P:c + SEQ], v1, z_a[:, n, SEQ:], start=False, stop=True, **m))
                h0 = g * GH + i
                grid = o[:, :].rearrange("p (k q) -> p k q", k=2)
                hi = act.do(lambda e, h0=h0, grid=grid: e.activation(act_hi[:, h0:h0 + 2, :], grid, ACT.Copy),
                            o_done, *act_free)
                lo = dve.do(lambda e, h0=h0, grid=grid: e.tensor_tensor(
                    act_lo[:, h0:h0 + 2, :], grid, act_hi[:, h0:h0 + 2, :].bitcast(F32), ALU.subtract), hi)
                wk_free[bank] = (lo,)
            pair_free[0] = (o_done,)
        o_ready = [hi, lo]

        def store_residual(panel):
            def store(t, n, m, bank, *after):
                at = resid[:, t, panel * PANEL + n:panel * PANEL + n + m]
                return dve.do(lambda e: e.tensor_tensor(at, bank[:, :m], at, ALU.add), *after)
            return store

        gain2_there = load(gain, spread(ins["norm_mlp_g"]), *normed, name="gain2_in")
        added = []
        for panel in range(2):
            done = gemm_panel(ins["sb_w_o"][0], 0, DK, panel * PANEL, PANEL, act_hi, act_lo, o_ready)
            added += take_panel(PANEL, done, store_residual(panel))
        act_free = (done,)

        normed = norm(wide, gain2_there, *added, *slab_free[0], *slab_free[1])
        x_ready = split_transposed(lambda t: wide[:, t, :], DK, act_hi, act_lo, *normed, *act_free)
        square = region(0, 2, BANK)
        slab_free = [tuple(x_ready), tuple(x_ready)]
        hid_state = {"free": ()}
        added = []

        def store_relu(dst):
            def store(t, n, m, bank, *after):
                if n == 0:
                    return act.do(lambda e: e.activation(dst[:, t, n:n + m], bank[:, :m], ACT.Relu), *after)
                return dve.do(lambda e: e.tensor_scalar(dst[:, t, n:n + m], bank[:, :m], 0.0, None, ALU.max), *after)
            return store

        def hidden_out(j, hid_ready):
            for panel in range(2):
                done = gemm_panel(ins["mlp_w_out"][0], j * PANEL, PANEL // P, panel * PANEL, PANEL, hid_hi, hid_lo,
                                  hid_ready)
                added[:] = added[-4:] + take_panel(PANEL, done, store_residual(panel))
            hid_state["free"] = (done,)

        NH = MLP // PANEL
        for j in range(NH):
            done = gemm_panel(ins["mlp_w_in"][0], 0, DK, j * PANEL, PANEL, act_hi, act_lo, x_ready)
            stored = take_panel(PANEL, done, store_relu(slab(j % 2)), *slab_free[j % 2])
            if j > 0:
                hidden_out(j - 1, hid_ready)
            v = slab(j % 2)
            hid_ready = split_transposed(lambda t: v[:, t, :], PANEL // P, hid_hi, hid_lo, *stored, *hid_state["free"],
                                         square=square)
            slab_free[j % 2] = tuple(hid_ready)
        act_free = (done,)
        hidden_out(NH - 1, hid_ready)

        gain3_there = load(gain, spread(ins["attn_norm_2"]), *normed, name="gain3_in")
        normed = norm(wide, gain3_there, *added, *slab_free[0], *slab_free[1])
        x_ready = split_transposed(lambda t: wide[:, t, :], DK, act_hi, act_lo, *normed, *act_free)

        q2_t = region(0, HEADS2, SEQ)
        kz = region(4096, 3, GROUPS2, 2, SEQ)
        kvg = region(7168, TT, 816)
        kvb = region(8800, TT, 256)
        ckv_t = region(9312, 2, GROUPS2, SEQ)
        v_block = region(9312, GROUPS2, BANK)
        flat = region(10336, DK, GROUPS2 * CMP_BLOCKS)
        w1 = region(10816, 2, DK, P)
        bias_a = region(10816, HEADS2, SEQ)
        e_buf = region(14912, 2, BANK)
        et_buf = region(15936, 2, BANK)
        twice = region(16960, 2, P)
        ckz = region(17216, GROUPS2, 2, CMP_BLOCKS + 1)
        cmp_hid = region(17280, 2 * CMP_BLOCKS)
        pos_t = stat[:, 64:64 + 2 * DK].rearrange("p (a k) -> p a k", a=2)

        clear = dve.then(lambda e: e.memset(region(4096, 3072), 0.0), *x_ready, *acc_free[0])
        clear2 = dve.then(lambda e: e.memset(region(17216, 64), 0.0), *normed)
        w1_there = [load(w1[:, i, :, :], ins[n][0].rearrange("(k p) h -> p k h", p=P), *x_ready, name=n + "_in")
                    for i, n in enumerate(("cmp_w1_k_2", "cmp_w1_v_2"))]
        pos_there = [load(stat[i * DK:(i + 1) * DK, 100:228], ins[n][0].rearrange("(k l) d -> k (l d)", l=2),
                          name=n + "_in") for i, n in enumerate(("cmp_pos_k_2", "cmp_pos_v_2"))]
        w2_there = [load(stat[:, 228 + 64 * i:292 + 64 * i], ins[n][0], name=n + "_in")
                    for i, n in enumerate(("cmp_w2_k_2", "cmp_w2_v_2"))]
        w2 = stat[:, 228:356].rearrange("p (a d) -> p a d", a=2)

        w_in2 = ins["w_in_2"][0]

        def pairs_post(panel, stored, first):
            def post():
                v = slab(panel)
                for t in range(TT):
                    for k0 in (0, 4):
                        bank = 2 * t + k0 // 4
                        there = transposes([v[:, t, k * P:(k + 1) * P] for k in range(k0, k0 + 4)], bank, *stored)
                        tok = act.do(lambda e, k0=k0, t=t, bank=bank: e.activation(
                            q2_t[:, first + k0:first + k0 + 4, t * P:(t + 1) * P],
                            wk[bank][:, :].rearrange("p (k q) -> p k q", k=4), ACT.Copy, scale=HD2 ** -0.5), there)
                        wk_free[bank] = (tok,)
                head_ready[10 + panel] = tok
            return post

        twice_free = [(), ()]

        def doubled(src, col, g, t, bank, n, *after):
            tw = twice[:, n % 2, :].rearrange("p (a d) -> p a d", a=2)
            cp = dve.then(lambda e: e.tensor_copy(tw, src[:, t, col + g * HD2:col + (g + 1) * HD2].unsqueeze(1)
                                                  .to_broadcast([P, 2, HD2])), *after, *twice_free[n % 2])
            there = transposes([twice[:, n % 2, :]], bank, cp)
            twice_free[n % 2] = (there,)
            return there

        def keys_to(src, col, which, *after):
            for g in range(GROUPS2):
                for t in range(TT):
                    bank = (2 * g + t) % 4
                    there = doubled(src, col, g, t, bank, t, *after)
                    for half in range(2):
                        rows = slice(half * HD2, (half + 1) * HD2)
                        tok = dve.then(lambda e, g=g, t=t, half=half, rows=rows, bank=bank: e.tensor_copy(
                            kz[rows, which, g, half, t * P:(t + 1) * P], wk[bank][rows, :P]), there, clear)
                    wk_free[bank] = (tok,)
            return tok

        done = gemm_panel(w_in2, 0, DK, W2_QA, PANEL, act_hi, act_lo, x_ready)
        stored = take_panel(PANEL, done, store_copy(slab(0)), *x_ready)
        state["post"] = pairs_post(0, stored, 0)
        done = gemm_panel(w_in2, 0, DK, W2_KV, 816, act_hi, act_lo, x_ready)
        kv_stored = take_panel(816, done, store_copy(kvg), *x_ready)
        state["post"] = None
        done = gemm_panel(w_in2, 0, DK, W2_QB, PANEL, act_hi, act_lo, x_ready)
        stored = take_panel(PANEL, done, store_copy(slab(1)), *x_ready)
        state["post"] = pairs_post(1, stored, 8)
        done = gemm_panel(w_in2, 0, DK, W2_KVB, 256, act_hi, act_lo, x_ready)
        kvb_stored = take_panel(256, done, store_copy(kvb), *x_ready)
        act_free = (done,)

        k_ready = [keys_to(kvg, KV_KS, 0, *kv_stored), keys_to(kvg, KV_KW, 1), keys_to(kvb, 0, 2, *kvb_stored)]

        pos_turned = pe.do(lambda e: e.transpose(wk[0][:, :2 * DK], stat[:2 * DK, 100:228], ident[:2 * DK, :2 * DK]),
                           *pos_there, *wk_free[0])
        pos_ready = dve.then(lambda e: e.tensor_copy(pos_t.rearrange("p a k -> p (a k)"), wk[0][:, :2 * DK]), pos_turned)
        wk_free[0] = (pos_ready,)
        for which, col in ((0, KV_KC), (1, KV_VC)):
            for g in range(GROUPS2):
                for t in range(TT):
                    bank = (2 * g + t) % 4
                    there = doubled(kvg, col, g, t, bank, t)
                    tok = dve.then(lambda e, w=which, g=g, t=t, bank=bank: e.tensor_copy(
                        ckv_t[:, w, g, t * P:(t + 1) * P], wk[bank][:, :P]), there)
                    wk_free[bank] = (tok,)
        cmp_done = ()
        for which in range(2):
            for g in range(GROUPS2):
                for l in range(2):
                    rows = slice(l * HD2, (l + 1) * HD2)
                    src = ckv_t[rows, which, g, l:l + 1]
                    view = bass.AP(tensor=src.tensor, offset=src.offset, ap=[list(src.ap[0]), [2, DK], [CMP_STRIDE, CMP_BLOCKS]])
                    flat_ready = dve.then(lambda e, g=g, rows=rows, view=view, w=which: e.tensor_tensor(
                        flat[rows, :, g * CMP_BLOCKS:(g + 1) * CMP_BLOCKS], view,
                        pos_t[rows, w, :].unsqueeze(2).to_broadcast([HD2, DK, CMP_BLOCKS]), ALU.add), *cmp_done)
            pe.wait(flat_ready, w1_there[which], *wk_free[0])
            for k in range(DK):
                f = (lambda e, k=k, w=which: e.matmul(wk[0][:, :2 * CMP_BLOCKS], w1[:, w, k, :], flat[:, k, :],
                                                      start=(k == 0), stop=(k == DK - 1)))
                hid = pe.do(f) if k == DK - 1 else pe.quiet(f)
            gel = act.then(lambda e: e.activation(cmp_hid, wk[0][:, :2 * CMP_BLOCKS], ACT.Gelu_apprx_tanh), hid, clear2)
            wk_free[0] = (gel,)
            if which == 0:
                tw = twice[:, 0, :].rearrange("p (a d) -> p a d", a=2)
                cp = dve.then(lambda e: e.tensor_copy(tw, w2[:, 0, :].unsqueeze(1).to_broadcast([P, 2, HD2])),
                              w2_there[0], *twice_free[0])
                ck = pe.do(lambda e: e.matmul(wk[1][:, :2 * CMP_BLOCKS], twice[:, 0, :], cmp_hid, start=True, stop=True),
                           cp, gel, *wk_free[1])
                twice_free[0] = (ck,)
                for half in range(2):
                    rows = slice(half * HD2, (half + 1) * HD2)
                    ck_ready = dve.then(lambda e, rows=rows, half=half: e.tensor_copy(
                        ckz[rows, :, half, :CMP_BLOCKS],
                        wk[1][rows, :2 * CMP_BLOCKS].rearrange("p (g c) -> p g c", g=2)), ck)
                wk_free[1] = (ck_ready,)
                cmp_done = (ck,)
            else:
                for g in range(GROUPS2):
                    rep = e_buf[:, g, :HPG2 * CMP_BLOCKS].rearrange("p (h c) -> p h c", h=HPG2)
                    cp = dve.then(lambda e, g=g, rep=rep: e.tensor_copy(
                        rep, cmp_hid[:, g * CMP_BLOCKS:(g + 1) * CMP_BLOCKS].unsqueeze(1)
                        .to_broadcast([P, HPG2, CMP_BLOCKS])), gel)
                    cv = pe.do(lambda e, g=g: e.matmul(wk[2 + g][:HPG2 * CMP_BLOCKS, :HD2],
                                                       e_buf[:, g, :HPG2 * CMP_BLOCKS], w2[:, 1, :], start=True, stop=True),
                               cp, w2_there[1], *wk_free[2 + g])
                    n = HPG2 * CMP_BLOCKS
                    vb_ready = dve.then(lambda e, g=g, n=n: e.tensor_tensor(
                        v_block[:n, g, :].rearrange("p (h d) -> p h d", h=HPG2),
                        wk[2 + g][:n, :HD2].unsqueeze(1).to_broadcast([n, HPG2, HD2]),
                        const[:n, C_BLOCK:C_BLOCK + HPG2].unsqueeze(2).to_broadcast([n, HPG2, HD2]), ALU.mult), cv)
                    wk_free[2 + g] = (vb_ready,)
        flush()

        gate = sb("gate", [P, TT, HEADS2, 3])
        g1 = act.then(lambda e: e.activation(gate[:, :, :, :].rearrange("p t h c -> p t (h c)"),
                                             kvg[:, :, KV_GATE:KV_GATE + 48], ACT.Exp, scale=-1.0), *kv_stored)
        gflat = gate[:, :, :, :].rearrange("p t h c -> p (t h c)")
        g2 = dve.then(lambda e: e.tensor_scalar(gflat, gflat, 1.0, None, ALU.add), g1)
        gate_ready = dve.then(lambda e: e.reciprocal(gflat, gflat))

        sums = sb("sums", [P, HEADS2, 3])
        sumb = sb("sumb", [P, HEADS2])
        nmax = sb("nmax", [P, HEADS2 + 2, 2])
        neg_sink = sb("neg_sink", [P, HEADS2])
        ns = dve.then(lambda e: e.tensor_scalar(neg_sink[:, :], sink[:, :], -1.0, None, ALU.mult), sink_there)
        L = [acc[0], acc[1]]
        T = [acc[2], acc[3]]
        skew = lambda h0: bass.AP(tensor=bias_rows.tensor, offset=h0 * TOE, ap=[[1, P], [TOE, HEADS2], [1, SEQ]])
        bias_there = load(bias_a, skew(0), bias_written, vb_ready, hid, name="bias_a_in")
        o_tok = [slab(0), slab(1)]
        unit = 0
        e_free, et_free = [(), ()], [(), ()]
        m = dict(skip_group_check=True)

        def softmax_unit(t, q_of, k_of, v_of, b_of, sum_to, col, sinks, o_banks, o_cols, first, *after):
            nonlocal unit
            u = unit % 2
            unit += 1
            W = (t + 1) * P
            off = SEQ - W if t == 0 else 0
            lg = L[u][:, :].rearrange("p (a w) -> p a w", a=2)
            pe.wait(*acc_free[u], *after)
            for i in range(2):
                pe.quiet(lambda e, i=i, b=b_of(i): e.matmul(lg[:, i, :W], flip, b[:, P - t * P:SEQ] if t == 0 else b,
                                                            start=(i == 0), stop=False, **m))
            for i in range(2):
                q, k = q_of(i), k_of(i)
                f = (lambda e, i=i, q=q, k=k: e.matmul(lg[:, i, :W], q, k[:, :W], start=False, stop=(i == 1), **m))
                lg_done = pe.do(f) if i == 1 else pe.quiet(f)
            nm = nmax[:, u, :]
            mx = dve.then(lambda e: e.tensor_reduce(nm, lg[:, :, :W], AX.X, ALU.max, negate=True), lg_done,
                          *e_free[u])
            if sinks is not None:
                mx = dve.then(lambda e: e.tensor_tensor(nm, nm, neg_sink[:, sinks:sinks + 2], ALU.min))
                keep = nmax[:, 2 + sinks // 2, :]
                mx = dve.then(lambda e: e.tensor_copy(keep, nm))
            eb = e_buf[:, u, :].rearrange("p (a w) -> p a w", a=2)
            for i in range(2):
                ex = act.do(lambda e, i=i, total=sum_to(i): e.activation(
                    eb[:, i, :W], lg[:, i, :W], ACT.Exp, bias=nm[:, i:i + 1], accum_out=total), mx, *e_free[u])
            acc_free[u] = (ex,)
            n = 2 * (t + 1)
            pe.wait(ex, *acc_free[2 + u])
            for j in range(n):
                i, kb = divmod(j, t + 1)
                f = (lambda e, j=j, i=i, kb=kb: e.transpose(T[u][:, j * P:(j + 1) * P], eb[:, i, kb * P:(kb + 1) * P], ident))
                tr = pe.do(f) if j == n - 1 else pe.quiet(f)
            e_free[u] = (tr,)
            if unit % 2:
                cp = dve.do(lambda e: e.tensor_copy(et_buf[:, u, :n * P], T[u][:, :n * P]), tr, *et_free[u])
            else:
                cp = act.do(lambda e: e.activation(et_buf[:, u, :n * P], T[u][:, :n * P], ACT.Copy), tr, *et_free[u])
            acc_free[2 + u] = (cp,)
            pe.wait(cp)
            for j in range(n):
                i, kb = divmod(j, t + 1)
                if first and kb == 0 and (i == 0 or o_banks[0] != o_banks[1]):
                    pe.wait(*wk_free[o_banks[i]])
                f = (lambda e, j=j, i=i, kb=kb, v=v_of(i, kb): e.matmul(
                    wk[o_banks[i]][:, o_cols[i]:o_cols[i] + HD2], et_buf[:, u, j * P:(j + 1) * P], v,
                    start=(kb == 0), stop=(kb == t), **m))
                pv = pe.do(f) if j == n - 1 else pe.quiet(f)
            et_free[u] = (pv,)
            return pv

        def query(pair, head, t):
            return q2_t[:, pair + head // 2, t * P:(t + 1) * P]

        cmp_et = region(16960, 2 * P)
        cmp_et_free = twice_free[0] + twice_free[1]
        for t in range(TT):
            nc_all = HEADS2 * CMP_BLOCKS
            pe.wait(*wk_free[3], ck_ready, head_ready[10], head_ready[11])
            for h in range(HEADS2):
                f = (lambda e, h=h, t=t: e.matmul(wk[3][:, h * CMP_BLOCKS:(h + 1) * CMP_BLOCKS], query(0, h, t),
                                                  ckz[:, h // HPG2, h % 2, :CMP_BLOCKS], start=True, stop=True, **m))
                lg_done = pe.do(f) if h == HEADS2 - 1 else pe.quiet(f)
            ec = e_buf[:, 0, :nc_all].rearrange("p (h c) -> p h c", c=CMP_BLOCKS)
            lg_c = wk[3][:, :nc_all].rearrange("p (h c) -> p h c", c=CMP_BLOCKS)
            a = dve.then(lambda e, t=t: e.tensor_tensor(ec, lg_c, biascmp[:, t, :, :].rearrange("p c h -> p h c"), ALU.add),
                         lg_done, *e_free[0])
            wk_free[3] = (a,)
            mc = nmax[:, 2:2 + 8, :].rearrange("p a b -> p (a b)")
            dve.then(lambda e: e.tensor_reduce(mc, ec, AX.X, ALU.max))
            b = dve.then(lambda e: e.tensor_tensor(ec, ec, mc.unsqueeze(2).to_broadcast([P, HEADS2, CMP_BLOCKS]), ALU.subtract))
            c = act.then(lambda e: e.activation(e_buf[:, 0, :nc_all], e_buf[:, 0, :nc_all], ACT.Exp), b)
            d = dve.then(lambda e: e.tensor_reduce(sums[:, :, 0], ec, AX.X, ALU.add), c)
            cmp_o = []
            for g in range(GROUPS2):
                n = HPG2 * CMP_BLOCKS
                tr = pe.do(lambda e, g=g, n=n: e.transpose(wk[3][:n, g * P:(g + 1) * P], e_buf[:, 0, g * n:(g + 1) * n], ident),
                           c, a)
            cp = dve.then(lambda e, n=n: e.tensor_copy(cmp_et[:n, :], wk[3][:n, :2 * P]), tr, *cmp_et_free)
            wk_free[3] = (cp,)
            e_free[0] = (tr, d)
            for g in range(GROUPS2):
                pe.wait(cp, vb_ready, *wk_free[2])
                oc = pe.do(lambda e, g=g, n=n: e.matmul(wk[2][:, :], cmp_et[:n, g * P:(g + 1) * P], v_block[:n, g, :],
                                                        start=True, stop=True))
                cmp_et_free = (oc,)
                for hh in range(HPG2):
                    h = g * HPG2 + hh
                    q = query(0, h, t)
                    pv = softmax_unit(
                        t, lambda i: q, lambda i: kz[:, i, g, h % 2, :],
                        lambda i, kb: kvg[:, kb, (KV_VS, KV_VW)[i] + g * HD2:(KV_VS, KV_VW)[i] + (g + 1) * HD2],
                        lambda i: bias_a[:, h, :], lambda i: sums[:, h, 1 + i:2 + i], 0, None, (0, 1),
                        (hh * HD2, hh * HD2), hh == 0, bias_there, *k_ready)
                hs = slice(g * HPG2, (g + 1) * HPG2)
                dve.then(lambda e, hs=hs: e.reciprocal(sums[:, hs, :], sums[:, hs, :]), (act.sem, act.count), d)
                dve.then(lambda e, hs=hs, t=t: e.tensor_tensor(sums[:, hs, :], sums[:, hs, :], gate[:, t, hs, :], ALU.mult),
                         gate_ready)
                if t == 0:
                    dve.then(lambda e, hs=hs: e.tensor_scalar(sums[:, hs, 0], sums[:, hs, 0], const[:, C_ROWOK:C_ROWOK + 1],
                                                              None, ALU.mult))
                dst = o_tok[0][:, t, g * BANK:(g + 1) * BANK].rearrange("p (h d) -> p h d", d=HD2)
                tmp = o_tok[1][:, t, g * BANK:(g + 1) * BANK].rearrange("p (h d) -> p h d", d=HD2)
                for i, bank in enumerate((2, 0, 1)):
                    w = sums[:, hs, i].unsqueeze(2).to_broadcast([P, HPG2, HD2])
                    src = wk[bank][:, :].rearrange("p (h d) -> p h d", d=HD2)
                    to = dst if i == 0 else tmp
                    rd = dve.then(lambda e, to=to, src=src, w=w: e.tensor_tensor(to, src, w, ALU.mult), oc, pv,
                                  head_ready[10], head_ready[11])
                    wk_free[bank] = (rd,)
                    if i:
                        rd = dve.then(lambda e, dst=dst, tmp=tmp: e.tensor_tensor(dst, dst, tmp, ALU.add))
        bias_there = load(bias_a, skew(HEADS2), pv, name="bias_b_in")
        for t in range(TT):
            for h in range(0, HEADS2, 2):
                g = h // HPG2
                bank = 2 * (t % 2) + g
                pv = softmax_unit(
                    t, lambda i: query(8, h + i, t), lambda i: kz[:, 2, g, (h + i) % 2, :],
                    lambda i, kb: kvb[:, kb, P + g * HD2:P + (g + 1) * HD2],
                    lambda i: bias_a[:, h + i, :], lambda i: sumb[:, h + i:h + i + 1], 0, h, (bank, bank),
                    ((h % HPG2) * HD2, (h % HPG2 + 1) * HD2), h % HPG2 == 0, bias_there)
            keep = nmax[:, 2:2 + 8, :].rearrange("p a b -> p (a b)")
            ad = dve.then(lambda e: e.tensor_tensor(keep, keep, sink[:, :], ALU.add))
            ex = act.then(lambda e: e.activation(keep, keep, ACT.Exp), ad)
            dve.then(lambda e: e.tensor_tensor(sumb[:, :], sumb[:, :], keep, ALU.add), ex)
            dve.then(lambda e: e.reciprocal(sumb[:, :], sumb[:, :]))
            for g in range(GROUPS2):
                bank = 2 * (t % 2) + g
                w = sumb[:, g * HPG2:(g + 1) * HPG2].unsqueeze(2).to_broadcast([P, HPG2, HD2])
                dst = o_tok[1][:, t, g * BANK:(g + 1) * BANK].rearrange("p (h d) -> p h d", d=HD2)
                src = wk[bank][:, :].rearrange("p (h d) -> p h d", d=HD2)
                rd = dve.then(lambda e, dst=dst, src=src, w=w: e.tensor_tensor(dst, src, w, ALU.mult), pv)
                wk_free[bank] = (rd,)
            act.wait(rd)
        gain4_there = load(gain, spread(ins["ffn_norm_2"]), pv, rd, name="gain4_in")
        tokens = []
        for half in range(2):
            hi_part, lo_part = act_hi[:, half * 8:(half + 1) * 8, :], act_lo[:, half * 8:(half + 1) * 8, :]
            tokens += split_transposed(lambda t: slab(half)[:, t, :], PANEL // P, hi_part, lo_part, rd, *act_free)
        o_ready = tokens

        added = []
        for panel in range(2):
            done = gemm_panel(ins["w_out_2"][0], 0, DK, panel * PANEL, PANEL, act_hi, act_lo, o_ready)
            added += take_panel(PANEL, done, store_residual(panel))
        act_free = (done,)

        xn = region(0, TT, D)
        scores = region(4096, TT, 2 * PEER_HEADS, NKEYS)
        qp_t = region(8192, 8, SEQ)
        cand = region(8192, PEER_HEADS, TOPK * TOPK)
        best = region(10240, 2 * PEER_HEADS, TOPK)
        pos_f = region(10496, 2 * PEER_HEADS, TOPK)
        top = region(10752, PEER_HEADS, TOPK)
        slot_f = region(10880, 3, SLOTS)
        route = region(11264, TT, SLOTS)
        hidden = region(11520, TT, SLOTS)
        onehot = region(14336, SLOTS, TOPK)
        sub_t = region(16384, 2, NKEYS)
        sub_raw = region(16640, 2, NKEYS)
        normed = norm(xn, gain4_there, *added, pv, rd)
        x_ready = split_transposed(lambda t: xn[:, t, :], DK, act_hi, act_lo, *normed, *act_free)
        sub_there = load(sub_raw, ins["peer_subkeys_2"][0].rearrange("a n d -> n a d"), *normed, name="subkeys_in")
        st = transposes([sub_raw[:, 0, :], sub_raw[:, 1, :]], 0, sub_there)
        sub_ready = dve.then(lambda e: e.tensor_copy(sub_t.rearrange("p a n -> p (a n)"), wk[0][:, :2 * P]), st)
        wk_free[0] = (sub_ready,)

        score_done = {}

        def scores_post(panel, stored):
            def post():
                v = slab(panel)
                toks = []
                for t in range(TT):
                    for k0 in (0, 4):
                        bank = 2 * t + k0 // 4
                        there = transposes([v[:, t, k * P:(k + 1) * P] for k in range(k0, k0 + 4)], bank, *stored)
                        tok = act.do(lambda e, k0=k0, t=t, bank=bank: e.activation(
                            qp_t[:, k0:k0 + 4, t * P:(t + 1) * P], wk[bank][:, :].rearrange("p (k q) -> p k q", k=4),
                            ACT.Copy), there, *score_done.values())
                        wk_free[bank] = (tok,)
                for t in range(TT):
                    for k0 in (0, 4):
                        bank = 2 * t + k0 // 4
                        pe.wait(tok, sub_ready, *wk_free[bank])
                        for i in range(4):
                            f = (lambda e, i=i, k0=k0, t=t, bank=bank: e.matmul(
                                wk[bank][:, i * P:(i + 1) * P], qp_t[:, k0 + i, t * P:(t + 1) * P], sub_t[:, (k0 + i) % 2, :],
                                start=True, stop=True, **m))
                            sc = pe.do(f) if i == 3 else pe.quiet(f)
                        r0 = panel * 8 + k0
                        tk = act.do(lambda e, r0=r0, t=t, bank=bank: e.activation(
                            scores[:, t, r0:r0 + 4, :], wk[bank][:, :].rearrange("p (k q) -> p k q", k=4), ACT.Copy), sc)
                        wk_free[bank] = (tk,)
                        score_done[(panel, t, k0)] = tk
            return post

        for panel in range(2):
            done = gemm_panel(ins["peer_wq_2"][0], 0, DK, panel * PANEL, PANEL, act_hi, act_lo, x_ready)
            stored = take_panel(PANEL, done, store_copy(slab(panel)), *x_ready)
            state["post"] = scores_post(panel, stored)
        flush()

        small = sb("small", [P, PEER_HEADS])
        iota = cst(C_IOTA, TOPK)

        def top16(row, values, where):
            for r in range(2):
                v8 = values[:, r * 8:r * 8 + 8]
                dve.then(lambda e, v8=v8: e.max(v8, row))
                dve.then(lambda e, v8=v8, r=r: e.max_index(where[:, r * 8:r * 8 + 8], v8, row))
                if r == 0:
                    dve.then(lambda e, v8=v8: e.match_replace(row, v8, row, LOWEST))

        def routing(t):
            dve.wait(*score_done.values())
            for r in range(2 * PEER_HEADS):
                top16(scores[:, t, r, :], best[:, r, :], top_pos[:, r, :])
            pair = best[:, :, :].rearrange("p (h a) i -> p h a i", a=2)
            cand4 = cand.rearrange("p h (i j) -> p h i j", j=TOPK)
            dve.then(lambda e: e.tensor_tensor(
                cand4, pair[:, :, 0, :].unsqueeze(3).to_broadcast([P, PEER_HEADS, TOPK, TOPK]),
                pair[:, :, 1, :].unsqueeze(2).to_broadcast([P, PEER_HEADS, TOPK, TOPK]), ALU.add))
            cpos = cand_pos[:, 0, :].rearrange("p (h s) -> p h s", s=TOPK)
            for h in range(PEER_HEADS):
                top16(cand[:, h, :], top[:, h, :], cpos[:, h, :])
            dve.then(lambda e: e.tensor_copy(pos_f[:, :, :], top_pos[:, :, :]))
            posp = pos_f[:, :, :].rearrange("p (h a) i -> p h a i", a=2)
            for a, (op, k) in enumerate(((ALU.logical_shift_right, 4), (ALU.bitwise_and, TOPK - 1))):
                dve.then(lambda e, op=op, k=k: e.tensor_scalar(cand_pos[:, 1, :], cand_pos[:, 0, :], k, None, op))
                dve.then(lambda e, a=a: e.tensor_copy(slot_f[:, a, :], cand_pos[:, 1, :]))
                dve.then(lambda e, a=a: e.tensor_tensor(
                    onehot, slot_f[:, a, :].unsqueeze(2).to_broadcast([P, SLOTS, TOPK]),
                    iota.unsqueeze(1).to_broadcast([P, SLOTS, TOPK]), ALU.is_equal))
                oh4 = onehot.rearrange("p (h s) i -> p h s i", s=TOPK)
                dve.then(lambda e, a=a, oh4=oh4: e.tensor_tensor(
                    oh4, oh4, posp[:, :, a, :].unsqueeze(2).to_broadcast([P, PEER_HEADS, TOPK, TOPK]), ALU.mult))
                dve.then(lambda e, a=a: e.tensor_reduce(slot_f[:, a, :], onehot, AX.X, ALU.add))
            dve.then(lambda e: e.scalar_tensor_tensor(slot_f[:, 2, :], slot_f[:, 0, :], float(NKEYS), slot_f[:, 1, :],
                                                      ALU.mult, ALU.add))
            chosen = dve.then(lambda e, t=t: e.tensor_copy(expert[:, t, :], slot_f[:, 2, :]))
            wt = route[:, t, :].rearrange("p (h s) -> p h s", s=TOPK)
            b = dve.then(lambda e: e.tensor_tensor(
                wt, top[:, :, :], top[:, :, 0:1].to_broadcast([P, PEER_HEADS, TOPK]), ALU.subtract))
            c = act.then(lambda e, t=t: e.activation(route[:, t, :], route[:, t, :], ACT.Exp), b)
            dve.then(lambda e: e.tensor_reduce(small[:, :], wt, AX.X, ALU.add), c)
            dve.then(lambda e: e.reciprocal(small[:, :], small[:, :]))
            dve.then(lambda e: e.tensor_tensor(wt, wt, small[:, :].unsqueeze(2).to_broadcast([P, PEER_HEADS, TOPK]), ALU.mult))
            return chosen

        SLOT_ROWS = RING // 2
        rows = ring[:, :, :].rearrange("p (s two) n -> p s (two n)", two=2)
        row_sem = [sem(f"rows{i}") for i in range(SLOT_ROWS)]
        gathered = {"n": 0}
        row_free = [tuple(ring_free[2 * i]) + tuple(ring_free[2 * i + 1]) for i in range(SLOT_ROWS)]

        def gather(tab, t, j, *after):
            n = gathered["n"]
            gathered["n"] += 1
            s = n % SLOT_ROWS
            pool.wait(*after, *row_free[s])
            pool.steps.append(lambda e: e.indirect_dma_start(
                rows[:, s, :], None, tab, bass.IndirectOffsetOnAxis(ap=expert[:, t, j:j + 1], axis=0))
                .then_inc(row_sem[s], 16))
            return s, (row_sem[s], 16 * (n // SLOT_ROWS + 1))

        u_tab, v_tab = ins["peer_u_2"][0], ins["peer_v_2"][0]
        chosen = [routing(t) for t in range(TT)]
        for t in range(TT):
            for j in range(SLOTS):
                s, there = gather(u_tab, t, j, chosen[t])
                dot = dve.do(lambda e, s=s, t=t, j=j: e.tensor_tensor_reduce(
                    out=rows[:, s, :], in0=rows[:, s, :], in1=xn[:, t, :], scale=1.0, scalar=0.0, op0=ALU.mult,
                    op1=ALU.add, accum_out=hidden[:, t, j:j + 1]), there)
                row_free[s] = (dot,)
            ge = act.then(lambda e, t=t: e.activation(hidden[:, t, :], hidden[:, t, :], ACT.Gelu_apprx_tanh), dot)
            dve.then(lambda e, t=t: e.tensor_tensor(route[:, t, :], route[:, t, :], hidden[:, t, :], ALU.mult), ge)
        gain5_there = load(gain, spread(ins["final_norm_2"]), chosen[-1], sub_ready, *score_done.values(), name="gain5_in")
        for t in range(TT):
            for j in range(SLOTS):
                s, there = gather(v_tab, t, j, chosen[t])
                last = dve.then(lambda e, s=s, t=t, j=j: e.scalar_tensor_tensor(
                    resid[:, t, :], rows[:, s, :], route[:, t, j:j + 1], resid[:, t, :], ALU.mult, ALU.add), there)
                row_free[s] = (last,)

        final = norm(wide, gain5_there, last)
        stored_out = sem("stored_out")
        sp.wait(*final)
        sp.steps.append(lambda e: e.dma_start(out.rearrange("b (t p) d -> p (b t) d", p=P), wide).then_inc(stored_out, 16))
        sp.wait((stored_out, 16))
        sp.wait(bias_written)

        block = ctx.enter_context(nc.Block())
        block.tensor(pe.run)
        block.scalar(act.run)
        block.vector(dve.run)
        block.gpsimd(pool.run)
        block.sync(sp.run)


NAMES = ["x", "norm_mix_g", "norm_mlp_g", "sb_w_qkv", "sb_q_norm_g", "sb_k_norm_g", "sb_w_o", "mlp_w_in", "mlp_w_out",
         "attn_norm_2", "w_in_2", "cmp_pos_k_2", "cmp_w1_k_2", "cmp_w2_k_2", "cmp_pos_v_2", "cmp_w1_v_2", "cmp_w2_v_2",
         "sinks_2", "w_out_2", "ffn_norm_2", "peer_wq_2", "peer_subkeys_2", "peer_u_2", "peer_v_2", "rel_bias_2",
         "final_norm_2"]


def kernel(**inputs):
    import numpy as _np
    import concourse.bacc as _bacc
    from concourse import mybir as _mybir
    from concourse.bass_utils import run_bass_kernel_spmd as _run

    nc = _bacc.Bacc("TRN2", target_bir_lowering=False, num_devices=1)
    arrays, ins = {}, {}
    given = {name: inputs[name] for name in NAMES}
    given["const"] = constants()
    given["onehot"] = onehots()
    for name, a in given.items():
        a = _np.ascontiguousarray(a)
        arrays[f"in_{name}_dram"] = a
        ins[name] = nc.dram_tensor(f"in_{name}_dram", a.shape, _mybir.dt.from_np(a.dtype), kind="ExternalInput").ap()
    out = nc.dram_tensor("out_dram", (1, SEQ, D), F32, kind="ExternalOutput").ap()
    build(nc, ins, out)
    r = _run(nc, [arrays], core_ids=[0])
    return r.results[0]["out_dram"]
```

```python
from contextlib import ExitStack

import concourse.bass as bass
import numpy as np
from concourse import mybir

F32 = mybir.dt.float32
F32R = mybir.dt.float32r
U32 = mybir.dt.uint32
ACT = mybir.ActivationFunctionType
ALU = mybir.AluOpType
AX = mybir.AxisListType

P = 128
SEQ = 256
TT = SEQ // P
D = 2048
DK = D // P
EPS = 1e-6
NEG = -1e30
PANEL = 1024
BANK = 512

HEADS1 = 16
HEADS2 = 16
HD2 = 64
GROUPS2 = 2
HPG2 = HEADS2 // GROUPS2
MLP = 4 * D
CMP_BLOCKS = 15
CMP_STRIDE = 16
CMP_LEN = 32
SWA_WINDOW = 128
PEER_HEADS = 8
NKEYS = 128
TOPK = 16
SLOTS = PEER_HEADS * TOPK
LOWEST = -3.0e38

W2_QA, W2_KV, W2_QB, W2_KVB = 0, 1024, 1840, 2864
KV_KC, KV_VC, KV_KS, KV_VS, KV_KW, KV_VW, KV_GATE = 0, 128, 256, 384, 512, 640, 768

TOE = 384
C_IDENT, C_FLIP, C_STICK, C_TRI, C_ONES, C_IOTA, C_BLOCK = 0, 128, 256, 384, 512, 640, 656
C_ROWOK, C_END = 664, 665
C_OHA, C_OHB, C_OHC = 0, TOE, 2 * TOE
OHC_BASE = 256
OH_END = C_OHC + 512


def rel_bucket(dist):
    d = np.maximum(dist, 0)
    large = 16 + (np.log(np.maximum(d, 1).astype(np.float32) / np.float32(16)) / np.float32(np.log(128.0))
                  * np.float32(16)).astype(np.int32)
    return np.where(d < 16, d, np.minimum(large, 31))


def constants():
    c = np.zeros((P, C_END), np.float32)
    r = np.arange(P)
    c[:, C_IDENT:C_IDENT + P] = np.eye(P)
    c[:, C_FLIP:C_FLIP + P] = np.eye(P)[::-1]
    c[:, C_STICK:C_STICK + P] = np.where(r[:, None] < r[None, :], 0.0, NEG)
    c[:, C_TRI:C_TRI + P] = -1.0 * (r[:, None] >= r[None, :])
    c[:, C_ONES:C_ONES + P] = -1.0
    c[:, C_IOTA:C_IOTA + TOPK] = np.arange(TOPK)
    for h in range(HPG2):
        c[h * CMP_BLOCKS:(h + 1) * CMP_BLOCKS, C_BLOCK + h] = 1.0
    c[:, C_ROWOK] = r >= CMP_LEN - 1
    return c


def onehots():
    c = np.zeros((33, OH_END), np.float32)
    dist = 255 - np.arange(TOE)
    for col, bad in ((C_OHA, dist < 0), (C_OHB, (dist < 0) | (dist >= SWA_WINDOW))):
        c[np.where(bad, 32, rel_bucket(dist)), col + np.arange(TOE)] = 1.0
    dist = np.arange(512) - OHC_BASE
    c[np.where(dist < 0, 32, rel_bucket(dist)), C_OHC + np.arange(512)] = 1.0
    return c


class Line:

    def __init__(self, sem=None):
        self.sem, self.count, self.steps, self.met = sem, 0, [], {}

    def wait(self, *tokens):
        for sem, value in tokens:
            if self.met.get(sem, 0) < value:
                self.met[sem] = value
                self.steps.append(lambda e, s=sem, v=value: e.wait_ge(s, v))

    def do(self, make, *after):
        self.wait(*after)
        self.count += 1
        self.steps.append(lambda e, s=self.sem: make(e).then_inc(s, 1))
        return (self.sem, self.count)

    def then(self, make, *after):
        if self.count:
            self.wait((self.sem, self.count))
        return self.do(make, *after)

    def quiet(self, make, *after):
        self.wait(*after)
        self.steps.append(lambda e: make(e))

    def run(self, e):
        for step in self.steps:
            step(e)


def build(nc, ins, out):
    with ExitStack() as ctx:
        def sb(name, shape, dt=F32):
            return ctx.enter_context(nc.sbuf_tensor(name, shape, dt))

        def sem(name):
            return ctx.enter_context(nc.semaphore(name))

        act_hi = sb("act_hi", [P, DK, SEQ], F32R)
        act_lo = sb("act_lo", [P, DK, SEQ], F32R)
        hid_hi = sb("hid_hi", [P, PANEL // P, SEQ], F32R)
        hid_lo = sb("hid_lo", [P, PANEL // P, SEQ], F32R)
        NSPLIT = 2
        w_hi = sb("w_hi", [P, NSPLIT, PANEL], F32R)
        w_lo = sb("w_lo", [P, NSPLIT, PANEL], F32R)
        RING = 8
        ring = sb("ring", [P, RING, PANEL])
        resid = sb("resid", [P, TT, D])
        panels = sb("panels", [P, 2, TT, PANEL])
        WORK = 17408
        work = sb("work", [P, WORK])
        stat = sb("stat", [P, 448])
        table = sb("table", [33, 32])
        biascmp = sb("biascmp", [P, TT, CMP_BLOCKS, HEADS2])
        qk_gain = sb("qk_gain", [P, 2, P])
        sink = sb("sink", [P, HEADS2])
        const = sb("const", [P, C_END])
        top_pos = sb("top_pos", [P, 2 * PEER_HEADS, TOPK], U32)
        cand_pos = sb("cand_pos", [P, 2, SLOTS], U32)
        expert = sb("expert", [P, TT, SLOTS], U32)
        acc = [ctx.enter_context(nc.psum_tensor(f"acc{i}", [P, BANK], F32)) for i in range(4)]
        wk = [ctx.enter_context(nc.psum_tensor(f"wk{i}", [P, BANK], F32)) for i in range(4)]
        bias_rows = nc.dram_tensor("bias_rows", [2 * HEADS2, TOE], F32, kind="Internal").ap()

        def region(at, *shape):
            n = int(np.prod(shape))
            v = work[:, at:at + n]
            if len(shape) == 1:
                return v
            names = "abcd"[:len(shape)]
            return v.rearrange(f"p ({' '.join(names)}) -> p {' '.join(names)}", **dict(zip(names, shape)))

        def cst(at, n=P):
            return const[:, at:at + n]

        ident, flip = cst(C_IDENT), cst(C_FLIP)
        gain = region(15360, D)

        pe, act, dve, pool, sp = (Line(sem("pe")), Line(sem("act")), Line(sem("dve")), Line(sem("pool")), Line())
        landing = [sem(f"chunk{i}") for i in range(RING)]
        landed = [0] * RING

        def load(dst, src, *after, name):
            s = sem(name)
            sp.wait(*after)
            sp.steps.append(lambda e: e.dma_start(dst, src).then_inc(s, 16))
            return (s, 16)

        acc_free = [()] * 4
        wk_free = [()] * 4
        ring_free = [()] * RING
        split_free = [()] * NSPLIT
        state = {"chunk": 0, "issued": 0, "posts": [], "side": None, "side_steps": 0}

        plan = []

        def plan_panels(w, row0, nk, *panels_):
            for col0, width in panels_:
                plan.extend((w, row0 + k * P, col0, width) for k in range(nk))

        both = [(0, PANEL), (PANEL, PANEL)]
        NH = MLP // PANEL
        plan_panels(ins["sb_w_qkv"][0], 0, DK, *[(i * PANEL, PANEL) for i in range(6)])
        plan_panels(ins["sb_w_o"][0], 0, DK, *both)
        for j in range(NH + 1):
            if j < NH:
                plan_panels(ins["mlp_w_in"][0], 0, DK, (j * PANEL, PANEL))
            if j > 0:
                plan_panels(ins["mlp_w_out"][0], (j - 1) * PANEL, PANEL // P, *both)
        plan_panels(ins["w_in_2"][0], 0, DK, (W2_QA, PANEL), (W2_KV, 816), (W2_QB, PANEL), (W2_KVB, 256))
        plan_panels(ins["w_out_2"][0], 0, DK, *both)
        plan_panels(ins["peer_wq_2"][0], 0, DK, *both)
        split_done = {}

        def issue(upto):
            while state["issued"] <= min(upto, len(plan) - 1):
                c = state["issued"]
                state["issued"] += 1
                w, row, col0, width = plan[c]
                s, b = c % RING, c % NSPLIT
                sp.wait(*ring_free[s])
                src, dst = w[row:row + P, col0:col0 + width], ring[:, s, :width]
                sp.steps.append(lambda e, d=dst, r=src, m=landing[s]: e.dma_start(d, r).then_inc(m, 16))
                landed[s] += 16
                there = (landing[s], landed[s])
                high = act.do(lambda e, s=s, b=b, width=width: e.activation(
                    w_hi[:, b, :width], ring[:, s, :width], ACT.Copy),
                    there, *split_free[b])
                low = dve.do(lambda e, s=s, b=b, width=width: e.tensor_tensor(
                    w_lo[:, b, :width], ring[:, s, :width], w_hi[:, b, :width].bitcast(F32), ALU.subtract),
                    high, there, *split_free[b])
                ring_free[s] = (low,)
                split_done[c] = (high, low)

        def gemm_panel(w, row0, nk, col0, width, hi, lo, after_x):
            cuts = [(n, min(BANK, width - n)) for n in range(0, width, BANK)]
            for k in range(nk):
                c = state["chunk"]
                state["chunk"] += 1
                assert plan[c][1:] == (row0 + k * P, col0, width) and plan[c][0].tensor.name == w.tensor.name
                b = c % NSPLIT
                issue(c + 1)
                high, low = split_done[c]
                pe.wait(*after_x, high)
                for t in range(TT):
                    xs = [x[:, k, t * P:(t + 1) * P] for x in (hi, lo)]
                    for i, (x, wp) in enumerate(((xs[0], w_hi), (xs[0], w_lo), (xs[1], w_hi))):
                        if i == 1:
                            pe.wait(low)
                        for j, (n, m) in enumerate(cuts):
                            if k == 0 and i == 0:
                                pe.wait(*acc_free[2 * t + j])
                            mm = (lambda e, x=x, wp=wp, j=j, t=t, n=n, m=m, i=i, k=k, b=b: e.matmul(
                                acc[2 * t + j][:, :m], x, wp[:, b, n:n + m],
                                start=(k == 0 and i == 0), stop=(k == nk - 1 and i == 2)))
                            if (t, i, j) == (TT - 1, 2, len(cuts) - 1):
                                done = pe.do(mm)
                            else:
                                pe.quiet(mm)
                split_free[b] = (done,)
                while state["posts"] and k >= state["posts"][0][0]:
                    state["posts"].pop(0)[1]()
                if k > 2 and state["side"]:
                    side(state["side_steps"])
            return done

        def side(n):
            for _ in range(n):
                if state["side"] and next(state["side"], "end") == "end":
                    state["side"] = None

        def flush():
            while state["posts"]:
                state["posts"].pop(0)[1]()

        def take_panel(width, done, store, *after):
            tokens = []
            for t in range(TT):
                for j, n in enumerate(range(0, width, BANK)):
                    bank = 2 * t + j
                    tok = store(t, n, min(BANK, width - n), acc[bank], done, *after)
                    acc_free[bank] = (tok,)
                    tokens.append(tok)
            return tokens

        def store_copy(dst):
            def store(t, n, m, bank, *after):
                if n == 0:
                    return act.do(lambda e: e.activation(dst[:, t, n:n + m], bank[:, :m], ACT.Copy), *after)
                return dve.do(lambda e: e.tensor_copy(dst[:, t, n:n + m], bank[:, :m]), *after)
            return store

        def transposes(srcs, bank, *after):
            pe.wait(*after, *wk_free[bank])
            for i, src in enumerate(srcs):
                f = (lambda e, i=i, src=src: e.transpose(wk[bank][:, i * P:(i + 1) * P], src, ident))
                if i == len(srcs) - 1:
                    return pe.do(f)
                pe.quiet(f)

        def split_transposed(src, nk, hi, lo, *after, square=None, tile_ready=None):
            tokens = []
            for t in range(TT):
                for k0 in range(0, nk, 4):
                    bank = (t * nk + k0) // 4 % 4
                    there = transposes([src(t)[:, k * P:(k + 1) * P] for k in range(k0, k0 + 4)], bank,
                                       *after, *(tile_ready[t:t + 1] if tile_ready else ()))
                    grid = wk[bank][:, :].rearrange("p (k q) -> p k q", k=4)
                    to = lambda x, k0=k0, t=t: x[:, k0:k0 + 4, t * P:(t + 1) * P]
                    if square is None:
                        h = act.do(lambda e, to=to, grid=grid: e.activation(to(hi), grid, ACT.Copy), there)
                        l = dve.do(lambda e, to=to, grid=grid: e.tensor_tensor(
                            to(lo), grid, to(hi).bitcast(F32), ALU.subtract), h)
                        wk_free[bank] = (l,)
                    else:
                        b = square[:, bank % 2, :].rearrange("p (k q) -> p k q", k=4)
                        sq = act.do(lambda e, b=b, grid=grid: e.activation(b, grid, ACT.Square),
                                    there, *tokens[-2:-1])
                        wk_free[bank] = (sq,)
                        h = act.then(lambda e, to=to, b=b: e.activation(to(hi), b, ACT.Copy))
                        l = dve.do(lambda e, to=to, b=b: e.tensor_tensor(
                            to(lo), b, to(hi).bitcast(F32), ALU.subtract), h)
                    tokens.append(l)
            return tokens[-1:] + [h]

        ss, rs = stat[:, 0:2], stat[:, 2:4]

        def inv_rms(total, width, dst, *after):
            a = dve.then(lambda e: e.tensor_scalar(dst, total, 1.0 / width, EPS, ALU.mult, ALU.add), *after)
            b = act.then(lambda e: e.activation(dst, dst, ACT.Sqrt), a)
            return dve.then(lambda e: e.reciprocal(dst, dst), b)

        def norm(dst, gain_there, *after):
            for t in range(TT):
                sq = act.then(lambda e, t=t: e.activation(dst[:, t, :], resid[:, t, :], ACT.Square,
                                                          accum_out=ss[:, t:t + 1]), *after)
            r = inv_rms(ss, D, rs, sq)
            return [dve.then(lambda e, t=t: e.scalar_tensor_tensor(dst[:, t, :], resid[:, t, :], rs[:, t:t + 1], gain,
                                                                   ALU.mult, ALU.mult), gain_there)
                    for t in range(TT)]

        def spread(row, n=D):
            return bass.AP(tensor=row.tensor, offset=0, ap=[[0, P], [1, n]])

        wide = panels[:, :, :, :].rearrange("p b t n -> p (b t n)").rearrange("p (t n) -> p t n", t=TT)
        slab = lambda b: panels[:, b, :, :]

        x_there = load(resid[:, :, :], ins["x"].rearrange("b (t p) d -> p (b t) d", p=P), name="x_in")
        gain1_there = load(gain, spread(ins["norm_mix_g"]), name="gain1_in")
        const_there = load(const[:, :], ins["const"], name="const_in")
        qg_there = load(qk_gain[:, 0, :], spread(ins["sb_q_norm_g"], P), name="qgain_in")
        kg_there = load(qk_gain[:, 1, :], spread(ins["sb_k_norm_g"], P), name="kgain_in")
        sink_there = load(sink[:, :], spread(ins["sinks_2"], HEADS2), name="sink_in")
        onehot_b = work[:33, 2048:2048 + OH_END]
        onehot_there = load(onehot_b, ins["onehot"], name="onehot_in")
        neg_row = dve.do(lambda e: e.memset(table[:, :], NEG))
        table_there = load(table[0:32, :], ins["rel_bias_2"], neg_row, name="table_in")

        normed = norm(wide, gain1_there, x_there)
        x_ready = split_transposed(lambda t: wide[:, t, :], DK, act_hi, act_lo, const_there, tile_ready=normed)

        bias_sb = work[:HEADS2, 0:2 * TOE].rearrange("p (a n) -> p a n", a=2)
        for half, oh in ((0, C_OHA), (1, C_OHB)):
            rows = pe.do(lambda e, half=half, oh=oh: e.matmul(
                wk[half][:HEADS2, :TOE], table[:, half * 16:half * 16 + 16], onehot_b[:, oh:oh + TOE],
                start=True, stop=True), table_there, onehot_there, *wk_free[half])
            taken = dve.do(lambda e, half=half: e.tensor_copy(bias_sb[:, half, :], wk[half][:HEADS2, :TOE]), rows)
            wk_free[half] = (taken,)
        bias_out = sem("bias_out")
        sp.wait(taken)
        sp.steps.append(lambda e: e.dma_start(bias_rows.rearrange("(a h) n -> h a n", a=2), bias_sb)
                        .then_inc(bias_out, 16))
        bias_written = (bias_out, 16)

        for t in range(TT):
            pe.wait(*wk_free[2 + t])
            for c in range(CMP_BLOCKS):
                col = C_OHC + OHC_BASE + t * P - CMP_STRIDE * c - (CMP_LEN - 1)
                f = (lambda e, t=t, c=c, col=col: e.matmul(
                    wk[2 + t][:, c * HEADS2:(c + 1) * HEADS2], onehot_b[:, col:col + P], table[:, 0:HEADS2],
                    start=True, stop=True))
                rows = pe.do(f) if c == CMP_BLOCKS - 1 else pe.quiet(f)
            taken = dve.do(lambda e, t=t: e.tensor_copy(
                biascmp[:, t, :, :].rearrange("p c h -> p (c h)"), wk[2 + t][:, :CMP_BLOCKS * HEADS2]), rows)
            wk_free[2 + t] = (taken,)

        q_t, k_t = region(0, HEADS1, SEQ), region(4096, HEADS1, SEQ)
        v_tok = region(8192, TT, D)
        w_qkv = ins["sb_w_qkv"][0]
        scale1 = float(P) ** -0.5
        sum8, inv8 = stat[:, 8:24].rearrange("p (t h) -> p t h", t=TT), stat[:, 24:40].rearrange("p (t h) -> p t h", t=TT)
        head_ready = {}
        slab_free = [(), ()]

        def heads_post(panel, stored, dst, which, scale):
            v = slab(panel % 2)
            last = []

            def normalize():
                heads = v.rearrange("p t (h d) -> p t h d", d=P)
                for t in range(TT):
                    sq = act.then(lambda e, t=t: e.activation(work[:, 12288:13312], v[:, t, :], ACT.Square), *stored)
                    sm = dve.then(lambda e, t=t: e.tensor_reduce(sum8[:, t, :], work[:, 12288:13312].rearrange(
                        "p (h d) -> p h d", d=P), AX.X, ALU.add), sq)
                    act.wait(sm)
                inv_rms(sum8.rearrange("p t h -> p (t h)"), P, inv8.rearrange("p t h -> p (t h)"), sm)
                for t in range(TT):
                    dve.then(lambda e, t=t: e.tensor_tensor(
                        heads[:, t], heads[:, t], inv8[:, t, :].unsqueeze(2).to_broadcast([P, 8, P]), ALU.mult))
                    n = dve.then(lambda e, t=t: e.scalar_tensor_tensor(
                        heads[:, t], heads[:, t], scale, qk_gain[:, which, :].unsqueeze(1).to_broadcast([P, 8, P]),
                        ALU.mult, ALU.mult), qg_there, kg_there)
                    last.append(n)

            def turn():
                for t in range(TT):
                    for k0 in (0, 4):
                        bank = 2 * t + k0 // 4
                        there = transposes([v[:, t, k * P:(k + 1) * P] for k in range(k0, k0 + 4)], bank, last[t])
                        h0 = (panel % 2) * 8 + k0
                        tok = act.do(lambda e, h0=h0, t=t, bank=bank: e.activation(
                            dst[:, h0:h0 + 4, t * P:(t + 1) * P], wk[bank][:, :].rearrange("p (k q) -> p k q", k=4),
                            ACT.Copy), there, bias_written)
                        wk_free[bank] = (tok,)
                slab_free[panel % 2] = (tok,)
                head_ready[panel] = tok
            return [(1, normalize), (8, turn)]

        for panel in range(4):
            done = gemm_panel(w_qkv, 0, DK, panel * PANEL, PANEL, act_hi, act_lo, x_ready)
            stored = take_panel(PANEL, done, store_copy(slab(panel % 2)), *slab_free[panel % 2], *normed)
            state["posts"] = heads_post(panel, stored, q_t if panel < 2 else k_t, panel // 2,
                                        scale1 if panel < 2 else 1.0)
        v_stored = []
        for panel in range(2):
            done = gemm_panel(w_qkv, 0, DK, 2 * D + panel * PANEL, PANEL, act_hi, act_lo, x_ready)
            v_stored += take_panel(PANEL, done, store_copy(v_tok[:, :, panel * PANEL:(panel + 1) * PANEL]), bias_written)
        act_free = (done,)

        GH = 2
        COLS = SEQ + P
        z_a = region(12288, 2, GH, COLS)
        z_b = region(13824, 2, GH, COLS)
        za_free, zb_free = [(), ()], [(), ()]
        stick, tri, ones = cst(C_STICK), cst(C_TRI), cst(C_ONES)
        m = dict(skip_group_check=True)

        def stick_scores(g):
            u, z_done, mag = g % 2, [], []
            for i in range(GH):
                h, z = g * GH + i, acc[GH * u + i]
                pe.wait(*acc_free[GH * u + i], head_ready[0], head_ready[1], head_ready[2], head_ready[3])
                pe.quiet(lambda e, z=z, h=h: e.matmul(z[:, :SEQ], k_t[:, h, :P], q_t[:, h, :], start=True, stop=False, **m))
                pe.quiet(lambda e, z=z, h=h: e.matmul(z[:, SEQ:COLS], k_t[:, h, P:], q_t[:, h, P:], start=False, stop=False, **m))
                pe.quiet(lambda e, z=z: e.matmul(z[:, :P], ident, stick, start=False, stop=False, **m))
                z_done.append(pe.do(lambda e, z=z: e.matmul(z[:, SEQ:COLS], ident, stick, start=False, stop=True, **m)))
            for i in range(GH):
                mag.append(act.do(lambda e, i=i: e.activation(z_a[:, u, i, :], acc[GH * u + i][:, :COLS], ACT.Abs),
                                  z_done[i], *za_free[u]))
            ex = act.do(lambda e: e.activation(z_a[:, u], z_a[:, u], ACT.Exp, scale=-1.0), *mag)
            ln = act.then(lambda e: e.activation(z_a[:, u], z_a[:, u], ACT.Ln, bias=1.0), ex)
            return [dve.do(lambda e, i=i: e.scalar_tensor_tensor(z_b[:, u, i, :], acc[GH * u + i][:, :COLS], 0.0,
                                                                 z_a[:, u, i, :], ALU.max, ALU.add), ln, *zb_free[u])
                    for i in range(GH)]

        def stick_weights(g, sp_done):
            u, a_done = g % 2, []
            for i in range(GH):
                z = acc[GH * u + i]
                pe.wait(sp_done[i])
                pe.quiet(lambda e, z=z, i=i: e.matmul(z[:, :SEQ], tri, z_b[:, u, i, :SEQ], start=False, stop=False, **m))
                pe.quiet(lambda e, z=z, i=i: e.matmul(z[:, P:SEQ], ones, z_b[:, u, i, SEQ:], start=False, stop=False, **m))
                s_done = pe.do(lambda e, z=z, i=i: e.matmul(z[:, SEQ:COLS], tri, z_b[:, u, i, SEQ:], start=False,
                                                            stop=True, **m))
                tok = act.do(lambda e, i=i: e.activation(z_a[:, u, i, :], acc[GH * u + i][:, :COLS], ACT.Exp),
                             s_done, sp_done[i])
                acc_free[GH * u + i] = (tok,)
                a_done.append(tok)
            zb_free[u] = (s_done,)
            return a_done

        def stick_values(g, a_done):
            u, bank = g % 2, g % 4
            o = wk[bank]
            pe.wait(*a_done, *v_stored, *wk_free[bank])
            for j in range(GH):
                h, c = g * GH + j, j * SEQ
                v0, v1 = (v_tok[:, t, h * P:(h + 1) * P] for t in range(TT))
                pe.quiet(lambda e, c=c, v0=v0, j=j: e.matmul(o[:, c:c + SEQ], v0, z_a[:, u, j, :SEQ],
                                                             start=True, stop=False, **m))
                o_done = pe.do(lambda e, c=c, v1=v1, j=j: e.matmul(o[:, c + P:c + SEQ], v1, z_a[:, u, j, SEQ:],
                                                                   start=False, stop=True, **m))
            za_free[u] = (o_done,)
            h0, grid = g * GH, o[:, :].rearrange("p (k q) -> p k q", k=2)
            hi = act.do(lambda e: e.activation(act_hi[:, h0:h0 + 2, :], grid, ACT.Copy), o_done, *act_free)
            lo = dve.do(lambda e: e.tensor_tensor(act_lo[:, h0:h0 + 2, :], grid, act_hi[:, h0:h0 + 2, :].bitcast(F32),
                                                  ALU.subtract), hi)
            wk_free[bank] = (lo,)
            return hi, lo

        act.quiet(lambda e: e.preload_act_table_set("natural_log_exp_and_others"))
        scored, weighed = {}, {}
        for g in range(HEADS1 // GH + 2):
            if g >= 2:
                hi, lo = stick_values(g - 2, weighed[g - 2])
            if g < HEADS1 // GH:
                scored[g] = stick_scores(g)
            if 1 <= g <= HEADS1 // GH:
                weighed[g - 1] = stick_weights(g - 1, scored[g - 1])
        o_ready = [hi, lo]

        def store_residual(panel):
            def store(t, n, m, bank, *after):
                at = resid[:, t, panel * PANEL + n:panel * PANEL + n + m]
                return dve.do(lambda e: e.tensor_tensor(at, bank[:, :m], at, ALU.add), *after)
            return store

        gain2_there = load(gain, spread(ins["norm_mlp_g"]), *normed, name="gain2_in")
        added = []
        for panel in range(2):
            done = gemm_panel(ins["sb_w_o"][0], 0, DK, panel * PANEL, PANEL, act_hi, act_lo, o_ready)
            added += take_panel(PANEL, done, store_residual(panel))
        act_free = (done,)

        normed = norm(wide, gain2_there, *added, *slab_free[0], *slab_free[1])
        x_ready = split_transposed(lambda t: wide[:, t, :], DK, act_hi, act_lo, *act_free, tile_ready=normed)
        square = region(0, 2, BANK)
        slab_free = [tuple(x_ready), tuple(x_ready)]
        hid_state = {"free": ()}
        added = []

        def store_relu(dst):
            def store(t, n, m, bank, *after):
                if n == 0:
                    return act.do(lambda e: e.activation(dst[:, t, n:n + m], bank[:, :m], ACT.Relu), *after)
                return dve.do(lambda e: e.tensor_scalar(dst[:, t, n:n + m], bank[:, :m], 0.0, None, ALU.max), *after)
            return store

        def hidden_out(j, hid_ready):
            for panel in range(2):
                done = gemm_panel(ins["mlp_w_out"][0], j * PANEL, PANEL // P, panel * PANEL, PANEL, hid_hi, hid_lo,
                                  hid_ready)
                added[:] = added[-4:] + take_panel(PANEL, done, store_residual(panel))
            hid_state["free"] = (done,)

        for j in range(NH):
            done = gemm_panel(ins["mlp_w_in"][0], 0, DK, j * PANEL, PANEL, act_hi, act_lo, x_ready)
            stored = take_panel(PANEL, done, store_relu(slab(j % 2)), *slab_free[j % 2])
            if j > 0:
                hidden_out(j - 1, hid_ready)
            v = slab(j % 2)
            hid_ready = split_transposed(lambda t: v[:, t, :], PANEL // P, hid_hi, hid_lo, *stored, *hid_state["free"],
                                         square=square)
            slab_free[j % 2] = tuple(hid_ready)
        act_free = (done,)
        hidden_out(NH - 1, hid_ready)

        gain3_there = load(gain, spread(ins["attn_norm_2"]), *normed, name="gain3_in")
        normed = norm(wide, gain3_there, *added, *slab_free[0], *slab_free[1])
        x_ready = split_transposed(lambda t: wide[:, t, :], DK, act_hi, act_lo, *act_free, tile_ready=normed)

        q2_t = region(0, HEADS2, SEQ)
        kz = region(4096, 3, GROUPS2, 2, SEQ)
        kvg = region(7168, TT, 816)
        kvb = region(8800, TT, 256)
        ckv_t = region(9312, 2, GROUPS2, SEQ)
        v_block = region(9312, GROUPS2, BANK)
        flat = region(10336, DK, GROUPS2 * CMP_BLOCKS)
        w1 = region(10816, 2, DK, P)
        bias_a = region(10816, HEADS2, SEQ)
        e_buf = region(14912, 2, BANK)
        et_buf = region(15936, 2, BANK)
        twice = region(16960, 2, P)
        ckz = region(17216, GROUPS2, 2, CMP_BLOCKS + 1)
        cmp_hid = region(17280, 2 * CMP_BLOCKS)
        pos_t = stat[:, 64:64 + 2 * DK].rearrange("p (a k) -> p a k", a=2)

        clear = dve.then(lambda e: e.memset(region(4096, 3072), 0.0), *x_ready, *acc_free[0])
        clear2 = dve.then(lambda e: e.memset(region(17216, 64), 0.0), *normed)
        w1_there = [load(w1[:, i, :, :], ins[n][0].rearrange("(k p) h -> p k h", p=P), *x_ready, name=n + "_in")
                    for i, n in enumerate(("cmp_w1_k_2", "cmp_w1_v_2"))]
        pos_there = [load(stat[i * DK:(i + 1) * DK, 100:228], ins[n][0].rearrange("(k l) d -> k (l d)", l=2),
                          name=n + "_in") for i, n in enumerate(("cmp_pos_k_2", "cmp_pos_v_2"))]
        w2_there = [load(stat[:, 228 + 64 * i:292 + 64 * i], ins[n][0], name=n + "_in")
                    for i, n in enumerate(("cmp_w2_k_2", "cmp_w2_v_2"))]
        w2 = stat[:, 228:356].rearrange("p (a d) -> p a d", a=2)

        w_in2 = ins["w_in_2"][0]

        def pairs_post(panel, stored, first):
            def post():
                v = slab(panel)
                for t in range(TT):
                    for k0 in (0, 4):
                        bank = 2 * t + k0 // 4
                        there = transposes([v[:, t, k * P:(k + 1) * P] for k in range(k0, k0 + 4)], bank, *stored)
                        tok = act.do(lambda e, k0=k0, t=t, bank=bank: e.activation(
                            q2_t[:, first + k0:first + k0 + 4, t * P:(t + 1) * P],
                            wk[bank][:, :].rearrange("p (k q) -> p k q", k=4), ACT.Copy, scale=HD2 ** -0.5), there)
                        wk_free[bank] = (tok,)
                head_ready[10 + panel] = tok
            return [(1, post)]

        twice_free = [(), ()]

        def doubled(src, col, g, t, bank, n, *after):
            tw = twice[:, n % 2, :].rearrange("p (a d) -> p a d", a=2)
            cp = dve.then(lambda e: e.tensor_copy(tw, src[:, t, col + g * HD2:col + (g + 1) * HD2].unsqueeze(1)
                                                  .to_broadcast([P, 2, HD2])), *after, *twice_free[n % 2])
            there = transposes([twice[:, n % 2, :]], bank, cp)
            twice_free[n % 2] = (there,)
            return there

        def keys_to(src, col, which, *after):
            for g in range(GROUPS2):
                for t in range(TT):
                    bank = (2 * g + t) % 4
                    there = doubled(src, col, g, t, bank, t, *after)
                    for half in range(2):
                        rows = slice(half * HD2, (half + 1) * HD2)
                        tok = dve.then(lambda e, g=g, t=t, half=half, rows=rows, bank=bank: e.tensor_copy(
                            kz[rows, which, g, half, t * P:(t + 1) * P], wk[bank][rows, :P]), there, clear)
                    wk_free[bank] = (tok,)
            return tok

        done = gemm_panel(w_in2, 0, DK, W2_QA, PANEL, act_hi, act_lo, x_ready)
        stored = take_panel(PANEL, done, store_copy(slab(0)), *x_ready)
        state["posts"] = pairs_post(0, stored, 0)
        done = gemm_panel(w_in2, 0, DK, W2_KV, 816, act_hi, act_lo, x_ready)
        kv_stored = take_panel(816, done, store_copy(kvg), *x_ready)
        done = gemm_panel(w_in2, 0, DK, W2_QB, PANEL, act_hi, act_lo, x_ready)
        stored = take_panel(PANEL, done, store_copy(slab(1)), *x_ready)
        state["posts"] = pairs_post(1, stored, 8)
        done = gemm_panel(w_in2, 0, DK, W2_KVB, 256, act_hi, act_lo, x_ready)
        kvb_stored = take_panel(256, done, store_copy(kvb), *x_ready)
        act_free = (done,)

        k_ready = [keys_to(kvg, KV_KS, 0, *kv_stored), keys_to(kvg, KV_KW, 1), keys_to(kvb, 0, 2, *kvb_stored)]

        pos_turned = pe.do(lambda e: e.transpose(wk[0][:, :2 * DK], stat[:2 * DK, 100:228], ident[:2 * DK, :2 * DK]),
                           *pos_there, *wk_free[0])
        pos_ready = dve.then(lambda e: e.tensor_copy(pos_t.rearrange("p a k -> p (a k)"), wk[0][:, :2 * DK]), pos_turned)
        wk_free[0] = (pos_ready,)
        for which, col in ((0, KV_KC), (1, KV_VC)):
            for g in range(GROUPS2):
                for t in range(TT):
                    bank = (2 * g + t) % 4
                    there = doubled(kvg, col, g, t, bank, t)
                    tok = dve.then(lambda e, w=which, g=g, t=t, bank=bank: e.tensor_copy(
                        ckv_t[:, w, g, t * P:(t + 1) * P], wk[bank][:, :P]), there)
                    wk_free[bank] = (tok,)
        cmp_done = ()
        for which in range(2):
            for g in range(GROUPS2):
                for l in range(2):
                    rows = slice(l * HD2, (l + 1) * HD2)
                    src = ckv_t[rows, which, g, l:l + 1]
                    view = bass.AP(tensor=src.tensor, offset=src.offset, ap=[list(src.ap[0]), [2, DK], [CMP_STRIDE, CMP_BLOCKS]])
                    flat_ready = dve.then(lambda e, g=g, rows=rows, view=view, w=which: e.tensor_tensor(
                        flat[rows, :, g * CMP_BLOCKS:(g + 1) * CMP_BLOCKS], view,
                        pos_t[rows, w, :].unsqueeze(2).to_broadcast([HD2, DK, CMP_BLOCKS]), ALU.add), *cmp_done)
            pe.wait(flat_ready, w1_there[which], *wk_free[0])
            for k in range(DK):
                f = (lambda e, k=k, w=which: e.matmul(wk[0][:, :2 * CMP_BLOCKS], w1[:, w, k, :], flat[:, k, :],
                                                      start=(k == 0), stop=(k == DK - 1)))
                hid = pe.do(f) if k == DK - 1 else pe.quiet(f)
            gel = act.then(lambda e: e.activation(cmp_hid, wk[0][:, :2 * CMP_BLOCKS], ACT.Gelu_apprx_tanh), hid, clear2)
            wk_free[0] = (gel,)
            if which == 0:
                tw = twice[:, 0, :].rearrange("p (a d) -> p a d", a=2)
                cp = dve.then(lambda e: e.tensor_copy(tw, w2[:, 0, :].unsqueeze(1).to_broadcast([P, 2, HD2])),
                              w2_there[0], *twice_free[0])
                ck = pe.do(lambda e: e.matmul(wk[1][:, :2 * CMP_BLOCKS], twice[:, 0, :], cmp_hid, start=True, stop=True),
                           cp, gel, *wk_free[1])
                twice_free[0] = (ck,)
                for half in range(2):
                    rows = slice(half * HD2, (half + 1) * HD2)
                    ck_ready = dve.then(lambda e, rows=rows, half=half: e.tensor_copy(
                        ckz[rows, :, half, :CMP_BLOCKS],
                        wk[1][rows, :2 * CMP_BLOCKS].rearrange("p (g c) -> p g c", g=2)), ck)
                wk_free[1] = (ck_ready,)
                cmp_done = (ck,)
            else:
                for g in range(GROUPS2):
                    rep = e_buf[:, g, :HPG2 * CMP_BLOCKS].rearrange("p (h c) -> p h c", h=HPG2)
                    cp = dve.then(lambda e, g=g, rep=rep: e.tensor_copy(
                        rep, cmp_hid[:, g * CMP_BLOCKS:(g + 1) * CMP_BLOCKS].unsqueeze(1)
                        .to_broadcast([P, HPG2, CMP_BLOCKS])), gel)
                    cv = pe.do(lambda e, g=g: e.matmul(wk[2 + g][:HPG2 * CMP_BLOCKS, :HD2],
                                                       e_buf[:, g, :HPG2 * CMP_BLOCKS], w2[:, 1, :], start=True, stop=True),
                               cp, w2_there[1], *wk_free[2 + g])
                    n = HPG2 * CMP_BLOCKS
                    vb_ready = dve.then(lambda e, g=g, n=n: e.tensor_tensor(
                        v_block[:n, g, :].rearrange("p (h d) -> p h d", h=HPG2),
                        wk[2 + g][:n, :HD2].unsqueeze(1).to_broadcast([n, HPG2, HD2]),
                        const[:n, C_BLOCK:C_BLOCK + HPG2].unsqueeze(2).to_broadcast([n, HPG2, HD2]), ALU.mult), cv)
                    wk_free[2 + g] = (vb_ready,)
        flush()

        gate = sb("gate", [P, TT, HEADS2, 3])
        g1 = act.then(lambda e: e.activation(gate[:, :, :, :].rearrange("p t h c -> p t (h c)"),
                                             kvg[:, :, KV_GATE:KV_GATE + 48], ACT.Exp, scale=-1.0), *kv_stored)
        gflat = gate[:, :, :, :].rearrange("p t h c -> p (t h c)")
        g2 = dve.then(lambda e: e.tensor_scalar(gflat, gflat, 1.0, None, ALU.add), g1)
        gate_ready = dve.then(lambda e: e.reciprocal(gflat, gflat))

        sums = sb("sums", [P, TT, HEADS2, 3])
        sumb = sb("sumb", [P, HEADS2])
        nmax = sb("nmax", [P, HEADS2 + 2, 2])
        neg_sink = sb("neg_sink", [P, HEADS2])
        ns = dve.then(lambda e: e.tensor_scalar(neg_sink[:, :], sink[:, :], -1.0, None, ALU.mult), sink_there)
        L = [acc[0], acc[1]]
        T = [acc[2], acc[3]]
        skew = lambda h0: bass.AP(tensor=bias_rows.tensor, offset=h0 * TOE, ap=[[1, P], [TOE, HPG2], [1, SEQ]])
        bias_state = {"n": 0}
        bias_ready = {}

        def bias_tiles(half, g, *after):
            n = bias_state["n"]
            bias_state["n"] += 1
            part = bias_a[:, g * HPG2:(g + 1) * HPG2, :]
            there = load(part, skew(half * HEADS2 + g * HPG2), bias_written, *after, name=f"bias{n}_in")
            for h in range(0, HPG2, 2):
                two = part[:, h:h + 2, :].rearrange("p h k -> p (h k)")
                turned = pe.do(lambda e, two=two: e.matmul(wk[3][:, :], flip, two, start=True, stop=True),
                               there, *wk_free[3])
                tok = act.do(lambda e, two=two: e.activation(two, wk[3][:, :], ACT.Copy), turned)
                wk_free[3] = (tok,)
            bias_ready[(half, g)] = tok
        o_tok = [slab(0), slab(1)]
        unit = 0
        e_free, et_free = [(), ()], [(), ()]
        m = dict(skip_group_check=True)

        def softmax_unit(t, q_of, k_of, v_of, b_of, sum_to, sinks, o_banks, o_cols, first, *after):
            nonlocal unit
            u = unit % 2
            unit += 1
            W = (t + 1) * P
            n = 2 * (t + 1)
            lg = L[u][:, :].rearrange("p (a w) -> p a w", a=2)
            eb = e_buf[:, u, :].rearrange("p (a w) -> p a w", a=2)
            nm = nmax[:, u, :]
            qs, ks, bs, totals = [q_of(0), q_of(1)], [k_of(0), k_of(1)], [b_of(0), b_of(1)], [sum_to(0), sum_to(1)]
            vs = [[v_of(i, kb) for kb in range(t + 1)] for i in range(2)]
            tokens = {}

            def logits():
                pe.wait(*acc_free[u], *after)
                for i in range(2):
                    f = (lambda e, i=i: e.matmul(lg[:, i, :W], qs[i], ks[i][:, :W], start=True, stop=True, **m))
                    lg_done = pe.do(f) if i == 1 else pe.quiet(f)
                for i in range(2):
                    mx = dve.do(lambda e, i=i: e.tensor_tensor_reduce(
                        out=eb[:, i, :W], in0=lg[:, i, :W], in1=bs[i][:, SEQ - W:SEQ], scale=1.0, scalar=-3.4e38,
                        op0=ALU.add, op1=ALU.max, accum_out=nm[:, i:i + 1]), lg_done, *e_free[u], *after)
                acc_free[u] = (mx,)
                if sinks is None:
                    mx = dve.then(lambda e: e.tensor_scalar(nm, nm, -1.0, None, ALU.mult))
                else:
                    keep = nmax[:, 2 + sinks // 2, :]
                    mx = dve.then(lambda e: e.scalar_tensor_tensor(nm, nm, -1.0, neg_sink[:, sinks:sinks + 2],
                                                                   ALU.mult, ALU.min))
                    mk = dve.then(lambda e: e.tensor_copy(keep, nm))
                for i in range(2):
                    ex = act.do(lambda e, i=i: e.activation(eb[:, i, :W], eb[:, i, :W], ACT.Exp, bias=nm[:, i:i + 1],
                                                            accum_out=totals[i]), mx)
                tokens["ex"] = ex

            def turn():
                pe.wait(tokens["ex"], *acc_free[2 + u])
                for j in range(n):
                    i, kb = divmod(j, t + 1)
                    f = (lambda e, j=j, i=i, kb=kb: e.transpose(T[u][:, j * P:(j + 1) * P],
                                                                eb[:, i, kb * P:(kb + 1) * P], ident))
                    tr = pe.do(f) if j == n - 1 else pe.quiet(f)
                e_free[u] = (tr, tokens["ex"])
                cp = act.do(lambda e: e.activation(et_buf[:, u, :n * P], T[u][:, :n * P], ACT.Copy), tr, *et_free[u])
                acc_free[2 + u] = (cp,)
                tokens["cp"] = cp

            def values():
                pe.wait(tokens["cp"])
                for j in range(n):
                    i, kb = divmod(j, t + 1)
                    if first and kb == 0 and (i == 0 or o_banks[0] != o_banks[1]):
                        pe.wait(*wk_free[o_banks[i]])
                    f = (lambda e, j=j, i=i, kb=kb: e.matmul(
                        wk[o_banks[i]][:, o_cols[i]:o_cols[i] + HD2], et_buf[:, u, j * P:(j + 1) * P], vs[i][kb],
                        start=(kb == 0), stop=(kb == t), **m))
                    pv = pe.do(f) if j == n - 1 else pe.quiet(f)
                et_free[u] = (pv,)
                tokens["pv"] = pv

            return logits, turn, values, tokens

        flying = []

        def push(stages):
            flying.append(stages)
            if len(flying) >= 3:
                flying.pop(0)[2]()
            stages[0]()
            if len(flying) >= 2:
                flying[-2][1]()

        def drain():
            while len(flying) > 1:
                flying.pop(0)[2]()
            last_unit = flying.pop(0)
            last_unit[1]()
            last_unit[2]()
            return last_unit[3]["pv"]

        def query(pair, head, t):
            return q2_t[:, pair + head // 2, t * P:(t + 1) * P]

        cmp_et_free = twice_free[0] + twice_free[1]
        nc_all = HEADS2 * CMP_BLOCKS
        n = HPG2 * CMP_BLOCKS
        cmp_et = [region(16960, 2 * P), region(10336, 2 * P)]
        cmp_done = {}
        bias_tiles(0, 0, vb_ready, hid)
        for t in range(TT):
            pe.wait(*wk_free[2], ck_ready, head_ready[10], head_ready[11])
            for h in range(HEADS2):
                f = (lambda e, h=h, t=t: e.matmul(wk[2][:, h * CMP_BLOCKS:(h + 1) * CMP_BLOCKS], query(0, h, t),
                                                  ckz[:, h // HPG2, h % 2, :CMP_BLOCKS], start=True, stop=True, **m))
                lg_done = pe.do(f) if h == HEADS2 - 1 else pe.quiet(f)
            ec = e_buf[:, t, :nc_all].rearrange("p (h c) -> p h c", c=CMP_BLOCKS)
            lg_c = wk[2][:, :nc_all].rearrange("p (h c) -> p h c", c=CMP_BLOCKS)
            a = dve.then(lambda e, t=t, ec=ec, lg_c=lg_c: e.tensor_tensor(
                ec, lg_c, biascmp[:, t, :, :].rearrange("p c h -> p h c"), ALU.add), lg_done)
            wk_free[2] = (a,)
            mc = nmax[:, 2:2 + 8, :].rearrange("p a b -> p (a b)")
            dve.then(lambda e, ec=ec: e.tensor_reduce(mc, ec, AX.X, ALU.max))
            b = dve.then(lambda e, ec=ec: e.tensor_tensor(
                ec, ec, mc.unsqueeze(2).to_broadcast([P, HEADS2, CMP_BLOCKS]), ALU.subtract))
            c = act.then(lambda e, t=t: e.activation(e_buf[:, t, :nc_all], e_buf[:, t, :nc_all], ACT.Exp), b)
            d = dve.then(lambda e, t=t, ec=ec: e.tensor_reduce(sums[:, t, :, 0], ec, AX.X, ALU.add), c)
            pe.wait(a)
            for g in range(GROUPS2):
                tr = pe.do(lambda e, g=g, t=t: e.transpose(wk[2][:n, g * P:(g + 1) * P], e_buf[:, t, g * n:(g + 1) * n],
                                                           ident), c)
            cp = dve.then(lambda e, t=t: e.tensor_copy(cmp_et[t][:n, :], wk[2][:n, :2 * P]), tr, *cmp_et_free)
            wk_free[2] = (cp,)
            e_free[t] = (tr, d)
            cmp_done[t] = (cp, d)
        bias_tiles(0, 1, vb_ready, hid)
        for g in range(GROUPS2):
            for t in range(TT):
                pe.wait(*cmp_done[t], vb_ready, *wk_free[2])
                oc = pe.do(lambda e, g=g, t=t: e.matmul(wk[2][:, :], cmp_et[t][:n, g * P:(g + 1) * P], v_block[:n, g, :],
                                                        start=True, stop=True))
                for hh in range(HPG2):
                    h = g * HPG2 + hh
                    q = query(0, h, t)
                    push(softmax_unit(
                        t, lambda i: q, lambda i: kz[:, i, g, h % 2, :],
                        lambda i, kb: kvg[:, kb, (KV_VS, KV_VW)[i] + g * HD2:(KV_VS, KV_VW)[i] + (g + 1) * HD2],
                        lambda i: bias_a[:, h, :], lambda i: sums[:, t, h, 1 + i:2 + i], None, (0, 1),
                        (hh * HD2, hh * HD2), hh == 0, bias_ready[(0, g)], *k_ready))
                pv = drain()
                hs = slice(g * HPG2, (g + 1) * HPG2)
                part = sums[:, t, hs, :]
                dve.then(lambda e, part=part: e.reciprocal(part, part), (act.sem, act.count), *cmp_done[t])
                dve.then(lambda e, hs=hs, t=t, part=part: e.tensor_tensor(part, part, gate[:, t, hs, :], ALU.mult),
                         gate_ready)
                if t == 0:
                    dve.then(lambda e, part=part: e.tensor_scalar(part[:, :, 0], part[:, :, 0],
                                                                  const[:, C_ROWOK:C_ROWOK + 1], None, ALU.mult))
                dst = o_tok[0][:, t, g * BANK:(g + 1) * BANK].rearrange("p (h d) -> p h d", d=HD2)
                tmp = o_tok[1][:, t, g * BANK:(g + 1) * BANK].rearrange("p (h d) -> p h d", d=HD2)
                for i, bank in enumerate((2, 0, 1)):
                    w = part[:, :, i].unsqueeze(2).to_broadcast([P, HPG2, HD2])
                    src = wk[bank][:, :].rearrange("p (h d) -> p h d", d=HD2)
                    to = dst if i == 0 else tmp
                    rd = dve.then(lambda e, to=to, src=src, w=w: e.tensor_tensor(to, src, w, ALU.mult), oc, pv,
                                  head_ready[10], head_ready[11])
                    wk_free[bank] = (rd,)
                    if i:
                        rd = dve.then(lambda e, dst=dst, tmp=tmp: e.tensor_tensor(dst, dst, tmp, ALU.add))
            bias_tiles(1, g, pv, (dve.sem, dve.count))
        for t in range(TT):
            for h in range(0, HEADS2, 2):
                g = h // HPG2
                bank = g
                push(softmax_unit(
                    t, lambda i: query(8, h + i, t), lambda i: kz[:, 2, g, (h + i) % 2, :],
                    lambda i, kb: kvb[:, kb, P + g * HD2:P + (g + 1) * HD2],
                    lambda i: bias_a[:, h + i, :], lambda i: sumb[:, h + i:h + i + 1], h, (bank, bank),
                    ((h % HPG2) * HD2, (h % HPG2 + 1) * HD2), h % HPG2 == 0, bias_ready[(1, g)]))
            pv = drain()
            keep = nmax[:, 2:2 + 8, :].rearrange("p a b -> p (a b)")
            ad = dve.then(lambda e, keep=keep: e.tensor_tensor(keep, keep, sink[:, :], ALU.add))
            ex = act.then(lambda e, keep=keep: e.activation(keep, keep, ACT.Exp), ad)
            dve.then(lambda e, keep=keep: e.tensor_tensor(sumb[:, :], sumb[:, :], keep, ALU.add), ex)
            dve.then(lambda e: e.reciprocal(sumb[:, :], sumb[:, :]))
            for g in range(GROUPS2):
                w = sumb[:, g * HPG2:(g + 1) * HPG2].unsqueeze(2).to_broadcast([P, HPG2, HD2])
                dst = o_tok[1][:, t, g * BANK:(g + 1) * BANK].rearrange("p (h d) -> p h d", d=HD2)
                src = wk[g][:, :].rearrange("p (h d) -> p h d", d=HD2)
                rd = dve.then(lambda e, dst=dst, src=src, w=w: e.tensor_tensor(dst, src, w, ALU.mult), pv)
                wk_free[g] = (rd,)
            act.wait(rd)
        gain4_there = load(gain, spread(ins["ffn_norm_2"]), pv, rd, name="gain4_in")
        tokens = []
        for half in range(2):
            hi_part, lo_part = act_hi[:, half * 8:(half + 1) * 8, :], act_lo[:, half * 8:(half + 1) * 8, :]
            tokens += split_transposed(lambda t: slab(half)[:, t, :], PANEL // P, hi_part, lo_part, rd, *act_free)
        o_ready = tokens

        added = []
        for panel in range(2):
            done = gemm_panel(ins["w_out_2"][0], 0, DK, panel * PANEL, PANEL, act_hi, act_lo, o_ready)
            added += take_panel(PANEL, done, store_residual(panel))
        act_free = (done,)

        xn = region(0, TT, D)
        scores = region(4096, TT, 2 * PEER_HEADS, NKEYS)
        qp_t = region(8192, 8, SEQ)
        route = region(11264, TT, SLOTS)
        hidden = region(11520, TT, SLOTS)
        sub_t = region(16384, 2, NKEYS)
        sub_raw = region(16640, 2, NKEYS)
        normed = norm(xn, gain4_there, *added, pv, rd)
        x_ready = split_transposed(lambda t: xn[:, t, :], DK, act_hi, act_lo, *act_free, tile_ready=normed)
        sub_there = load(sub_raw, ins["peer_subkeys_2"][0].rearrange("a n d -> n a d"), *normed, name="subkeys_in")
        st = transposes([sub_raw[:, 0, :], sub_raw[:, 1, :]], 0, sub_there)
        sub_ready = dve.then(lambda e: e.tensor_copy(sub_t.rearrange("p a n -> p (a n)"), wk[0][:, :2 * P]), st)
        wk_free[0] = (sub_ready,)

        score_done = {}

        def scores_post(panel, stored):
            v = slab(panel)
            turned = []

            def turn():
                for t in range(TT):
                    for k0 in (0, 4):
                        bank = 2 * t + k0 // 4
                        there = transposes([v[:, t, k * P:(k + 1) * P] for k in range(k0, k0 + 4)], bank, *stored)
                        tok = act.do(lambda e, k0=k0, t=t, bank=bank: e.activation(
                            qp_t[:, k0:k0 + 4, t * P:(t + 1) * P], wk[bank][:, :].rearrange("p (k q) -> p k q", k=4),
                            ACT.Copy), there, *score_done.values())
                        wk_free[bank] = (tok,)
                turned.append(tok)

            def score():
                for t in range(TT):
                    for k0 in (0, 4):
                        bank = 2 * t + k0 // 4
                        pe.wait(*turned, sub_ready, *wk_free[bank])
                        for i in range(4):
                            f = (lambda e, i=i, k0=k0, t=t, bank=bank: e.matmul(
                                wk[bank][:, i * P:(i + 1) * P], qp_t[:, k0 + i, t * P:(t + 1) * P], sub_t[:, (k0 + i) % 2, :],
                                start=True, stop=True, **m))
                            sc = pe.do(f) if i == 3 else pe.quiet(f)
                        r0 = panel * 8 + k0
                        tk = act.do(lambda e, r0=r0, t=t, bank=bank: e.activation(
                            scores[:, t, r0:r0 + 4, :], wk[bank][:, :].rearrange("p (k q) -> p k q", k=4), ACT.Copy), sc)
                        wk_free[bank] = (tk,)
                        score_done[(panel, t, k0)] = tk
            return [(1, turn), (2, score)]

        HALF = PEER_HEADS // 2
        HS = HALF * TOPK
        cand = region(12288, HALF, TOPK * TOPK)
        best = region(10240, 2 * HALF, TOPK)
        pos_f = region(10496, 2 * HALF, TOPK)
        top = region(10752, HALF, TOPK)
        slot_f = region(10880, 3, HS)
        onehot = region(13312, HS, TOPK)
        small = sb("small", [P, HALF])
        iota = cst(C_IOTA, TOPK)
        chosen = {}

        def top16(row, values, where):
            for r in range(2):
                v8 = values[:, r * 8:r * 8 + 8]
                dve.then(lambda e, v8=v8: e.max(v8, row))
                yield
                dve.then(lambda e, v8=v8, r=r: e.max_index(where[:, r * 8:r * 8 + 8], v8, row))
                yield
                if r == 0:
                    dve.then(lambda e, v8=v8: e.match_replace(row, v8, row, LOWEST))
                    yield

        def route_half(t, half):
            dve.wait(*[score_done[(half, t, k0)] for k0 in (0, 4)])
            for r in range(2 * HALF):
                yield from top16(scores[:, t, half * 2 * HALF + r, :], best[:, r, :], top_pos[:, r, :])
            pair = best[:, :, :].rearrange("p (h a) i -> p h a i", a=2)
            cand4 = cand.rearrange("p h (i j) -> p h i j", j=TOPK)
            dve.then(lambda e: e.tensor_tensor(
                cand4, pair[:, :, 0, :].unsqueeze(3).to_broadcast([P, HALF, TOPK, TOPK]),
                pair[:, :, 1, :].unsqueeze(2).to_broadcast([P, HALF, TOPK, TOPK]), ALU.add))
            yield
            where = cand_pos[:, 0, :HS]
            for h in range(HALF):
                yield from top16(cand[:, h, :], top[:, h, :], where[:, h * TOPK:(h + 1) * TOPK])
            dve.then(lambda e: e.tensor_copy(pos_f[:, :, :], top_pos[:, :2 * HALF, :]))
            posp = pos_f[:, :, :].rearrange("p (h a) i -> p h a i", a=2)
            oh4 = onehot.rearrange("p (h s) i -> p h s i", s=TOPK)
            for a, (op, k) in enumerate(((ALU.logical_shift_right, 4), (ALU.bitwise_and, TOPK - 1))):
                dve.then(lambda e, op=op, k=k: e.tensor_scalar(cand_pos[:, 1, :HS], where, k, None, op))
                dve.then(lambda e, a=a: e.tensor_copy(slot_f[:, a, :], cand_pos[:, 1, :HS]))
                yield
                dve.then(lambda e, a=a: e.tensor_tensor(
                    onehot, slot_f[:, a, :].unsqueeze(2).to_broadcast([P, HS, TOPK]),
                    iota.unsqueeze(1).to_broadcast([P, HS, TOPK]), ALU.is_equal))
                yield
                dve.then(lambda e, a=a: e.tensor_tensor(
                    oh4, oh4, posp[:, :, a, :].unsqueeze(2).to_broadcast([P, HALF, TOPK, TOPK]), ALU.mult))
                yield
                dve.then(lambda e, a=a: e.tensor_reduce(slot_f[:, a, :], onehot, AX.X, ALU.add))
                yield
            dve.then(lambda e: e.scalar_tensor_tensor(slot_f[:, 2, :], slot_f[:, 0, :], float(NKEYS), slot_f[:, 1, :],
                                                      ALU.mult, ALU.add))
            chosen[(t, half)] = dve.then(lambda e: e.tensor_copy(expert[:, t, half * HS:(half + 1) * HS],
                                                                 slot_f[:, 2, :]))
            yield
            share = route[:, t, half * HS:(half + 1) * HS]
            wt = share.rearrange("p (h s) -> p h s", s=TOPK)
            b = dve.then(lambda e: e.tensor_tensor(
                wt, top[:, :, :], top[:, :, 0:1].to_broadcast([P, HALF, TOPK]), ALU.subtract))
            c = act.then(lambda e: e.activation(share, share, ACT.Exp), b)
            yield
            dve.then(lambda e: e.tensor_reduce(small[:, :], wt, AX.X, ALU.add), c)
            dve.then(lambda e: e.reciprocal(small[:, :], small[:, :]))
            dve.then(lambda e: e.tensor_tensor(wt, wt, small[:, :].unsqueeze(2).to_broadcast([P, HALF, TOPK]), ALU.mult))
            yield

        def routing():
            for half in range(2):
                for t in range(TT):
                    yield from route_half(t, half)

        for panel in range(2):
            if panel == 1:
                state["side"], state["side_steps"] = routing(), 7
            done = gemm_panel(ins["peer_wq_2"][0], 0, DK, panel * PANEL, PANEL, act_hi, act_lo, x_ready)
            stored = take_panel(PANEL, done, store_copy(slab(panel)), *x_ready)
            state["posts"] = scores_post(panel, stored)
        flush()

        SLOT_ROWS = RING // 2
        rows = ring[:, :, :].rearrange("p (s two) n -> p s (two n)", two=2)
        row_sem = [sem(f"rows{i}") for i in range(SLOT_ROWS)]
        gathered = {"n": 0}
        row_free = [tuple(ring_free[2 * i]) + tuple(ring_free[2 * i + 1]) for i in range(SLOT_ROWS)]

        def gather(tab, t, j, *after):
            n = gathered["n"]
            gathered["n"] += 1
            s = n % SLOT_ROWS
            pool.wait(*after, *row_free[s])
            pool.steps.append(lambda e: e.indirect_dma_start(
                rows[:, s, :], None, tab, bass.IndirectOffsetOnAxis(ap=expert[:, t, j:j + 1], axis=0))
                .then_inc(row_sem[s], 16))
            return s, (row_sem[s], 16 * (n // SLOT_ROWS + 1))

        u_tab, v_tab = ins["peer_u_2"][0], ins["peer_v_2"][0]
        for t in range(TT):
            for j in range(SLOTS):
                while (t, j // HS) not in chosen:
                    side(1)
                s, there = gather(u_tab, t, j, chosen[(t, j // HS)])
                dot = dve.do(lambda e, s=s, t=t, j=j: e.tensor_tensor_reduce(
                    out=rows[:, s, :], in0=rows[:, s, :], in1=xn[:, t, :], scale=1.0, scalar=0.0, op0=ALU.mult,
                    op1=ALU.add, accum_out=hidden[:, t, j:j + 1]), there)
                row_free[s] = (dot,)
                side(2)
            while t == TT - 1 and state["side"]:
                side(1)
            ge = act.then(lambda e, t=t: e.activation(hidden[:, t, :], hidden[:, t, :], ACT.Gelu_apprx_tanh), dot)
            dve.then(lambda e, t=t: e.tensor_tensor(route[:, t, :], route[:, t, :], hidden[:, t, :], ALU.mult), ge)
        gain5_there = load(gain, spread(ins["final_norm_2"]), sub_ready, *score_done.values(), name="gain5_in")
        for t in range(TT):
            for j in range(SLOTS):
                s, there = gather(v_tab, t, j)
                last = dve.then(lambda e, s=s, t=t, j=j: e.scalar_tensor_tensor(
                    resid[:, t, :], rows[:, s, :], route[:, t, j:j + 1], resid[:, t, :], ALU.mult, ALU.add), there)
                row_free[s] = (last,)

        final = norm(wide, gain5_there, last)
        stored_out = sem("stored_out")
        sp.wait(*final)
        sp.steps.append(lambda e: e.dma_start(out.rearrange("b (t p) d -> p (b t) d", p=P), wide).then_inc(stored_out, 16))
        sp.wait((stored_out, 16))
        sp.wait(bias_written)

        block = ctx.enter_context(nc.Block())
        block.tensor(pe.run)
        block.scalar(act.run)
        block.vector(dve.run)
        block.gpsimd(pool.run)
        block.sync(sp.run)


NAMES = ["x", "norm_mix_g", "norm_mlp_g", "sb_w_qkv", "sb_q_norm_g", "sb_k_norm_g", "sb_w_o", "mlp_w_in", "mlp_w_out",
         "attn_norm_2", "w_in_2", "cmp_pos_k_2", "cmp_w1_k_2", "cmp_w2_k_2", "cmp_pos_v_2", "cmp_w1_v_2", "cmp_w2_v_2",
         "sinks_2", "w_out_2", "ffn_norm_2", "peer_wq_2", "peer_subkeys_2", "peer_u_2", "peer_v_2", "rel_bias_2",
         "final_norm_2"]


def kernel(**inputs):
    import numpy as _np
    import concourse.bacc as _bacc
    from concourse import mybir as _mybir
    from concourse.bass_utils import run_bass_kernel_spmd as _run

    nc = _bacc.Bacc("TRN2", target_bir_lowering=False, num_devices=1)
    arrays, ins = {}, {}
    given = {name: inputs[name] for name in NAMES}
    given["const"] = constants()
    given["onehot"] = onehots()
    for name, a in given.items():
        a = _np.ascontiguousarray(a)
        arrays[f"in_{name}_dram"] = a
        ins[name] = nc.dram_tensor(f"in_{name}_dram", a.shape, _mybir.dt.from_np(a.dtype), kind="ExternalInput").ap()
    out = nc.dram_tensor("out_dram", (1, SEQ, D), F32, kind="ExternalOutput").ap()
    build(nc, ins, out)
    r = _run(nc, [arrays], core_ids=[0])
    return r.results[0]["out_dram"]
```

```python
from contextlib import ExitStack

import concourse.bass as bass
import numpy as np
from concourse import mybir

F32 = mybir.dt.float32
F32R = mybir.dt.float32r
U32 = mybir.dt.uint32
ACT = mybir.ActivationFunctionType
ALU = mybir.AluOpType
AX = mybir.AxisListType

P = 128
SEQ = 256
TT = SEQ // P
D = 2048
DK = D // P
EPS = 1e-6
NEG = -1e30
PANEL = 1024
BANK = 512

HEADS1 = 16
HEADS2 = 16
HD2 = 64
GROUPS2 = 2
HPG2 = HEADS2 // GROUPS2
MLP = 4 * D
CMP_BLOCKS = 15
CMP_STRIDE = 16
CMP_LEN = 32
SWA_WINDOW = 128
PEER_HEADS = 8
NKEYS = 128
TOPK = 16
SLOTS = PEER_HEADS * TOPK
LOWEST = -3.0e38

W2_QA, W2_KV, W2_QB, W2_KVB = 0, 1024, 1840, 2864
KV_KC, KV_VC, KV_KS, KV_VS, KV_KW, KV_VW, KV_GATE = 0, 128, 256, 384, 512, 640, 768

TOE = 384
C_IDENT, C_FLIP, C_STICK, C_TRI, C_ONES, C_IOTA, C_BLOCK = 0, 128, 256, 384, 512, 640, 656
C_ROWOK, C_END = 664, 665
C_OHA, C_OHB, C_OHC = 0, TOE, 2 * TOE
OHC_BASE = 256
OH_END = C_OHC + 512


def rel_bucket(dist):
    d = np.maximum(dist, 0)
    large = 16 + (np.log(np.maximum(d, 1).astype(np.float32) / np.float32(16)) / np.float32(np.log(128.0))
                  * np.float32(16)).astype(np.int32)
    return np.where(d < 16, d, np.minimum(large, 31))


def constants():
    c = np.zeros((P, C_END), np.float32)
    r = np.arange(P)
    c[:, C_IDENT:C_IDENT + P] = np.eye(P)
    c[:, C_FLIP:C_FLIP + P] = np.eye(P)[::-1]
    c[:, C_STICK:C_STICK + P] = np.where(r[:, None] < r[None, :], 0.0, NEG)
    c[:, C_TRI:C_TRI + P] = -1.0 * (r[:, None] >= r[None, :])
    c[:, C_ONES:C_ONES + P] = -1.0
    c[:, C_IOTA:C_IOTA + TOPK] = np.arange(TOPK)
    for h in range(HPG2):
        c[h * CMP_BLOCKS:(h + 1) * CMP_BLOCKS, C_BLOCK + h] = 1.0
    c[:, C_ROWOK] = r >= CMP_LEN - 1
    return c


def onehots():
    c = np.zeros((33, OH_END), np.float32)
    dist = 255 - np.arange(TOE)
    for col, bad in ((C_OHA, dist < 0), (C_OHB, (dist < 0) | (dist >= SWA_WINDOW))):
        c[np.where(bad, 32, rel_bucket(dist)), col + np.arange(TOE)] = 1.0
    dist = np.arange(512) - OHC_BASE
    c[np.where(dist < 0, 32, rel_bucket(dist)), C_OHC + np.arange(512)] = 1.0
    return c


class Line:

    def __init__(self, sem=None):
        self.sem, self.count, self.steps, self.met = sem, 0, [], {}

    def wait(self, *tokens):
        for sem, value in tokens:
            if self.met.get(sem, 0) < value:
                self.met[sem] = value
                self.steps.append(lambda e, s=sem, v=value: e.wait_ge(s, v))

    def do(self, make, *after):
        self.wait(*after)
        self.count += 1
        self.steps.append(lambda e, s=self.sem: make(e).then_inc(s, 1))
        return (self.sem, self.count)

    def then(self, make, *after):
        if self.count:
            self.wait((self.sem, self.count))
        return self.do(make, *after)

    def quiet(self, make, *after):
        self.wait(*after)
        self.steps.append(lambda e: make(e))

    def run(self, e):
        for step in self.steps:
            step(e)


def build(nc, ins, out):
    with ExitStack() as ctx:
        def sb(name, shape, dt=F32):
            return ctx.enter_context(nc.sbuf_tensor(name, shape, dt))

        def sem(name):
            return ctx.enter_context(nc.semaphore(name))

        act_hi = sb("act_hi", [P, DK, SEQ], F32R)
        act_lo = sb("act_lo", [P, DK, SEQ], F32R)
        hid_hi = sb("hid_hi", [P, PANEL // P, SEQ], F32R)
        hid_lo = sb("hid_lo", [P, PANEL // P, SEQ], F32R)
        NSPLIT = 3
        w_hi = sb("w_hi", [P, NSPLIT, PANEL], F32R)
        w_lo = sb("w_lo", [P, NSPLIT, PANEL], F32R)
        RING = 6
        ring = sb("ring", [P, RING, PANEL])
        resid = sb("resid", [P, TT, D])
        panels = sb("panels", [P, 2, TT, PANEL])
        WORK = 17408
        work = sb("work", [P, WORK])
        stat = sb("stat", [P, 448])
        table = sb("table", [33, 32])
        biascmp = sb("biascmp", [P, TT, CMP_BLOCKS, HEADS2])
        qk_gain = sb("qk_gain", [P, 2, P])
        sink = sb("sink", [P, HEADS2])
        const = sb("const", [P, C_END])
        top_pos = sb("top_pos", [P, 2 * PEER_HEADS, TOPK], U32)
        cand_pos = sb("cand_pos", [P, 2, SLOTS], U32)
        expert = sb("expert", [P, TT, SLOTS], U32)
        acc = [ctx.enter_context(nc.psum_tensor(f"acc{i}", [P, BANK], F32)) for i in range(4)]
        wk = [ctx.enter_context(nc.psum_tensor(f"wk{i}", [P, BANK], F32)) for i in range(4)]
        bias_rows = nc.dram_tensor("bias_rows", [2 * HEADS2, TOE], F32, kind="Internal").ap()

        def region(at, *shape):
            n = int(np.prod(shape))
            v = work[:, at:at + n]
            if len(shape) == 1:
                return v
            names = "abcd"[:len(shape)]
            return v.rearrange(f"p ({' '.join(names)}) -> p {' '.join(names)}", **dict(zip(names, shape)))

        def cst(at, n=P):
            return const[:, at:at + n]

        ident, flip = cst(C_IDENT), cst(C_FLIP)
        gain = region(15360, D)

        pe, act, dve, pool, sp = (Line(sem("pe")), Line(sem("act")), Line(sem("dve")), Line(sem("pool")), Line())
        landing = [sem(f"chunk{i}") for i in range(RING)]
        landed = [0] * RING

        def load(dst, src, *after, name, queue=sp):
            s = sem(name)
            queue.wait(*after)
            queue.steps.append(lambda e: e.dma_start(dst, src).then_inc(s, 16))
            return (s, 16)

        acc_free = [()] * 4
        wk_free = [()] * 4
        ring_free = [()] * RING
        split_free = [()] * NSPLIT
        state = {"chunk": 0, "issued": 0, "posts": [], "side": None, "side_steps": 0, "done": [None] * TT}

        plan = []

        def plan_panels(w, row0, nk, *panels_):
            for col0, width in panels_:
                plan.extend((w, row0 + k * P, col0, width) for k in range(nk))

        both = [(0, PANEL), (PANEL, PANEL)]
        NH = MLP // PANEL
        plan_panels(ins["sb_w_qkv"][0], 0, DK, *[(i * PANEL, PANEL) for i in range(6)])
        plan_panels(ins["sb_w_o"][0], 0, DK, *both)
        for j in range(NH + 1):
            if j < NH:
                plan_panels(ins["mlp_w_in"][0], 0, DK, (j * PANEL, PANEL))
            if j > 0:
                plan_panels(ins["mlp_w_out"][0], (j - 1) * PANEL, PANEL // P, *both)
        plan_panels(ins["w_in_2"][0], 0, DK, (W2_KV, 816), (W2_KVB, 256), (W2_QA, PANEL), (W2_QB, PANEL))
        plan_panels(ins["w_out_2"][0], 0, DK, *both)
        plan_panels(ins["peer_wq_2"][0], 0, DK, *both)
        split_done = {}

        def issue(upto):
            while state["issued"] <= min(upto, len(plan) - 1):
                c = state["issued"]
                state["issued"] += 1
                w, row, col0, width = plan[c]
                s, b = c % RING, c % NSPLIT
                sp.wait(*ring_free[s])
                src, dst = w[row:row + P, col0:col0 + width], ring[:, s, :width]
                sp.steps.append(lambda e, d=dst, r=src, m=landing[s]: e.dma_start(d, r).then_inc(m, 16))
                landed[s] += 16
                there = (landing[s], landed[s])
                high = act.do(lambda e, s=s, b=b, width=width: e.activation(
                    w_hi[:, b, :width], ring[:, s, :width], ACT.Copy),
                    there, *split_free[b])
                low = dve.do(lambda e, s=s, b=b, width=width: e.tensor_tensor(
                    w_lo[:, b, :width], ring[:, s, :width], w_hi[:, b, :width].bitcast(F32), ALU.subtract),
                    high, there, *split_free[b])
                ring_free[s] = (low,)
                split_done[c] = (high, low)

        def gemm_panel(w, row0, nk, col0, width, hi, lo, after_x):
            cuts = [(n, min(BANK, width - n)) for n in range(0, width, BANK)]
            for k in range(nk):
                c = state["chunk"]
                state["chunk"] += 1
                assert plan[c][1:] == (row0 + k * P, col0, width) and plan[c][0].tensor.name == w.tensor.name
                b = c % NSPLIT
                issue(c + NSPLIT - 1)
                high, low = split_done[c]
                pe.wait(*(after_x[k // 4] if isinstance(after_x, dict) else after_x), high)
                for t in range(TT):
                    xs = [x[:, k, t * P:(t + 1) * P] for x in (hi, lo)]
                    for i, (x, wp) in enumerate(((xs[0], w_hi), (xs[0], w_lo), (xs[1], w_hi))):
                        if i == 1:
                            pe.wait(low)
                        for j, (n, m) in enumerate(cuts):
                            if k == 0 and i == 0:
                                pe.wait(*acc_free[2 * t + j])
                            mm = (lambda e, x=x, wp=wp, j=j, t=t, n=n, m=m, i=i, k=k, b=b: e.matmul(
                                acc[2 * t + j][:, :m], x, wp[:, b, n:n + m],
                                start=(k == 0 and i == 0), stop=(k == nk - 1 and i == 2)))
                            if (i, j) == (2, len(cuts) - 1) and (t == TT - 1 or k == nk - 1):
                                done = pe.do(mm)
                                state["done"][t] = done
                            else:
                                pe.quiet(mm)
                split_free[b] = (done,)
                while state["posts"] and k >= state["posts"][0][0]:
                    state["posts"].pop(0)[1]()
                if k > 2 and state["side"]:
                    side(state["side_steps"])
            return done

        def side(n):
            for _ in range(n):
                if state["side"] and next(state["side"], "end") == "end":
                    state["side"] = None

        def flush():
            while state["posts"]:
                state["posts"].pop(0)[1]()

        def take_panel(width, store, *after):
            tokens = []
            for t in range(TT):
                for j, n in enumerate(range(0, width, BANK)):
                    bank = 2 * t + j
                    tok = store(t, n, min(BANK, width - n), acc[bank], state["done"][t], *after)
                    acc_free[bank] = (tok,)
                    tokens.append(tok)
            return tokens

        def store_copy(dst):
            def store(t, n, m, bank, *after):
                if n == 0:
                    return act.do(lambda e: e.activation(dst[:, t, n:n + m], bank[:, :m], ACT.Copy), *after)
                return dve.do(lambda e: e.tensor_copy(dst[:, t, n:n + m], bank[:, :m]), *after)
            return store

        def transposes(srcs, bank, *after):
            pe.wait(*after, *wk_free[bank])
            for i, src in enumerate(srcs):
                f = (lambda e, i=i, src=src: e.transpose(wk[bank][:, i * P:(i + 1) * P], src, ident))
                if i == len(srcs) - 1:
                    return pe.do(f)
                pe.quiet(f)

        def split_transposed(src, nk, hi, lo, *after, ready, square=None):
            tokens = []
            for t in range(TT):
                for k0 in range(0, nk, 4):
                    if t or k0:
                        yield
                    bank = (t * nk + k0) // 4 % 4
                    there = transposes([src(t)[:, k * P:(k + 1) * P] for k in range(k0, k0 + 4)], bank,
                                       *after)
                    grid = wk[bank][:, :].rearrange("p (k q) -> p k q", k=4)
                    to = lambda x, k0=k0, t=t: x[:, k0:k0 + 4, t * P:(t + 1) * P]
                    if square is None:
                        h = act.do(lambda e, to=to, grid=grid: e.activation(to(hi), grid, ACT.Copy), there)
                        l = dve.do(lambda e, to=to, grid=grid: e.tensor_tensor(
                            to(lo), grid, to(hi).bitcast(F32), ALU.subtract), h)
                        wk_free[bank] = (l,)
                    else:
                        b = square[:, bank % 2, :].rearrange("p (k q) -> p k q", k=4)
                        sq = act.do(lambda e, b=b, grid=grid: e.activation(b, grid, ACT.Square),
                                    there, *tokens[-2:-1])
                        wk_free[bank] = (sq,)
                        h = act.then(lambda e, to=to, b=b: e.activation(to(hi), b, ACT.Copy))
                        l = dve.do(lambda e, to=to, b=b: e.tensor_tensor(
                            to(lo), b, to(hi).bitcast(F32), ALU.subtract), h)
                    tokens.append(l)
            ready[:] = tokens[-1:] + [h]

        ss, rs = stat[:, 0:4].rearrange("p (a t) -> p a t", a=2), stat[:, 4:6]

        def inv_rms(total, width, dst, *after):
            a = dve.then(lambda e: e.tensor_scalar(dst, total, 1.0 / width, EPS, ALU.mult, ALU.add), *after)
            b = act.then(lambda e: e.activation(dst, dst, ACT.Sqrt), a)
            return dve.then(lambda e: e.reciprocal(dst, dst), b)

        def squares(dst, half, *after):
            cols = slice(half * PANEL, (half + 1) * PANEL)
            for t in range(TT):
                sq = act.then(lambda e, t=t: e.activation(dst[:, t, cols], resid[:, t, cols], ACT.Square,
                                                          accum_out=ss[:, half, t:t + 1]), *after)
            return sq

        def norm_turned(dst, gain_there, free, *after):
            sq = squares(dst, 1, *after)
            both_halves = dve.then(lambda e: e.tensor_tensor(rs, ss[:, 0, :], ss[:, 1, :], ALU.add), sq)
            inv_rms(rs, D, rs, both_halves)
            ready = {}

            def group(q):
                cols, k0 = slice(q * BANK, (q + 1) * BANK), 4 * q
                normed = [dve.then(lambda e, t=t: e.scalar_tensor_tensor(
                    dst[:, t, cols], resid[:, t, cols], rs[:, t:t + 1], gain[:, cols], ALU.mult, ALU.mult), gain_there)
                    for t in range(TT)]
                ready[q] = []
                for t in range(TT):
                    bank = 2 * (q % 2) + t
                    there = transposes([dst[:, t, k * P:(k + 1) * P] for k in range(k0, k0 + 4)], bank, normed[t],
                                       const_there)
                    grid = wk[bank][:, :].rearrange("p (k q) -> p k q", k=4)
                    hi, lo = (x[:, k0:k0 + 4, t * P:(t + 1) * P] for x in (act_hi, act_lo))
                    h = act.do(lambda e, hi=hi, grid=grid: e.activation(hi, grid, ACT.Copy), there, *free)
                    l = dve.do(lambda e, hi=hi, lo=lo, grid=grid: e.tensor_tensor(lo, grid, hi.bitcast(F32),
                                                                                  ALU.subtract), h)
                    wk_free[bank] = (l,)
                    ready[q] += [h, l]

            group(0)
            assert not state["posts"]
            state["posts"] = [(0, lambda: group(1)), (2, lambda: group(2)), (5, lambda: group(3))]
            return ready

        def flat_tokens(ready):
            return [tok for q in range(4) for tok in ready[q]]

        def spread(row, n=D):
            return bass.AP(tensor=row.tensor, offset=0, ap=[[0, P], [1, n]])

        wide = panels[:, :, :, :].rearrange("p b t n -> p (b t n)").rearrange("p (t n) -> p t n", t=TT)
        slab = lambda b: panels[:, b, :, :]

        x_view = ins["x"].rearrange("b (t p) d -> p (b t) d", p=P)
        x_there = [load(resid[:, :, n:n + PANEL], x_view[:, :, n:n + PANEL], name=f"x{n}_in") for n in (0, PANEL)]
        gain1_there = load(gain, spread(ins["norm_mix_g"]), name="gain1_in")
        const_there = load(const[:, :], ins["const"], name="const_in")
        qg_there = load(qk_gain[:, 0, :], spread(ins["sb_q_norm_g"], P), name="qgain_in")
        kg_there = load(qk_gain[:, 1, :], spread(ins["sb_k_norm_g"], P), name="kgain_in")
        squares(wide, 0, x_there[0])
        sink_there = load(sink[:, :], spread(ins["sinks_2"], HEADS2), name="sink_in")
        onehot_b = work[:33, 2048:2048 + OH_END]
        onehot_there = load(onehot_b, ins["onehot"], name="onehot_in")
        neg_row = dve.do(lambda e: e.memset(table[:, :], NEG))
        table_there = load(table[0:32, :], ins["rel_bias_2"], neg_row, name="table_in")

        issue(1)
        x_ready = norm_turned(wide, gain1_there, (), *x_there)

        q_t, k_t = region(0, HEADS1, SEQ), region(4096, HEADS1, SEQ)
        v_tok = region(8192, TT, D)
        w_qkv = ins["sb_w_qkv"][0]
        scale1 = float(P) ** -0.5
        sum8, inv8 = stat[:, 8:24].rearrange("p (t h) -> p t h", t=TT), stat[:, 24:40].rearrange("p (t h) -> p t h", t=TT)
        head_ready = {}
        slab_free = [(), ()]

        def heads_post(panel, stored, dst, which, scale):
            v = slab(panel % 2)
            heads = v.rearrange("p t (h d) -> p t h d", d=P)
            squares = work[:, 12288:14336].rearrange("p (t h d) -> p t h d", t=TT, d=P)
            got = {}

            def square():
                got["sq"] = [act.then(lambda e, t=t: e.activation(squares[:, t], heads[:, t], ACT.Square), *stored)
                             for t in range(TT)]

            def total(t):
                got["sum"] = dve.then(lambda e: e.tensor_reduce(sum8[:, t, :], squares[:, t], AX.X, ALU.add),
                                      got["sq"][t])

            def root():
                got["inv"] = inv_rms(sum8.rearrange("p t h -> p (t h)"), P, inv8.rearrange("p t h -> p (t h)"),
                                     got["sum"])

            def scaled(t):
                dve.then(lambda e: e.tensor_tensor(
                    heads[:, t], heads[:, t], inv8[:, t, :].unsqueeze(2).to_broadcast([P, 8, P]), ALU.mult))
                got[t] = dve.then(lambda e: e.scalar_tensor_tensor(
                    heads[:, t], heads[:, t], scale, qk_gain[:, which, :].unsqueeze(1).to_broadcast([P, 8, P]),
                    ALU.mult, ALU.mult), qg_there, kg_there)

            def turn(t):
                for k0 in (0, 4):
                    bank = 2 * t + k0 // 4
                    there = transposes([v[:, t, k * P:(k + 1) * P] for k in range(k0, k0 + 4)], bank, got[t])
                    h0 = (panel % 2) * 8 + k0
                    tok = act.do(lambda e, h0=h0, bank=bank: e.activation(
                        dst[:, h0:h0 + 4, t * P:(t + 1) * P], wk[bank][:, :].rearrange("p (k q) -> p k q", k=4),
                        ACT.Copy), there, bias_written)
                    wk_free[bank] = (tok,)
                slab_free[panel % 2] = (tok,)
                head_ready[panel] = tok

            return [(1, square), (2, lambda: total(0)), (3, lambda: total(1)), (4, root), (5, lambda: scaled(0)),
                    (7, lambda: scaled(1)), (8, lambda: turn(0)), (10, lambda: turn(1))]

        bias_out = sem("bias_out")
        bias_written = (bias_out, 16)

        def bias_tables():
            bias_sb = work[:HEADS2, 0:2 * TOE].rearrange("p (a n) -> p a n", a=2)
            for half, oh in ((0, C_OHA), (1, C_OHB)):
                rows = pe.do(lambda e, half=half, oh=oh: e.matmul(
                    wk[half][:HEADS2, :TOE], table[:, half * 16:half * 16 + 16], onehot_b[:, oh:oh + TOE],
                    start=True, stop=True), table_there, onehot_there, *wk_free[half])
                taken = dve.do(lambda e, half=half: e.tensor_copy(bias_sb[:, half, :], wk[half][:HEADS2, :TOE]), rows)
                wk_free[half] = (taken,)
            pool.wait(taken)
            pool.steps.append(lambda e: e.dma_start(bias_rows.rearrange("(a h) n -> h a n", a=2), bias_sb)
                            .then_inc(bias_out, 16))

            for t in range(TT):
                pe.wait(*wk_free[2 + t])
                for c in range(CMP_BLOCKS):
                    col = C_OHC + OHC_BASE + t * P - CMP_STRIDE * c - (CMP_LEN - 1)
                    f = (lambda e, t=t, c=c, col=col: e.matmul(
                        wk[2 + t][:, c * HEADS2:(c + 1) * HEADS2], onehot_b[:, col:col + P], table[:, 0:HEADS2],
                        start=True, stop=True))
                    rows = pe.do(f) if c == CMP_BLOCKS - 1 else pe.quiet(f)
                taken = dve.do(lambda e, t=t: e.tensor_copy(
                    biascmp[:, t, :, :].rearrange("p c h -> p (c h)"), wk[2 + t][:, :CMP_BLOCKS * HEADS2]), rows)
                wk_free[2 + t] = (taken,)

        state["posts"].append((8, bias_tables))
        for panel in range(4):
            done = gemm_panel(w_qkv, 0, DK, panel * PANEL, PANEL, act_hi, act_lo, x_ready)
            stored = take_panel(PANEL, store_copy(slab(panel % 2)), *slab_free[panel % 2],
                                *flat_tokens(x_ready))
            state["posts"] = heads_post(panel, stored, q_t if panel < 2 else k_t, panel // 2,
                                        scale1 if panel < 2 else 1.0)
        v_stored = []
        for panel in range(2):
            done = gemm_panel(w_qkv, 0, DK, 2 * D + panel * PANEL, PANEL, act_hi, act_lo, x_ready)
            v_stored += take_panel(PANEL, store_copy(v_tok[:, :, panel * PANEL:(panel + 1) * PANEL]), bias_written)
        act_free = (done,)

        GH = 2
        COLS = SEQ + P
        z_a = region(12288, 2, GH, COLS)
        z_b = region(13824, 2, GH, COLS)
        za_free, zb_free = [(), ()], [(), ()]
        stick, tri, ones = cst(C_STICK), cst(C_TRI), cst(C_ONES)
        m = dict(skip_group_check=True)

        def stick_scores(g):
            u, z_done, mag = g % 2, [], []
            for i in range(GH):
                h, z = g * GH + i, acc[GH * u + i]
                pe.wait(*acc_free[GH * u + i], head_ready[0], head_ready[1], head_ready[2], head_ready[3])
                pe.quiet(lambda e, z=z, h=h: e.matmul(z[:, :SEQ], k_t[:, h, :P], q_t[:, h, :], start=True, stop=False, **m))
                pe.quiet(lambda e, z=z, h=h: e.matmul(z[:, SEQ:COLS], k_t[:, h, P:], q_t[:, h, P:], start=False, stop=False, **m))
                pe.quiet(lambda e, z=z: e.matmul(z[:, :P], ident, stick, start=False, stop=False, **m))
                z_done.append(pe.do(lambda e, z=z: e.matmul(z[:, SEQ:COLS], ident, stick, start=False, stop=True, **m)))
            for i in range(GH):
                mag.append(act.do(lambda e, i=i: e.activation(z_a[:, u, i, :], acc[GH * u + i][:, :COLS], ACT.Abs),
                                  z_done[i], *za_free[u]))
            ex = act.do(lambda e: e.activation(z_a[:, u], z_a[:, u], ACT.Exp, scale=-1.0), *mag)
            ln = act.then(lambda e: e.activation(z_a[:, u], z_a[:, u], ACT.Ln, bias=1.0), ex)
            return [dve.do(lambda e, i=i: e.scalar_tensor_tensor(z_b[:, u, i, :], acc[GH * u + i][:, :COLS], 0.0,
                                                                 z_a[:, u, i, :], ALU.max, ALU.add), ln, *zb_free[u])
                    for i in range(GH)]

        def stick_weights(g, sp_done):
            u, a_done = g % 2, []
            for i in range(GH):
                z = acc[GH * u + i]
                pe.wait(sp_done[i])
                pe.quiet(lambda e, z=z, i=i: e.matmul(z[:, :SEQ], tri, z_b[:, u, i, :SEQ], start=False, stop=False, **m))
                pe.quiet(lambda e, z=z, i=i: e.matmul(z[:, P:SEQ], ones, z_b[:, u, i, SEQ:], start=False, stop=False, **m))
                s_done = pe.do(lambda e, z=z, i=i: e.matmul(z[:, SEQ:COLS], tri, z_b[:, u, i, SEQ:], start=False,
                                                            stop=True, **m))
                tok = act.do(lambda e, i=i: e.activation(z_a[:, u, i, :], acc[GH * u + i][:, :COLS], ACT.Exp),
                             s_done, sp_done[i])
                acc_free[GH * u + i] = (tok,)
                a_done.append(tok)
            zb_free[u] = (s_done,)
            return a_done

        def stick_values(g, a_done):
            u, bank = g % 2, g % 4
            o = wk[bank]
            pe.wait(*a_done, *v_stored, *wk_free[bank])
            for j in range(GH):
                h, c = g * GH + j, j * SEQ
                v0, v1 = (v_tok[:, t, h * P:(h + 1) * P] for t in range(TT))
                pe.quiet(lambda e, c=c, v0=v0, j=j: e.matmul(o[:, c:c + SEQ], v0, z_a[:, u, j, :SEQ],
                                                             start=True, stop=False, **m))
                o_done = pe.do(lambda e, c=c, v1=v1, j=j: e.matmul(o[:, c + P:c + SEQ], v1, z_a[:, u, j, SEQ:],
                                                                   start=False, stop=True, **m))
            za_free[u] = (o_done,)
            h0, grid = g * GH, o[:, :].rearrange("p (k q) -> p k q", k=2)
            hi = act.do(lambda e: e.activation(act_hi[:, h0:h0 + 2, :], grid, ACT.Copy), o_done, *act_free)
            lo = dve.do(lambda e: e.tensor_tensor(act_lo[:, h0:h0 + 2, :], grid, act_hi[:, h0:h0 + 2, :].bitcast(F32),
                                                  ALU.subtract), hi)
            wk_free[bank] = (lo,)
            return hi, lo

        act.quiet(lambda e: e.preload_act_table_set("natural_log_exp_and_others"))
        scored, weighed = {}, {}
        for g in range(HEADS1 // GH + 2):
            if g >= 2:
                hi, lo = stick_values(g - 2, weighed[g - 2])
            if g < HEADS1 // GH:
                scored[g] = stick_scores(g)
            if 1 <= g <= HEADS1 // GH:
                weighed[g - 1] = stick_weights(g - 1, scored[g - 1])
        o_ready = [hi, lo]

        def store_residual(panel):
            def store(t, n, m, bank, *after):
                at = resid[:, t, panel * PANEL + n:panel * PANEL + n + m]
                return dve.do(lambda e: e.tensor_tensor(at, bank[:, :m], at, ALU.add), *after)
            return store

        gain2_there = load(gain, spread(ins["norm_mlp_g"]), *flat_tokens(x_ready), name="gain2_in", queue=pool)
        added = []
        for panel in range(2):
            done = gemm_panel(ins["sb_w_o"][0], 0, DK, panel * PANEL, PANEL, act_hi, act_lo, o_ready)
            added += take_panel(PANEL, store_residual(panel))
            if panel == 0:
                state["posts"] = [(3, lambda: squares(wide, 0, *added, *slab_free[0], *slab_free[1]))]
        act_free = (done,)

        x_ready = norm_turned(wide, gain2_there, act_free, *added)
        square = region(0, 2, BANK)
        hid_state = {"free": ()}
        added = []

        def store_relu(dst):
            def store(t, n, m, bank, *after):
                if n == 0:
                    return act.do(lambda e: e.activation(dst[:, t, n:n + m], bank[:, :m], ACT.Relu), *after)
                return dve.do(lambda e: e.tensor_scalar(dst[:, t, n:n + m], bank[:, :m], 0.0, None, ALU.max), *after)
            return store

        def hidden_out(j, hid_ready):
            for panel in range(2):
                done = gemm_panel(ins["mlp_w_out"][0], j * PANEL, PANEL // P, panel * PANEL, PANEL, hid_hi, hid_lo,
                                  hid_ready)
                added[:] = added[-4:] + take_panel(PANEL, store_residual(panel))
                if j == NH - 1 and panel == 0:
                    state["posts"] = [(3, lambda: squares(wide, 0, *added, *slab_free[0], *slab_free[1]))]
            hid_state["free"] = (done,)

        hid_ready = []
        for j in range(NH):
            done = gemm_panel(ins["mlp_w_in"][0], 0, DK, j * PANEL, PANEL, act_hi, act_lo, x_ready)
            if j == 0:
                slab_free = [tuple(flat_tokens(x_ready))] * 2
            stored = take_panel(PANEL, store_relu(slab(j % 2)), *slab_free[j % 2])
            if j > 0:
                hidden_out(j - 1, hid_ready)
            turned = split_transposed(lambda t, v=slab(j % 2): v[:, t, :], PANEL // P, hid_hi, hid_lo, *stored,
                                      *hid_state["free"], square=square, ready=hid_ready)

            def finish_turn(turned=turned, j=j):
                for _ in turned:
                    pass
                slab_free[j % 2] = tuple(hid_ready)

            state["posts"] = [(k, lambda turned=turned: next(turned)) for k in (0, 2, 4)] + [(6, finish_turn)]
        flush()
        act_free = (done,)
        hidden_out(NH - 1, hid_ready)

        gain3_there = load(gain, spread(ins["attn_norm_2"]), *flat_tokens(x_ready), name="gain3_in", queue=pool)
        x_ready = norm_turned(wide, gain3_there, act_free, *added)

        q2_t = region(0, HEADS2, SEQ)
        kz = region(4096, 3, GROUPS2, 2, SEQ)
        kvg = region(7168, TT, 816)
        kvb = region(8800, TT, 256)
        ckv_t = region(9312, 2, GROUPS2, SEQ)
        v_block = region(9312, GROUPS2, BANK)
        flat = region(10336, DK, GROUPS2 * CMP_BLOCKS)
        w1 = region(10816, 2, DK, P)
        bias_a = region(10816, HEADS2, SEQ)
        e_buf = region(14912, 2, BANK)
        et_buf = region(15936, 2, BANK)
        twice = region(16960, 2, P)
        ckz = region(17216, GROUPS2, 2, CMP_BLOCKS + 1)
        cmp_hid = region(17280, 2 * CMP_BLOCKS)
        pos_t = stat[:, 64:64 + 2 * DK].rearrange("p (a k) -> p a k", a=2)

        w2 = stat[:, 228:356].rearrange("p (a d) -> p a d", a=2)

        w_in2 = ins["w_in_2"][0]

        def pairs_post(panel, stored, first):
            def post():
                v = slab(panel)
                for t in range(TT):
                    for k0 in (0, 4):
                        bank = 2 * t + k0 // 4
                        there = transposes([v[:, t, k * P:(k + 1) * P] for k in range(k0, k0 + 4)], bank, *stored)
                        tok = act.do(lambda e, k0=k0, t=t, bank=bank: e.activation(
                            q2_t[:, first + k0:first + k0 + 4, t * P:(t + 1) * P],
                            wk[bank][:, :].rearrange("p (k q) -> p k q", k=4), ACT.Copy, scale=HD2 ** -0.5), there)
                        wk_free[bank] = (tok,)
                head_ready[10 + panel] = tok
            return [(1, post)]

        gate = sb("gate", [P, TT, HEADS2, 3])
        sums = sb("sums", [P, TT, HEADS2, 3])
        sumb = sb("sumb", [P, TT, HEADS2])
        nmax = sb("nmax", [P, 2 + TT * HPG2, 2])
        neg_sink = sb("neg_sink", [P, HEADS2])
        e_free, et_free = [(), ()], [(), ()]
        twice_free = [(), ()]
        ready = {}
        n_cmp = HPG2 * CMP_BLOCKS
        cmp_et = [region(16960, 2 * P), region(10336, 2 * P)]
        skew = lambda h0: bass.AP(tensor=bias_rows.tensor, offset=h0 * TOE, ap=[[1, P], [TOE, HPG2], [1, SEQ]])
        bias_landed, bias_ready = {}, {}

        def query(pair, head, t):
            return q2_t[:, pair + head // 2, t * P:(t + 1) * P]

        def doubled(src, col, g, evacuate, *after):
            copies = []
            for t in range(TT):
                tw = twice[:, t, :].rearrange("p (a d) -> p a d", a=2)
                copies.append(dve.then(lambda e, t=t, tw=tw: e.tensor_copy(
                    tw, src[:, t, col + g * HD2:col + (g + 1) * HD2].unsqueeze(1).to_broadcast([P, 2, HD2])),
                    *after, *twice_free[t]))
            yield
            bank = 2 + g
            there = transposes([twice[:, t, :] for t in range(TT)], bank, *copies)
            twice_free[:] = [(there,), (there,)]
            wk_free[bank] = (evacuate(wk[bank][:, :SEQ], there),)
            yield

        def keys_to(name, src, col, which, *after):
            for g in range(GROUPS2):
                def evacuate(turned, there, g=g):
                    for half in range(2):
                        rows = slice(half * HD2, (half + 1) * HD2)
                        tok = dve.then(lambda e, half=half, rows=rows: e.tensor_copy(
                            kz[rows, which, g, half, :], turned[rows, :]), there, clear)
                    return tok
                yield from doubled(src, col, g, evacuate, *after)
            ready[name] = dve.sem, dve.count

        def compressed_keys():
            pos_turned = pe.do(lambda e: e.transpose(wk[0][:, :2 * DK], stat[:2 * DK, 100:228], ident[:2 * DK, :2 * DK]),
                               *pos_there, *wk_free[0])
            pos_ready = dve.then(lambda e: e.tensor_copy(pos_t.rearrange("p a k -> p (a k)"), wk[0][:, :2 * DK]),
                                 pos_turned)
            wk_free[0] = (pos_ready,)
            for which, col in ((0, KV_KC), (1, KV_VC)):
                for g in range(GROUPS2):
                    def evacuate(turned, there, which=which, g=g):
                        return dve.then(lambda e: e.tensor_copy(ckv_t[:, which, g, :], turned), there)
                    yield from doubled(kvg, col, g, evacuate)
            cmp_done = ()
            for which in range(2):
                for g in range(GROUPS2):
                    for l in range(2):
                        rows = slice(l * HD2, (l + 1) * HD2)
                        src = ckv_t[rows, which, g, l:l + 1]
                        view = bass.AP(tensor=src.tensor, offset=src.offset,
                                       ap=[list(src.ap[0]), [2, DK], [CMP_STRIDE, CMP_BLOCKS]])
                        flat_ready = dve.then(lambda e, g=g, rows=rows, view=view, w=which: e.tensor_tensor(
                            flat[rows, :, g * CMP_BLOCKS:(g + 1) * CMP_BLOCKS], view,
                            pos_t[rows, w, :].unsqueeze(2).to_broadcast([HD2, DK, CMP_BLOCKS]), ALU.add), *cmp_done)
                yield
                pe.wait(flat_ready, w1_there[which], *wk_free[0])
                for k in range(DK):
                    f = (lambda e, k=k, w=which: e.matmul(wk[0][:, :2 * CMP_BLOCKS], w1[:, w, k, :], flat[:, k, :],
                                                          start=(k == 0), stop=(k == DK - 1)))
                    hid = pe.do(f) if k == DK - 1 else pe.quiet(f)
                gel = act.then(lambda e: e.activation(cmp_hid, wk[0][:, :2 * CMP_BLOCKS], ACT.Gelu_apprx_tanh),
                               hid, clear2, *cmp_done)
                wk_free[0] = (gel,)
                if which == 0:
                    tw = twice[:, 0, :].rearrange("p (a d) -> p a d", a=2)
                    cp = dve.then(lambda e: e.tensor_copy(tw, w2[:, 0, :].unsqueeze(1).to_broadcast([P, 2, HD2])),
                                  w2_there[0], *twice_free[0])
                    yield
                    ck = pe.do(lambda e: e.matmul(wk[1][:, :2 * CMP_BLOCKS], twice[:, 0, :], cmp_hid,
                                                  start=True, stop=True), cp, gel, *wk_free[1])
                    twice_free[0] = (ck,)
                    for half in range(2):
                        rows = slice(half * HD2, (half + 1) * HD2)
                        ready["ck"] = dve.then(lambda e, rows=rows, half=half: e.tensor_copy(
                            ckz[rows, :, half, :CMP_BLOCKS],
                            wk[1][rows, :2 * CMP_BLOCKS].rearrange("p (g c) -> p g c", g=2)), ck, clear2)
                    wk_free[1] = (ready["ck"],)
                    cmp_done = (ck,)
                else:
                    ready["w1"] = hid
                    copies = []
                    for g in range(GROUPS2):
                        rep = e_buf[:, g, :n_cmp].rearrange("p (h c) -> p h c", h=HPG2)
                        copies.append(dve.then(lambda e, g=g, rep=rep: e.tensor_copy(
                            rep, cmp_hid[:, g * CMP_BLOCKS:(g + 1) * CMP_BLOCKS].unsqueeze(1)
                            .to_broadcast([P, HPG2, CMP_BLOCKS])), gel))
                    yield
                    for g in range(GROUPS2):
                        cv = pe.do(lambda e, g=g: e.matmul(wk[2 + g][:n_cmp, :HD2], e_buf[:, g, :n_cmp], w2[:, 1, :],
                                                           start=True, stop=True),
                                   copies[g], w2_there[1], *wk_free[2 + g])
                        e_free[g] = (cv,)
                        ready["vb"] = dve.then(lambda e, g=g: e.tensor_tensor(
                            v_block[:n_cmp, g, :].rearrange("p (h d) -> p h d", h=HPG2),
                            wk[2 + g][:n_cmp, :HD2].unsqueeze(1).to_broadcast([n_cmp, HPG2, HD2]),
                            const[:n_cmp, C_BLOCK:C_BLOCK + HPG2].unsqueeze(2).to_broadcast([n_cmp, HPG2, HD2]),
                            ALU.mult), cv)
                        wk_free[2 + g] = (ready["vb"],)
            yield

        def bias_load(half, g, *after):
            bias_landed[(half, g)] = load(bias_a[:, g * HPG2:(g + 1) * HPG2, :], skew(half * HEADS2 + g * HPG2),
                                          bias_written, *after, name=f"bias{half}{g}_in", queue=pool)

        def bias_turn(half, g):
            for h in range(g * HPG2, (g + 1) * HPG2, 2):
                two = bias_a[:, h:h + 2, :].rearrange("p h k -> p (h k)")
                turned = pe.do(lambda e, two=two: e.matmul(wk[3][:, :], flip, two, start=True, stop=True),
                               bias_landed[(half, g)], *wk_free[3])
                tok = act.do(lambda e, two=two: e.activation(two, wk[3][:, :], ACT.Copy), turned)
                wk_free[3] = (tok,)
                yield
            bias_ready[(half, g)] = tok

        def compressed(t):
            nc_all = HEADS2 * CMP_BLOCKS
            pe.wait(*wk_free[2], ready["ck"], head_ready[10])
            for h in range(HEADS2):
                f = (lambda e, h=h: e.matmul(wk[2][:, h * CMP_BLOCKS:(h + 1) * CMP_BLOCKS], query(0, h, t),
                                             ckz[:, h // HPG2, h % 2, :CMP_BLOCKS], start=True, stop=True, **m))
                lg_done = pe.do(f) if h == HEADS2 - 1 else pe.quiet(f)
            ec = e_buf[:, t, :nc_all].rearrange("p (h c) -> p h c", c=CMP_BLOCKS)
            lg_c = wk[2][:, :nc_all].rearrange("p (h c) -> p h c", c=CMP_BLOCKS)
            a = dve.then(lambda e: e.tensor_tensor(
                ec, lg_c, biascmp[:, t, :, :].rearrange("p c h -> p h c"), ALU.add), lg_done, *e_free[t])
            wk_free[2] = (a,)
            mc = nmax[:, 2:2 + HPG2, :].rearrange("p a b -> p (a b)")
            dve.then(lambda e: e.tensor_reduce(mc, ec, AX.X, ALU.max))
            b = dve.then(lambda e: e.tensor_tensor(
                ec, ec, mc.unsqueeze(2).to_broadcast([P, HEADS2, CMP_BLOCKS]), ALU.subtract))
            c = act.then(lambda e: e.activation(e_buf[:, t, :nc_all], e_buf[:, t, :nc_all], ACT.Exp), b)
            yield
            d = dve.then(lambda e: e.tensor_reduce(sums[:, t, :, 0], ec, AX.X, ALU.add), c)
            pe.wait(c, *wk_free[2])
            for g in range(GROUPS2):
                tr = pe.do(lambda e, g=g: e.transpose(wk[2][:n_cmp, g * P:(g + 1) * P],
                                                      e_buf[:, t, g * n_cmp:(g + 1) * n_cmp], ident))
            cp = dve.then(lambda e: e.tensor_copy(cmp_et[t][:n_cmp, :], wk[2][:n_cmp, :2 * P]), tr,
                          *twice_free[0], *twice_free[1], ready["w1"])
            wk_free[2] = (cp,)
            e_free[t] = (tr, d)
            ready["cmp", t] = (cp, d)
            yield

        def mixer_prep():
            yield from keys_to("ks", kvg, KV_KS, 0, *kv_stored)
            yield from keys_to("kw", kvg, KV_KW, 1)
            yield from compressed_keys()
            for g in range(GROUPS2):
                bias_load(0, g, ready["w1"])
            yield from keys_to("kb", kvb, 0, 2, *kvb_stored)
            g1 = act.then(lambda e: e.activation(gate[:, :, :, :].rearrange("p t h c -> p t (h c)"),
                                                 kvg[:, :, KV_GATE:KV_GATE + 48], ACT.Exp, scale=-1.0))
            gflat = gate[:, :, :, :].rearrange("p t h c -> p (t h c)")
            yield
            dve.then(lambda e: e.tensor_scalar(gflat, gflat, 1.0, None, ALU.add), g1)
            ready["gate"] = dve.then(lambda e: e.reciprocal(gflat, gflat))
            dve.then(lambda e: e.tensor_scalar(neg_sink[:, :], sink[:, :], -1.0, None, ALU.mult), sink_there)
            yield from bias_turn(0, 0)
            yield from bias_turn(0, 1)
            while 10 not in head_ready:
                yield
            for t in range(TT):
                yield from compressed(t)

        done = gemm_panel(w_in2, 0, DK, W2_KV, 816, act_hi, act_lo, x_ready)
        x_done = flat_tokens(x_ready)
        clear = dve.then(lambda e: e.memset(region(4096, 3072), 0.0), *x_done)
        clear2 = dve.then(lambda e: e.memset(region(17216, 64), 0.0), *x_done)
        w1_there = [load(w1[:, i, :, :], ins[n][0].rearrange("(k p) h -> p k h", p=P), *x_done, name=n + "_in", queue=pool)
                    for i, n in enumerate(("cmp_w1_k_2", "cmp_w1_v_2"))]
        pos_there = [load(stat[i * DK:(i + 1) * DK, 100:228], ins[n][0].rearrange("(k l) d -> k (l d)", l=2),
                          name=n + "_in", queue=pool) for i, n in enumerate(("cmp_pos_k_2", "cmp_pos_v_2"))]
        w2_there = [load(stat[:, 228 + 64 * i:292 + 64 * i], ins[n][0], name=n + "_in", queue=pool)
                    for i, n in enumerate(("cmp_w2_k_2", "cmp_w2_v_2"))]
        kv_stored = take_panel(816, store_copy(kvg), *x_done)
        done = gemm_panel(w_in2, 0, DK, W2_KVB, 256, act_hi, act_lo, x_ready)
        kvb_stored = take_panel(256, store_copy(kvb), *x_done)
        state["side"], state["side_steps"] = mixer_prep(), 3
        for panel, col in ((0, W2_QA), (1, W2_QB)):
            done = gemm_panel(w_in2, 0, DK, col, PANEL, act_hi, act_lo, x_ready)
            stored = take_panel(PANEL, store_copy(slab(panel)), *x_done)
            state["posts"] = pairs_post(panel, stored, panel * 8)
        act_free = (done,)
        flush()
        while state["side"]:
            side(1)
        k_ready = [ready["ks"], ready["kw"], ready["kb"]]

        L = [acc[0], acc[1]]
        T = [acc[2], acc[3]]
        o_tok = [slab(0), slab(1)]
        unit = 0

        def softmax_unit(t, q_of, k_of, v_of, b_of, sum_to, sinks, o_banks, o_cols, first, *after):
            nonlocal unit
            u = unit % 2
            unit += 1
            W = (t + 1) * P
            n = 2 * (t + 1)
            lg = L[u][:, :].rearrange("p (a w) -> p a w", a=2)
            eb = e_buf[:, u, :].rearrange("p (a w) -> p a w", a=2)
            nm = nmax[:, u, :]
            qs, ks, bs, totals = [q_of(0), q_of(1)], [k_of(0), k_of(1)], [b_of(0), b_of(1)], [sum_to(0), sum_to(1)]
            vs = [[v_of(i, kb) for kb in range(t + 1)] for i in range(2)]
            tokens = {}

            def logits():
                pe.wait(*acc_free[u], *after)
                for i in range(2):
                    f = (lambda e, i=i: e.matmul(lg[:, i, :W], qs[i], ks[i][:, :W], start=True, stop=True, **m))
                    lg_done = pe.do(f) if i == 1 else pe.quiet(f)
                for i in range(2):
                    mx = dve.do(lambda e, i=i: e.tensor_tensor_reduce(
                        out=eb[:, i, :W], in0=lg[:, i, :W], in1=bs[i][:, SEQ - W:SEQ], scale=1.0, scalar=-3.4e38,
                        op0=ALU.add, op1=ALU.max, accum_out=nm[:, i:i + 1]), lg_done, *e_free[u], *after)
                acc_free[u] = (mx,)
                tokens["mx"] = mx
                if sinks is None:
                    mx = dve.then(lambda e: e.tensor_scalar(nm, nm, -1.0, None, ALU.mult))
                else:
                    keep = nmax[:, 2 + t * HPG2 + sinks // 2, :]
                    mx = dve.then(lambda e: e.scalar_tensor_tensor(nm, nm, -1.0, neg_sink[:, sinks:sinks + 2],
                                                                   ALU.mult, ALU.min))
                    dve.then(lambda e: e.tensor_copy(keep, nm))
                for i in range(2):
                    ex = act.do(lambda e, i=i: e.activation(eb[:, i, :W], eb[:, i, :W], ACT.Exp, bias=nm[:, i:i + 1],
                                                            accum_out=totals[i]), mx)
                tokens["ex"] = ex

            def turn():
                pe.wait(tokens["ex"], *acc_free[2 + u])
                for j in range(n):
                    i, kb = divmod(j, t + 1)
                    f = (lambda e, j=j, i=i, kb=kb: e.transpose(T[u][:, j * P:(j + 1) * P],
                                                                eb[:, i, kb * P:(kb + 1) * P], ident))
                    tr = pe.do(f) if j == n - 1 else pe.quiet(f)
                e_free[u] = (tr, tokens["ex"])
                cp = dve.do(lambda e: e.tensor_copy(et_buf[:, u, :n * P], T[u][:, :n * P]), tr, *et_free[u])
                acc_free[2 + u] = (cp,)
                tokens["cp"] = cp

            def values():
                pe.wait(tokens["cp"])
                for j in range(n):
                    i, kb = divmod(j, t + 1)
                    if first and kb == 0 and (i == 0 or o_banks[0] != o_banks[1]):
                        pe.wait(*wk_free[o_banks[i]])
                    f = (lambda e, j=j, i=i, kb=kb: e.matmul(
                        wk[o_banks[i]][:, o_cols[i]:o_cols[i] + HD2], et_buf[:, u, j * P:(j + 1) * P], vs[i][kb],
                        start=(kb == 0), stop=(kb == t), **m))
                    pv = pe.do(f) if j == n - 1 else pe.quiet(f)
                et_free[u] = (pv,)
                tokens["pv"] = pv

            return logits, turn, values, tokens

        flying = []

        def push(stages):
            flying.append(stages)
            stages[0]()
            if len(flying) >= 2:
                flying[-2][1]()
            if len(flying) >= 3:
                flying.pop(0)[2]()

        def drain():
            while len(flying) > 1:
                flying.pop(0)[2]()
            last_unit = flying.pop(0)
            last_unit[1]()
            last_unit[2]()
            return last_unit[3]["pv"]

        unfinished = []

        def finish_last():
            if unfinished:
                unfinished.pop(0)()

        def weighted(g, t, last_unit, oc):
            hs = slice(g * HPG2, (g + 1) * HPG2)
            part = sums[:, t, hs, :]
            pv = last_unit["pv"]
            dve.then(lambda e: e.reciprocal(part, part), last_unit["ex"], *ready["cmp", t])
            dve.then(lambda e: e.tensor_tensor(part, part, gate[:, t, hs, :], ALU.mult), ready["gate"])
            if t == 0:
                dve.then(lambda e: e.tensor_scalar(part[:, :, 0], part[:, :, 0], const[:, C_ROWOK:C_ROWOK + 1],
                                                   None, ALU.mult))
            dst = o_tok[0][:, t, g * BANK:(g + 1) * BANK].rearrange("p (h d) -> p h d", d=HD2)
            tmp = o_tok[1][:, t, g * BANK:(g + 1) * BANK].rearrange("p (h d) -> p h d", d=HD2)
            for i, bank in enumerate((2, 0, 1)):
                w = part[:, :, i].unsqueeze(2).to_broadcast([P, HPG2, HD2])
                src = wk[bank][:, :].rearrange("p (h d) -> p h d", d=HD2)
                to = dst if i == 0 else tmp
                rd = dve.then(lambda e, to=to, src=src, w=w: e.tensor_tensor(to, src, w, ALU.mult), oc, pv,
                              head_ready[10], head_ready[11])
                wk_free[bank] = (rd,)
                if i:
                    dve.then(lambda e: e.tensor_tensor(dst, dst, tmp, ALU.add))
            if t == TT - 1:
                bias_load(1, g, last_unit["mx"])

        for g in range(GROUPS2):
            for t in range(TT):
                for hh in range(HPG2):
                    h = g * HPG2 + hh
                    q = query(0, h, t)
                    stages = softmax_unit(
                        t, lambda i: q, lambda i: kz[:, i, g, h % 2, :],
                        lambda i, kb: kvg[:, kb, (KV_VS, KV_VW)[i] + g * HD2:(KV_VS, KV_VW)[i] + (g + 1) * HD2],
                        lambda i: bias_a[:, h, :], lambda i: sums[:, t, h, 1 + i:2 + i], None, (0, 1),
                        (hh * HD2, hh * HD2), hh == 0, bias_ready[(0, g)], *k_ready)
                    push(stages)
                    if hh == 1:
                        finish_last()
                        oc = pe.do(lambda e, g=g, t=t: e.matmul(
                            wk[2][:, :], cmp_et[t][:n_cmp, g * P:(g + 1) * P], v_block[:n_cmp, g, :],
                            start=True, stop=True), *ready["cmp", t], ready["vb"], *wk_free[2])
                    if (g, t) == (1, 1) and hh == 3:
                        for _ in bias_turn(1, 0):
                            pass
                unfinished.append(lambda g=g, t=t, last_unit=stages[3], oc=oc: weighted(g, t, last_unit, oc))

        def with_sinks(t, last_unit):
            keep = nmax[:, 2 + t * HPG2:2 + (t + 1) * HPG2, :].rearrange("p a b -> p (a b)")
            ad = dve.then(lambda e: e.tensor_tensor(keep, keep, sink[:, :], ALU.add), last_unit["ex"])
            ex = act.then(lambda e: e.activation(keep, keep, ACT.Exp), ad)
            dve.then(lambda e: e.tensor_tensor(sumb[:, t, :], sumb[:, t, :], keep, ALU.add), ex)
            dve.then(lambda e: e.reciprocal(sumb[:, t, :], sumb[:, t, :]))
            for g in range(GROUPS2):
                w = sumb[:, t, g * HPG2:(g + 1) * HPG2].unsqueeze(2).to_broadcast([P, HPG2, HD2])
                dst = o_tok[1][:, t, g * BANK:(g + 1) * BANK].rearrange("p (h d) -> p h d", d=HD2)
                src = wk[g][:, :].rearrange("p (h d) -> p h d", d=HD2)
                rd = dve.then(lambda e, dst=dst, src=src, w=w: e.tensor_tensor(dst, src, w, ALU.mult), last_unit["pv"])
                wk_free[g] = (rd,)

        for t in range(TT):
            for h in range(0, HEADS2, 2):
                g = h // HPG2
                stages = softmax_unit(
                    t, lambda i: query(8, h + i, t), lambda i: kz[:, 2, g, (h + i) % 2, :],
                    lambda i, kb: kvb[:, kb, P + g * HD2:P + (g + 1) * HD2],
                    lambda i: bias_a[:, h + i, :], lambda i: sumb[:, t, h + i:h + i + 1], h, (g, g),
                    ((h % HPG2) * HD2, (h % HPG2 + 1) * HD2), h % HPG2 == 0, bias_ready[(1, g)],
                    head_ready[11])
                push(stages)
                if h == 2:
                    finish_last()
                if t == 0 and h == 4:
                    for _ in bias_turn(1, 1):
                        pass
            unfinished.append(lambda t=t, last_unit=stages[3]: with_sinks(t, last_unit))
        pv = drain()
        finish_last()
        rd = (dve.sem, dve.count)
        gain4_there = load(gain, spread(ins["ffn_norm_2"]), pv, rd, name="gain4_in", queue=pool)
        tokens = []
        for half in range(2):
            hi_part, lo_part = act_hi[:, half * 8:(half + 1) * 8, :], act_lo[:, half * 8:(half + 1) * 8, :]
            ready_half = []
            for _ in split_transposed(lambda t: slab(half)[:, t, :], PANEL // P, hi_part, lo_part, rd, *act_free,
                                      ready=ready_half):
                pass
            tokens += ready_half
        o_ready = tokens

        xn = region(0, TT, D)
        added = []
        for panel in range(2):
            done = gemm_panel(ins["w_out_2"][0], 0, DK, panel * PANEL, PANEL, act_hi, act_lo, o_ready)
            added += take_panel(PANEL, store_residual(panel))
            if panel == 0:
                state["posts"] = [(3, lambda: squares(xn, 0, *added, pv, rd))]
        act_free = (done,)

        scores = region(4096, TT, 2 * PEER_HEADS, NKEYS)
        qp_t = region(8192, 8, SEQ)
        route = region(11264, TT, SLOTS)
        hidden = region(11520, TT, SLOTS)
        sub_t = region(16384, 2, NKEYS)
        sub_raw = region(16640, 2, NKEYS)
        x_ready = norm_turned(xn, gain4_there, act_free, *added)

        score_done = {}

        def scores_post(panel, stored):
            v = slab(panel)
            turned = []

            def turn():
                for t in range(TT):
                    for k0 in (0, 4):
                        bank = 2 * t + k0 // 4
                        there = transposes([v[:, t, k * P:(k + 1) * P] for k in range(k0, k0 + 4)], bank, *stored)
                        tok = act.do(lambda e, k0=k0, t=t, bank=bank: e.activation(
                            qp_t[:, k0:k0 + 4, t * P:(t + 1) * P], wk[bank][:, :].rearrange("p (k q) -> p k q", k=4),
                            ACT.Copy), there, *score_done.values())
                        wk_free[bank] = (tok,)
                turned.append(tok)

            def score():
                for t in range(TT):
                    for k0 in (0, 4):
                        bank = 2 * t + k0 // 4
                        pe.wait(*turned, sub_ready, *wk_free[bank])
                        for i in range(4):
                            f = (lambda e, i=i, k0=k0, t=t, bank=bank: e.matmul(
                                wk[bank][:, i * P:(i + 1) * P], qp_t[:, k0 + i, t * P:(t + 1) * P], sub_t[:, (k0 + i) % 2, :],
                                start=True, stop=True, **m))
                            sc = pe.do(f) if i == 3 else pe.quiet(f)
                        r0 = panel * 8 + k0
                        tk = act.do(lambda e, r0=r0, t=t, bank=bank: e.activation(
                            scores[:, t, r0:r0 + 4, :], wk[bank][:, :].rearrange("p (k q) -> p k q", k=4), ACT.Copy), sc)
                        wk_free[bank] = (tk,)
                        score_done[(panel, t, k0)] = tk
            return [(1, turn), (2, score)]

        HALF = PEER_HEADS // 2
        HS = HALF * TOPK
        cand = region(12288, HALF, TOPK * TOPK)
        best = region(10240, 2 * HALF, TOPK)
        pos_f = region(10496, 2 * HALF, TOPK)
        top = region(10752, HALF, TOPK)
        slot_f = region(10880, 3, HS)
        onehot = region(13312, HS, TOPK)
        small = sb("small", [P, HALF])
        iota = cst(C_IOTA, TOPK)
        chosen = {}

        def top16(row, values, where):
            for r in range(2):
                v8 = values[:, r * 8:r * 8 + 8]
                dve.then(lambda e, v8=v8: e.max(v8, row))
                yield
                dve.then(lambda e, v8=v8, r=r: e.max_index(where[:, r * 8:r * 8 + 8], v8, row))
                yield
                if r == 0:
                    dve.then(lambda e, v8=v8: e.match_replace(row, v8, row, LOWEST))
                    yield

        def route_half(t, half):
            dve.wait(*[score_done[(half, t, k0)] for k0 in (0, 4)])
            for r in range(2 * HALF):
                yield from top16(scores[:, t, half * 2 * HALF + r, :], best[:, r, :], top_pos[:, r, :])
            pair = best[:, :, :].rearrange("p (h a) i -> p h a i", a=2)
            cand4 = cand.rearrange("p h (i j) -> p h i j", j=TOPK)
            dve.then(lambda e: e.tensor_tensor(
                cand4, pair[:, :, 0, :].unsqueeze(3).to_broadcast([P, HALF, TOPK, TOPK]),
                pair[:, :, 1, :].unsqueeze(2).to_broadcast([P, HALF, TOPK, TOPK]), ALU.add))
            yield
            where = cand_pos[:, 0, :HS]
            for h in range(HALF):
                yield from top16(cand[:, h, :], top[:, h, :], where[:, h * TOPK:(h + 1) * TOPK])
            dve.then(lambda e: e.tensor_copy(pos_f[:, :, :], top_pos[:, :2 * HALF, :]))
            posp = pos_f[:, :, :].rearrange("p (h a) i -> p h a i", a=2)
            oh4 = onehot.rearrange("p (h s) i -> p h s i", s=TOPK)
            for a, (op, k) in enumerate(((ALU.logical_shift_right, 4), (ALU.bitwise_and, TOPK - 1))):
                dve.then(lambda e, op=op, k=k: e.tensor_scalar(cand_pos[:, 1, :HS], where, k, None, op))
                dve.then(lambda e, a=a: e.tensor_copy(slot_f[:, a, :], cand_pos[:, 1, :HS]))
                yield
                dve.then(lambda e, a=a: e.tensor_tensor(
                    onehot, slot_f[:, a, :].unsqueeze(2).to_broadcast([P, HS, TOPK]),
                    iota.unsqueeze(1).to_broadcast([P, HS, TOPK]), ALU.is_equal))
                yield
                dve.then(lambda e, a=a: e.tensor_tensor(
                    oh4, oh4, posp[:, :, a, :].unsqueeze(2).to_broadcast([P, HALF, TOPK, TOPK]), ALU.mult))
                yield
                dve.then(lambda e, a=a: e.tensor_reduce(slot_f[:, a, :], onehot, AX.X, ALU.add))
                yield
            dve.then(lambda e: e.scalar_tensor_tensor(slot_f[:, 2, :], slot_f[:, 0, :], float(NKEYS), slot_f[:, 1, :],
                                                      ALU.mult, ALU.add))
            chosen[(t, half)] = dve.then(lambda e: e.tensor_copy(expert[:, t, half * HS:(half + 1) * HS],
                                                                 slot_f[:, 2, :]))
            yield
            share = route[:, t, half * HS:(half + 1) * HS]
            wt = share.rearrange("p (h s) -> p h s", s=TOPK)
            b = dve.then(lambda e: e.tensor_tensor(
                wt, top[:, :, :], top[:, :, 0:1].to_broadcast([P, HALF, TOPK]), ALU.subtract))
            c = act.then(lambda e: e.activation(share, share, ACT.Exp), b)
            yield
            dve.then(lambda e: e.tensor_reduce(small[:, :], wt, AX.X, ALU.add), c)
            dve.then(lambda e: e.reciprocal(small[:, :], small[:, :]))
            dve.then(lambda e: e.tensor_tensor(wt, wt, small[:, :].unsqueeze(2).to_broadcast([P, HALF, TOPK]), ALU.mult))
            yield

        def routing():
            for half in range(2):
                for t in range(TT):
                    yield from route_half(t, half)

        for panel in range(2):
            if panel == 1:
                state["side"], state["side_steps"] = routing(), 7
            done = gemm_panel(ins["peer_wq_2"][0], 0, DK, panel * PANEL, PANEL, act_hi, act_lo, x_ready)
            stored = take_panel(PANEL, store_copy(slab(panel)), *flat_tokens(x_ready))
            if panel == 0:
                x_done = flat_tokens(x_ready)
                sub_there = load(sub_raw, ins["peer_subkeys_2"][0].rearrange("a n d -> n a d"), *x_done,
                                 name="subkeys_in", queue=pool)
                st = transposes([sub_raw[:, 0, :], sub_raw[:, 1, :]], 0, sub_there)
                sub_ready = dve.then(lambda e: e.tensor_copy(sub_t.rearrange("p a n -> p (a n)"), wk[0][:, :2 * P]), st)
                wk_free[0] = (sub_ready,)
            state["posts"] = scores_post(panel, stored)
        flush()

        rows = [ring[:, i:i + 2, :].rearrange("p s n -> p (s n)") for i in range(0, RING, 2)]
        rows += [slab(b).rearrange("p t n -> p (t n)") for b in range(2)]
        SLOT_ROWS = len(rows)
        row_sem = [sem(f"rows{i}") for i in range(SLOT_ROWS)]
        gathered = {"n": 0}
        row_free = [tuple(ring_free[2 * i]) + tuple(ring_free[2 * i + 1]) for i in range(RING // 2)]
        row_free += [tuple(score_done.values())] * 2

        def gather(tab, t, j, *after):
            n = gathered["n"]
            gathered["n"] += 1
            s = n % SLOT_ROWS
            pool.wait(*after, *row_free[s])
            pool.steps.append(lambda e: e.indirect_dma_start(
                rows[s], None, tab, bass.IndirectOffsetOnAxis(ap=expert[:, t, j:j + 1], axis=0))
                .then_inc(row_sem[s], 16))
            return s, (row_sem[s], 16 * (n // SLOT_ROWS + 1))

        u_tab, v_tab = ins["peer_u_2"][0], ins["peer_v_2"][0]
        for t in range(TT):
            for j in range(SLOTS):
                while (t, j // HS) not in chosen:
                    side(1)
                s, there = gather(u_tab, t, j, chosen[(t, j // HS)])
                dot = dve.do(lambda e, s=s, t=t, j=j: e.tensor_tensor_reduce(
                    out=rows[s], in0=rows[s], in1=xn[:, t, :], scale=1.0, scalar=0.0, op0=ALU.mult,
                    op1=ALU.add, accum_out=hidden[:, t, j:j + 1]), there)
                row_free[s] = (dot,)
                side(2)
            while t == TT - 1 and state["side"]:
                side(1)
            ge = act.then(lambda e, t=t: e.activation(hidden[:, t, :], hidden[:, t, :], ACT.Gelu_apprx_tanh), dot)
            dve.then(lambda e, t=t: e.tensor_tensor(route[:, t, :], route[:, t, :], hidden[:, t, :], ALU.mult), ge)
        stored_out = [sem(f"stored_out{t}") for t in range(TT)]
        gain5_there = load(gain, spread(ins["final_norm_2"]), sub_ready, *score_done.values(), name="gain5_in", queue=pool)
        for t in range(TT):
            for j in range(SLOTS):
                s, there = gather(v_tab, t, j)
                last = dve.then(lambda e, s=s, t=t, j=j: e.scalar_tensor_tensor(
                    resid[:, t, :], rows[s], route[:, t, j:j + 1], resid[:, t, :], ALU.mult, ALU.add), there)
                row_free[s] = (last,)
            sq = act.do(lambda e, t=t: e.activation(xn[:, t, :], resid[:, t, :], ACT.Square,
                                                    accum_out=rs[:, t:t + 1]), last)
            inv_rms(rs[:, t:t + 1], D, rs[:, t:t + 1], sq)
            final = dve.then(lambda e, t=t: e.scalar_tensor_tensor(
                xn[:, t, :], resid[:, t, :], rs[:, t:t + 1], gain, ALU.mult, ALU.mult), gain5_there)
            sp.wait(final)
            sp.steps.append(lambda e, t=t: e.dma_start(out[0, t * P:(t + 1) * P, :], xn[:, t, :])
                            .then_inc(stored_out[t], 16))
        for t in range(TT):
            sp.wait((stored_out[t], 16))
        sp.wait(bias_written)

        block = ctx.enter_context(nc.Block())
        block.tensor(pe.run)
        block.scalar(act.run)
        block.vector(dve.run)
        block.gpsimd(pool.run)
        block.sync(sp.run)


NAMES = ["x", "norm_mix_g", "norm_mlp_g", "sb_w_qkv", "sb_q_norm_g", "sb_k_norm_g", "sb_w_o", "mlp_w_in", "mlp_w_out",
         "attn_norm_2", "w_in_2", "cmp_pos_k_2", "cmp_w1_k_2", "cmp_w2_k_2", "cmp_pos_v_2", "cmp_w1_v_2", "cmp_w2_v_2",
         "sinks_2", "w_out_2", "ffn_norm_2", "peer_wq_2", "peer_subkeys_2", "peer_u_2", "peer_v_2", "rel_bias_2",
         "final_norm_2"]


def kernel(**inputs):
    import numpy as _np
    import concourse.bacc as _bacc
    from concourse import mybir as _mybir
    from concourse.bass_utils import run_bass_kernel_spmd as _run

    nc = _bacc.Bacc("TRN2", target_bir_lowering=False, num_devices=1)
    arrays, ins = {}, {}
    given = {name: inputs[name] for name in NAMES}
    given["const"] = constants()
    given["onehot"] = onehots()
    for name, a in given.items():
        a = _np.ascontiguousarray(a)
        arrays[f"in_{name}_dram"] = a
        ins[name] = nc.dram_tensor(f"in_{name}_dram", a.shape, _mybir.dt.from_np(a.dtype), kind="ExternalInput").ap()
    out = nc.dram_tensor("out_dram", (1, SEQ, D), F32, kind="ExternalOutput").ap()
    build(nc, ins, out)
    r = _run(nc, [arrays], core_ids=[0])
    return r.results[0]["out_dram"]
```
